# Optimizing a Trainium2 kernel written in Bass

```python
import jax, jax.numpy as jnp
from jax import lax
import numpy as np

D_MODEL = 2048
BATCH = 1
SEQ = 256
DEPTH = 1

N_MEM = 256
EPS = 1e-6
F32 = jnp.float32

LRU_WIDTH = D_MODEL // 2
LRU_BLOCKS = 8
LRU_BLOCK_W = LRU_WIDTH // LRU_BLOCKS
LRU_C = 8.0
CONV_A = 4

DSA_HEADS = 8
DSA_HEAD_DIM = 128
DSA_Q_RANK = D_MODEL // 4
DSA_KV_RANK = D_MODEL // 8
IDX_HEADS = 8
IDX_DIM = 64
DSA_TOPK_MAX = 256
Q_BLOCK = 128

GDN_HEADS = 8
GDN_DK = 128
GDN_DV = 128
GDN_CHUNK = 64
CONV_C = 4

XATTN_HEADS = 4
XATTN_HEAD_DIM = 128

D_FF = 5632
CONV_F = 3

N_BRANCH = 3
IN_SPLITS = (LRU_WIDTH, LRU_WIDTH,
             DSA_Q_RANK, DSA_KV_RANK, IDX_DIM, IDX_HEADS,
             GDN_HEADS * GDN_DK, GDN_HEADS * GDN_DK, GDN_HEADS * GDN_DV,
             GDN_HEADS, GDN_HEADS, GDN_HEADS * GDN_DV,
             N_BRANCH * D_MODEL)
IN_OFFSETS = tuple(int(o) for o in np.cumsum(IN_SPLITS)[:-1])
N_IN = int(sum(IN_SPLITS))

kernel_name = 'hybrid_rglru_dsa_gdn_block'

def rmsnorm(x, g):
    xf = x.astype(F32)
    y = xf * lax.rsqrt(jnp.mean(xf * xf, axis=-1, keepdims=True) + EPS)
    return (y * g.astype(F32)).astype(x.dtype)

def l2norm(x):
    return x * lax.rsqrt(jnp.sum(x * x, axis=-1, keepdims=True) + EPS)

def causal_dwconv(x, w, b=None):
    k, c = w.shape
    y = lax.conv_general_dilated(x, w[:, None, :].astype(x.dtype), window_strides=(1,),
                                 padding=[(k - 1, 0)], dimension_numbers=('NWC', 'WIO', 'NWC'),
                                 feature_group_count=c)
    return y if b is None else y + b.astype(x.dtype)

def rg_lru(x, w_a, b_a, w_x, b_x, lam):
    bsz, s, w = x.shape
    xf = x.astype(F32)
    xb = xf.reshape(bsz, s, LRU_BLOCKS, LRU_BLOCK_W)
    r = jax.nn.sigmoid(jnp.einsum('bsnc,ncd->bsnd', xb, w_a.astype(F32)).reshape(bsz, s, w) + b_a.astype(F32))
    i = jax.nn.sigmoid(jnp.einsum('bsnc,ncd->bsnd', xb, w_x.astype(F32)).reshape(bsz, s, w) + b_x.astype(F32))
    log_a = -LRU_C * r * jax.nn.softplus(-lam.astype(F32))
    a = jnp.exp(log_a)
    mult = jnp.sqrt(-jnp.expm1(2.0 * log_a))
    mult = jnp.where(jnp.arange(s)[None, :, None] == 0, 1.0, mult)
    drive = mult * i * xf

    def combine(c1, c2):
        a1, b1 = c1
        a2, b2 = c2
        return a1 * a2, a2 * b1 + b2

    _, h = lax.associative_scan(combine, (a, drive), axis=1)
    return h.astype(x.dtype)

def dsa_attention(c_q, c_kv, k_idx, w_idx, q_norm, w_uq, w_uqi, kv_norm, w_uk, w_uv):
    bsz, s, _ = c_q.shape
    n_blk = s // Q_BLOCK
    topk = min(DSA_TOPK_MAX, s // 4)
    cq = rmsnorm(c_q, q_norm)
    ckv = rmsnorm(c_kv, kv_norm)
    q = jnp.einsum('bsr,rhd->bshd', cq, w_uq)
    q_lat = jnp.einsum('bshd,rhd->bshr', q, w_uk) * (DSA_HEAD_DIM ** -0.5)
    q_idx = jnp.einsum('bsr,rhd->bshd', cq, w_uqi)
    w_h = w_idx * ((IDX_HEADS ** -0.5) * (IDX_DIM ** -0.5))

    def to_blocks(t):
        return jnp.moveaxis(t.reshape(bsz, n_blk, Q_BLOCK, *t.shape[2:]), 1, 0)

    starts = jnp.arange(n_blk, dtype=jnp.int32) * Q_BLOCK
    key_pos = jnp.arange(s, dtype=jnp.int32)
    gather = jax.vmap(lambda src, idx: src[idx])

    def block(args):
        ql, qi, wi, start = args
        qpos = start + jnp.arange(Q_BLOCK, dtype=jnp.int32)
        causal = key_pos[None, :] <= qpos[:, None]
        logits = jnp.einsum('bqhd,bsd->bqhs', qi, k_idx).astype(F32)
        score = jnp.einsum('bqhs,bqh->bqs', jax.nn.relu(logits), wi.astype(F32))
        score = jnp.where(causal[None], score, -jnp.inf)
        _, sel = lax.top_k(score, topk)
        valid = sel <= qpos[None, :, None]
        kv_sel = gather(ckv, sel)
        att = jnp.einsum('bqhr,bqkr->bqhk', ql, kv_sel).astype(F32)
        att = jnp.where(valid[:, :, None, :], att, -jnp.inf)
        p = jax.nn.softmax(att, axis=-1).astype(ckv.dtype)
        return jnp.einsum('bqhk,bqkr->bqhr', p, kv_sel)

    o_lat = lax.map(block, (to_blocks(q_lat), to_blocks(q_idx), to_blocks(w_h), starts))
    o_lat = jnp.moveaxis(o_lat, 0, 1).reshape(bsz, s, DSA_HEADS, DSA_KV_RANK)
    o = jnp.einsum('bshr,rhd->bshd', o_lat, w_uv)
    return o.reshape(bsz, s, DSA_HEADS * DSA_HEAD_DIM)

def chunk_gated_delta_rule(q, k, v, g, beta):
    bsz, s, h, dk = q.shape
    dv = v.shape[-1]
    c = GDN_CHUNK
    n = s // c

    def chunks(t):
        return t.reshape(bsz, n, c, h, -1).transpose(0, 3, 1, 2, 4)

    qc, kc, vc = chunks(q * (dk ** -0.5)), chunks(k), chunks(v)
    gc = jnp.cumsum(g.reshape(bsz, n, c, h).transpose(0, 3, 1, 2), axis=-1)
    bc = beta.reshape(bsz, n, c, h).transpose(0, 3, 1, 2)[..., None]
    incl = jnp.tril(jnp.ones((c, c), dtype=bool))
    strict = jnp.tril(jnp.ones((c, c), dtype=bool), -1)
    diff = gc[..., :, None] - gc[..., None, :]
    decay = jnp.where(incl, jnp.exp(jnp.where(incl, diff, 0.0)), 0.0)
    kb = kc * bc
    a_low = jnp.where(strict, jnp.einsum('bhnik,bhnjk->bhnij', kb, kc) * decay, 0.0)
    rhs = jnp.concatenate([vc * bc, kb * jnp.exp(gc)[..., None]], axis=-1)
    sol = lax.linalg.triangular_solve(a_low + jnp.eye(c, dtype=F32), rhs, left_side=True,
                                      lower=True, unit_diagonal=True)
    u, w = sol[..., :dv], sol[..., dv:]
    qk = jnp.einsum('bhnik,bhnjk->bhnij', qc, kc) * decay
    q_dec = qc * jnp.exp(gc)[..., None]
    k_tail = kc * jnp.exp(gc[..., -1:] - gc)[..., None]
    g_tot = jnp.exp(gc[..., -1])
    xs = tuple(jnp.moveaxis(t, 2, 0) for t in (u, w, qk, q_dec, k_tail, g_tot))

    def step(state, inp):
        u_n, w_n, qk_n, qd_n, kt_n, gt_n = inp
        v_new = u_n - jnp.einsum('bhck,bhkv->bhcv', w_n, state)
        o_n = jnp.einsum('bhck,bhkv->bhcv', qd_n, state) + jnp.einsum('bhcj,bhjv->bhcv', qk_n, v_new)
        state = state * gt_n[..., None, None] + jnp.einsum('bhck,bhcv->bhkv', kt_n, v_new)
        return state, o_n

    s0 = jnp.zeros((bsz, h, dk, dv), F32)
    _, o = lax.scan(step, s0, xs)
    return o.transpose(1, 0, 3, 2, 4).reshape(bsz, s, h, dv)

def gated_deltanet(q, k, v, b, a, z, conv_w, a_log, dt_bias, o_norm):
    bsz, s, _ = q.shape
    qkv = jax.nn.silu(causal_dwconv(jnp.concatenate([q, k, v], axis=-1), conv_w)).astype(F32)
    qf, kf, vf = jnp.split(qkv, [GDN_HEADS * GDN_DK, 2 * GDN_HEADS * GDN_DK], axis=-1)
    qf = l2norm(qf.reshape(bsz, s, GDN_HEADS, GDN_DK))
    kf = l2norm(kf.reshape(bsz, s, GDN_HEADS, GDN_DK))
    vf = vf.reshape(bsz, s, GDN_HEADS, GDN_DV)
    beta = jax.nn.sigmoid(b.astype(F32))
    g = -jnp.exp(a_log.astype(F32)) * jax.nn.softplus(a.astype(F32) + dt_bias.astype(F32))
    o = chunk_gated_delta_rule(qf, kf, vf, g, beta)
    o = rmsnorm(o, o_norm) * jax.nn.silu(z.astype(F32).reshape(bsz, s, GDN_HEADS, GDN_DV))
    return o.reshape(bsz, s, GDN_HEADS * GDN_DV).astype(z.dtype)

def memory_xattn(h, m, w_q, w_kv, w_o):
    bsz, s, _ = h.shape
    n_mem = m.shape[1]
    q = (h @ w_q).reshape(bsz, s, XATTN_HEADS, XATTN_HEAD_DIM)
    kv = (m @ w_kv).reshape(bsz, n_mem, 2, XATTN_HEADS, XATTN_HEAD_DIM)
    att = jnp.einsum('bshd,bmhd->bhsm', q, kv[:, :, 0]).astype(F32) * (XATTN_HEAD_DIM ** -0.5)
    p = jax.nn.softmax(att, axis=-1).astype(h.dtype)
    o = jnp.einsum('bhsm,bmhd->bshd', p, kv[:, :, 1]).reshape(bsz, s, XATTN_HEADS * XATTN_HEAD_DIM)
    return o @ w_o

def conv_ffn(h, w_up, conv_w, w_down):
    u = causal_dwconv(h @ w_up, conv_w)
    gate, up = jnp.split(u, 2, axis=-1)
    return (jax.nn.silu(gate) * up) @ w_down

def setup_inputs(seed: int = 0) -> dict:
    key = jax.random.key(seed)
    ks = iter(jax.random.split(key, 48))
    L, D = DEPTH, D_MODEL

    def nrm(shape, scale):
        return jax.random.normal(next(ks), shape, F32) * scale

    def gain(shape):
        return 1.0 + 0.02 * jax.random.normal(next(ks), shape, F32)

    a0 = jax.random.uniform(next(ks), (L, LRU_WIDTH), F32, minval=0.9, maxval=0.999)
    s_root = a0 ** (1.0 / LRU_C)
    lru_lambda = jnp.log(s_root) - jnp.log1p(-s_root)
    dt = jnp.exp(jax.random.uniform(next(ks), (L, GDN_HEADS), F32, minval=float(np.log(1e-3)), maxval=float(np.log(1e-1))))
    gdn_dt_bias = dt + jnp.log(-jnp.expm1(-dt))
    gdn_a_log = jnp.log(jax.random.uniform(next(ks), (L, GDN_HEADS), F32, minval=1.0, maxval=16.0))

    return {
        'x': nrm((BATCH, SEQ, D), 1.0),
        'mem': nrm((BATCH, N_MEM, D), 1.0),
        'ln_mix': gain((L, D)),
        'w_in': nrm((L, D, N_IN), D ** -0.5),
        'conv_a_w': nrm((L, CONV_A, LRU_WIDTH), CONV_A ** -0.5),
        'conv_a_b': nrm((L, LRU_WIDTH), 0.02),
        'lru_wa': nrm((L, LRU_BLOCKS, LRU_BLOCK_W, LRU_BLOCK_W), LRU_BLOCK_W ** -0.5),
        'lru_ba': nrm((L, LRU_WIDTH), 0.02),
        'lru_wx': nrm((L, LRU_BLOCKS, LRU_BLOCK_W, LRU_BLOCK_W), LRU_BLOCK_W ** -0.5),
        'lru_bx': nrm((L, LRU_WIDTH), 0.02),
        'lru_lambda': lru_lambda,
        'dsa_q_norm': gain((L, DSA_Q_RANK)),
        'dsa_w_uq': nrm((L, DSA_Q_RANK, DSA_HEADS, DSA_HEAD_DIM), DSA_Q_RANK ** -0.5),
        'dsa_w_uqi': nrm((L, DSA_Q_RANK, IDX_HEADS, IDX_DIM), DSA_Q_RANK ** -0.5),
        'dsa_kv_norm': gain((L, DSA_KV_RANK)),
        'dsa_w_uk': nrm((L, DSA_KV_RANK, DSA_HEADS, DSA_HEAD_DIM), DSA_KV_RANK ** -0.5),
        'dsa_w_uv': nrm((L, DSA_KV_RANK, DSA_HEADS, DSA_HEAD_DIM), DSA_KV_RANK ** -0.5),
        'gdn_conv_w': nrm((L, CONV_C, 2 * GDN_HEADS * GDN_DK + GDN_HEADS * GDN_DV), CONV_C ** -0.5),
        'gdn_a_log': gdn_a_log,
        'gdn_dt_bias': gdn_dt_bias,
        'gdn_o_norm': gain((L, GDN_DV)),
        'p_a': nrm((L, LRU_WIDTH, D), LRU_WIDTH ** -0.5),
        'p_b': nrm((L, DSA_HEADS * DSA_HEAD_DIM, D), (DSA_HEADS * DSA_HEAD_DIM) ** -0.5),
        'p_c': nrm((L, GDN_HEADS * GDN_DV, D), (GDN_HEADS * GDN_DV) ** -0.5),
        'w_o': nrm((L, D, D), D ** -0.5),
        'ln_mem': gain((L, D)),
        'mem_norm': gain((L, D)),
        'x_wq': nrm((L, D, XATTN_HEADS * XATTN_HEAD_DIM), D ** -0.5),
        'x_wkv': nrm((L, D, 2 * XATTN_HEADS * XATTN_HEAD_DIM), D ** -0.5),
        'x_wo': nrm((L, XATTN_HEADS * XATTN_HEAD_DIM, D), (XATTN_HEADS * XATTN_HEAD_DIM) ** -0.5),
        'ln_ffn': gain((L, D)),
        'ffn_w_up': nrm((L, D, 2 * D_FF), D ** -0.5),
        'ffn_conv_w': nrm((L, CONV_F, 2 * D_FF), CONV_F ** -0.5),
        'ffn_w_down': nrm((L, D_FF, D), D_FF ** -0.5),
        'ln_f': gain((D,)),
    }

def reference(x, mem, ln_mix, w_in, conv_a_w, conv_a_b, lru_wa, lru_ba, lru_wx, lru_bx, lru_lambda,
              dsa_q_norm, dsa_w_uq, dsa_w_uqi, dsa_kv_norm, dsa_w_uk, dsa_w_uv,
              gdn_conv_w, gdn_a_log, gdn_dt_bias, gdn_o_norm,
              p_a, p_b, p_c, w_o, ln_mem, mem_norm, x_wq, x_wkv, x_wo,
              ln_ffn, ffn_w_up, ffn_conv_w, ffn_w_down, ln_f):
    bsz, s, d = x.shape
    for l in range(DEPTH):
        h = rmsnorm(x, ln_mix[l])
        (a_x, a_gate, c_q, c_kv, k_idx, w_idx, g_q, g_k, g_v, g_b, g_a, g_z,
         gate_logits) = jnp.split(h @ w_in[l], IN_OFFSETS, axis=-1)
        y_a = jax.nn.gelu(a_gate) * rg_lru(causal_dwconv(a_x, conv_a_w[l], conv_a_b[l]),
                                           lru_wa[l], lru_ba[l], lru_wx[l], lru_bx[l], lru_lambda[l])
        y_b = dsa_attention(c_q, c_kv, k_idx, w_idx, dsa_q_norm[l], dsa_w_uq[l], dsa_w_uqi[l],
                            dsa_kv_norm[l], dsa_w_uk[l], dsa_w_uv[l])
        y_c = gated_deltanet(g_q, g_k, g_v, g_b, g_a, g_z, gdn_conv_w[l], gdn_a_log[l],
                             gdn_dt_bias[l], gdn_o_norm[l])
        gates = jax.nn.sigmoid(gate_logits.reshape(bsz, s, N_BRANCH, d))
        merged = (gates[:, :, 0] * (y_a @ p_a[l]) + gates[:, :, 1] * (y_b @ p_b[l])
                  + gates[:, :, 2] * (y_c @ p_c[l]))
        x = x + merged @ w_o[l]
        h = rmsnorm(x, ln_mem[l])
        x = x + memory_xattn(h, rmsnorm(mem, mem_norm[l]), x_wq[l], x_wkv[l], x_wo[l])
        h = rmsnorm(x, ln_ffn[l])
        x = x + conv_ffn(h, ffn_w_up[l], ffn_conv_w[l], ffn_w_down[l])
    return rmsnorm(x, ln_f)


_drawn_inputs = setup_inputs


def setup_inputs(seed=0):
    import zlib

    import numpy as np

    out = dict(_drawn_inputs(seed))
    spreads = {}
    factors = {'ln_mix': 2.813,
     'lru_ba': 8.0,
     'lru_bx': 8.0,
     'dsa_q_norm': 4.705,
     'dsa_kv_norm': 8.0,
     'gdn_o_norm': 8.0,
     'ln_mem': 8.0,
     'mem_norm': 8.0,
     'ln_ffn': 12.116,
     'ln_f': 8.233}
    for name, (base, spread) in spreads.items():
        noise = np.random.default_rng([zlib.crc32(name.encode()), seed]).standard_normal(out[name].shape)
        drawn = base * np.exp(spread * noise) if base else spread * noise
        out[name] = __import__('jax').numpy.asarray(drawn.astype(out[name].dtype))
    for name, factor in factors.items():
        out[name] = (out[name] * factor).astype(out[name].dtype)
    return out
```

```python
from contextlib import ExitStack

import numpy as np

import concourse.bass as bass
from concourse import mybir

F32 = mybir.dt.float32
ALU = mybir.AluOpType
ACT = mybir.ActivationFunctionType
AX = mybir.AxisListType

P = 128
T = 256
NT = T // P
D = 2048
KC = D // P
N_MEM = 256
EPS = 1e-6
LRU_CH = 8
LRU_C = 8.0
QR, KVR = 4, 2
HEADS = 8
IDX_DIM = 64
TOPK = min(256, T // 4)
XHEADS = 4
FF_CH = 44
DOWN_BLOCKS = 22
LEVELS = 7
WSLOTS = 4
NEG = -1.0e30
TAKEN = -float(2.0 ** 127)

Z_GZ, Z_AGATE, Z_AX, Z_CQ, Z_CKV, Z_KIDX, Z_SMALL, Z_Q, Z_K, Z_V = 0, 8, 16, 24, 28, 30, 31, 32, 40, 48
Z_CH = 56
Z_FLAT = 32

C_ID, C_ONE, C_TRI, C_MASK = 0, 128, 256, 384
C_NEG = C_MASK + LEVELS * P
C_EPS = C_NEG + NT * T
C_N = C_EPS + 8

PARAMS = [("ln_mix", 16), ("mem_norm", 16), ("ln_mem", 16), ("ln_ffn", 16), ("ln_f", 16),
          ("conv_a_w", 4 * 8), ("conv_a_b", 8), ("lru_ba", 8), ("lru_bx", 8), ("lru_lambda", 8),
          ("dsa_q_norm", 4), ("dsa_kv_norm", 2), ("gdn_conv_w", 4 * 24), ("gdn_o_norm", 1),
          ("ffn_conv_w", 3 * 88), ("gdn_a_log", 8), ("gdn_dt_bias", 8)]
PCOL, _at = {}, 0
for _n, _w in PARAMS:
    PCOL[_n] = _at
    _at += _w
P_N = _at

R_MEM = 0
R_IN = R_MEM + 8 // WSLOTS
R_DSA = R_IN + Z_CH // WSLOTS
R_AB = R_DSA + 8 // WSLOTS
R_C = R_AB + 48 // WSLOTS
R_WO = R_C + 24 // WSLOTS
R_X = R_WO + KC // WSLOTS
R_UP = R_X + 8 // WSLOTS
R_DOWN = R_UP + 2 * FF_CH // WSLOTS


def build(nc, dr, out):
    ctx = ExitStack()
    with ctx:
        def sb(name, shape):
            return ctx.enter_context(nc.sbuf_tensor(name, shape, F32))

        def sem(name):
            return ctx.enter_context(nc.semaphore(name))

        consts = sb("consts", [P, C_N])
        prm = sb("prm", [P, P_N])
        xT = sb("xT", [P, KC, T])
        hT = sb("hT", [P, KC, T])
        mem_k = sb("mem_k", [P, XHEADS, N_MEM])
        mem_v = sb("mem_v", [P, NT, XHEADS * P])
        z = sb("z", [P, Z_CH, T])
        W = sb("W", [P, 56, T])
        wring = [sb(f"wring{s}", [P, DOWN_BLOCKS * P]) for s in range(WSLOTS)]
        tiny = sb("tiny", [P, 640])
        G = [ctx.enter_context(nc.psum_tensor(f"G{i}", [P, 512], F32)) for i in range(2)]
        M = [ctx.enter_context(nc.psum_tensor(f"M{i}", [P, 512], F32)) for i in range(6)]

        ident = consts[:, C_ID:C_ID + P]
        ones = consts[:, C_ONE:C_ONE + P]
        tri = consts[:, C_TRI:C_TRI + P]
        negmask = consts[:, C_NEG:C_NEG + NT * T].rearrange("p (m t) -> p m t", m=NT)
        eps = consts[:, C_EPS:C_EPS + 1]

        def level_mask(l):
            return consts[:, C_MASK + l * P:C_MASK + (l + 1) * P]

        def col(name, c):
            return prm[:, bass.ds(PCOL[name] + c, 1)]

        def flat(ap):
            return ap.rearrange("p c t -> p (c t)")

        def wide(lo, hi):
            return flat(W[:, lo:hi, :])

        sq = W[:, 0:KC, :]
        rt = wide(16, 17)
        mem_in, mem_h = z[:, 0:KC, :], z[:, KC:2 * KC, :]
        ctmp = [wide(40, 41), wide(41, 42)]
        xc, lr, li, la, lt = (W[:, 8 * i:8 * i + 8, :] for i in range(5))
        dsq, drt = W[:, 42:48, :], wide(48, 50)
        qF, kF, qiF = W[:, 0:8, :], W[:, 8:16, :], W[:, 24:28, :]
        vT = wide(16, 24).rearrange("p (m n) -> p m n", m=NT)
        score = W[:, 28:30, :]
        rl = [wide(30, 31), wide(31, 32)]
        sbias = W[:, 32:34, :]
        att_s = [W[:, 34:36, :], W[:, 36:38, :]]
        att_pT = [W[:, 38:40, :], W[:, 40:42, :]]
        att_q = [wide(42, 43), wide(43, 44)]
        att_v = [wide(44, 45).rearrange("p (m n) -> p m n", m=NT), wide(45, 46).rearrange("p (m n) -> p m n", m=NT)]
        yB = W[:, 48:56, :]
        xqF = W[:, 0:4, :]
        yX = W[:, 48:52, :]
        yA = z[:, Z_AGATE:Z_AGATE + 8, :]
        yC = z[:, Z_GZ:Z_GZ + 8, :]
        merged = z[:, 16:32, :]
        ff = z[:, 0:FF_CH, :]

        def quad(ap):
            return ap.rearrange("p (q n) -> p q n", q=4)

        g_sq, g_rt = wide(0, 4), wide(4, 8)
        g_ug, g_db = wide(0, 2), wide(2, 4)
        g_bd, g_at = wide(0, 2), wide(2, 4)
        g_dec, g_qk = wide(4, 6), wide(6, 8)
        g_q2, g_k2, g_v2 = wide(8, 10), wide(10, 12), wide(12, 14)
        g_eg, g_vt = wide(14, 16), wide(16, 18)
        g_kt, g_ktail = wide(18, 19), wide(19, 20)
        g_kw, g_qd = wide(20, 22), wide(22, 24)
        EBUF = 4
        g_e = [wide(24 + 2 * i, 26 + 2 * i) for i in range(EBUF)]
        sg, gt = wide(32, 34), wide(34, 36)
        g_t, g_tt, g_ms, g_tb = wide(38, 40), wide(40, 42), wide(42, 44), wide(44, 46)
        g_v0, g_s, g_r, g_v1 = wide(46, 47), wide(47, 48), wide(36, 37), wide(37, 38)
        g_osq, g_ort = wide(24, 26), wide(26, 28)

        _t = [0]

        def small(n):
            _t[0] += n
            return tiny[:, _t[0] - n:_t[0]]

        tokc = small(64).rearrange("p (m n) -> p m n", m=NT)
        widx = small(16).rearrange("p (m n) -> p m n", m=NT)
        beta = small(16)
        gdec = small(16)
        gcum = small(16)
        sp_x, sp_e, sp_s, sp_z, sp_p = (small(24) for _ in range(5))
        sp = small(24)
        ea = small(8)
        lam_n, lam_p = small(8), small(8)
        top8 = small(16).rearrange("p (m n) -> p m n", m=NT)
        amax = [small(2), small(2)]
        asum = [small(2), small(2)]

        w_landed = [sem(f"w_landed{s}") for s in range(WSLOTS)]
        w_used = [sem(f"w_used{s}") for s in range(WSLOTS)]
        const_in, x_in, mem_loaded = sem("const_in"), sem("x_in"), sem("mem_loaded")
        n_sq, n_ss, n_rt, n_h = sem("n_sq"), sem("n_ss"), sem("n_rt"), sem("n_h")
        memk_mm, memk_ev = sem("memk_mm"), sem("memk_ev")
        memv_mm, memv_ev = sem("memv_mm"), sem("memv_ev")
        in_mm, in_ev = sem("in_mm"), sem("in_ev")
        xconv, qconv, qsilu = sem("xconv"), sem("qconv"), sem("qsilu")
        lat_sq, lat_ss, lat_rt, lat_n = sem("lat_sq"), sem("lat_ss"), sem("lat_rt"), sem("lat_n")
        tok_mm, tok_ev, sp_in, sp_ex, sp_done, beta_done = (sem(n) for n in
            ("tok_mm", "tok_ev", "sp_in", "sp_ex", "sp_done", "beta_done"))
        gcum_mm, gcum_ev = sem("gcum_mm"), sem("gcum_ev")
        lru_mm, lru_sig, lru_at, lru_m2, lru_root, gates_act, lru_done = (sem(n) for n in
            ("lru_mm", "lru_sig", "lru_at", "lru_m2", "lru_root", "gates_act", "lru_done"))
        prj_mm, prj_ev = sem("prj_mm"), sem("prj_ev")
        idx_mm, idx_relu, idx_acc, sel_done = sem("idx_mm"), sem("idx_relu"), sem("idx_acc"), sem("sel_done")
        a_stage, a_mm, a_max, a_exp, a_p, a_tr, a_pt, a_o, a_ev = (sem(n) for n in
            ("a_stage", "a_mm", "a_max", "a_exp", "a_p", "a_tr", "a_pt", "a_o", "a_ev"))
        d = {n: sem("d_" + n) for n in (
            "sq", "ss", "rt", "v2", "rank1", "qk", "bc", "vtr", "prod", "diff", "dec", "vt", "at", "kt",
            "e", "etr", "t", "m1", "ms", "x", "tb", "v0mm", "v0", "smm", "s", "ksmm", "r", "v1mm", "v1",
            "o", "osq", "oss", "ort", "y")}
        b_gate, b_exp, b_proj, b_sum = sem("b_gate"), sem("b_exp"), sem("b_proj"), sem("b_sum")
        o_mm, o_ev = sem("o_mm"), sem("o_ev")
        xq_mm, xq_ev, xo_mm, xo_ev = sem("xq_mm"), sem("xq_ev"), sem("xo_mm"), sem("xo_ev")
        up_mm, up_conv, up_silu, up_h = sem("up_mm"), sem("up_conv"), sem("up_silu"), sem("up_h")
        dn_mm, dn_ev = sem("dn_mm"), sem("dn_ev")
        act_turns, stored = sem("act_turns"), sem("stored")

        block = ctx.enter_context(nc.Block())

        def dyn(ap, i, n=1):
            return ap[:, bass.ds(i, n), :].rearrange("p c t -> p (c t)")

        @block.sync
        def _(sp_eng):
            def load(s, r, src, cols):
                sp_eng.wait_ge(w_used[s], r)
                sp_eng.dma_start(wring[s][:, 0:cols], src).then_inc(w_landed[s], 16)

            def job(name, i):
                return dr[name][bass.ds(i, 1)].rearrange("a p c -> p (a c)")

            for s in range(WSLOTS):
                sp_eng.dma_start(wring[s][:, 0:D], job("x_wk", s)).then_inc(w_landed[s], 16)
            for s in range(WSLOTS):
                load(s, R_MEM + 1, job("x_wv", s), D)
            with sp_eng.Fori(0, Z_CH // WSLOTS) as r:
                for s in range(WSLOTS):
                    load(s, R_IN + r, job("w_in", r * WSLOTS + s), D)
            load(0, R_DSA, dr["lru_wa"], LRU_CH * P)
            load(1, R_DSA, dr["lru_wx"], LRU_CH * P)
            load(2, R_DSA, dr["w_uqi"], 16 * P)
            load(3, R_DSA, dr["w_uk"], 16 * P)
            load(0, R_DSA + 1, job("w_uq", 0), D)
            load(1, R_DSA + 1, job("w_uq", 1), D)
            load(2, R_DSA + 1, job("w_uv", 0), 8 * P)
            load(3, R_DSA + 1, job("w_uv", 1), 8 * P)
            with sp_eng.Fori(0, 4) as it:
                for j in range(4):
                    br, pair = j // 2, it * 2 + j % 2
                    for i in range(3):
                        n = 3 * j + i
                        src = job("w_gate", br * KC + pair * 2 + i) if i < 2 else job("p_ab"[0:2] + "ab"[br], pair)
                        load(n % WSLOTS, R_AB + it * 3 + n // WSLOTS, src, D)
            with sp_eng.Fori(0, 2) as it:
                for j in range(4):
                    pair = it * 4 + j
                    for i in range(3):
                        n = 3 * j + i
                        src = job("w_gate", 2 * KC + pair * 2 + i) if i < 2 else job("p_c", pair)
                        load(n % WSLOTS, R_C + it * 3 + n // WSLOTS, src, D)
            with sp_eng.Fori(0, KC // WSLOTS) as r:
                for s in range(WSLOTS):
                    load(s, R_WO + r, job("w_o", r * WSLOTS + s), D)
            for s in range(WSLOTS):
                load(s, R_X, job("x_wq", s), D)
            for s in range(WSLOTS):
                load(s, R_X + 1, job("x_wo", s), D)
            with sp_eng.Fori(0, 2 * FF_CH // WSLOTS) as r:
                for s in range(WSLOTS):
                    load(s, R_UP + r, job("w_up", (s % 2) * FF_CH + r * 2 + s // 2), D)
            with sp_eng.Fori(0, 2 * KC // WSLOTS) as r:
                for s in range(WSLOTS):
                    src = dr["w_down"][bass.ds(r * 2 + s // 2, 1)].rearrange("a p c -> p (a c)")
                    n = DOWN_BLOCKS * P
                    load(s, R_DOWN + r, src[:, (s % 2) * n:(s % 2 + 1) * n], n)
            sp_eng.wait_ge(n_h, 5 * KC)
            sp_eng.dma_start(out, hT[:]).then_inc(stored, 16)
            sp_eng.wait_ge(stored, 16)

        @block.tensor
        def _(pe):
            def landed(s, r):
                pe.wait_ge(w_landed[s], (r + 1) * 16)

            def norm_sums(n):
                pe.wait_ge(n_sq, 4 * n + 4)
                for c in range(KC):
                    q = pe.matmul(M[0][:, 0:T], ones, sq[:, c, :], start=c == 0, stop=c == KC - 1)
                q.then_inc(n_ss, 1)

            def chunk(dst, s, first, count, rhs, step=P):
                for k in range(count):
                    q = pe.matmul(dst, wring[s][:, (first + k) * P:(first + k + 1) * P], rhs(k),
                                  start=k == 0, stop=k == count - 1)
                return q

            pe.wait_ge(const_in, 32)
            norm_sums(0)
            norm_sums(1)
            pe.wait_ge(n_h, KC)
            for s in range(WSLOTS):
                landed(s, R_MEM)
                if s >= 2:
                    pe.wait_ge(memk_ev, s - 1)
                chunk(G[s % 2][:, 0:T], s, 0, KC, lambda k: mem_h[:, k, :]).then_inc(memk_mm, 1)
                pe.drain().then_inc(w_used[s], 1)
            for s in range(WSLOTS):
                landed(s, R_MEM + 1)
                for kk in range(4):
                    k = 4 * s + kk
                    for m in range(NT):
                        q = pe.matmul(M[1 + m][:], mem_h[:, k, m * P:(m + 1) * P],
                                      wring[s][:, kk * 512:(kk + 1) * 512], start=k == 0, stop=k == KC - 1)
                q.then_inc(w_used[s], 1)
            pe.drain().then_inc(memv_mm, 1)
            pe.wait_ge(n_h, 2 * KC)
            pe.wait_ge(memk_ev, 4)
            with pe.Fori(0, Z_CH // WSLOTS) as r:
                for s in range(WSLOTS):
                    landed(s, R_IN + r)
                    pe.wait_ge(in_ev, r * WSLOTS + s + 1)
                    q = chunk(G[s % 2][:, 0:T], s, 0, KC, lambda k: hT[:, k, :])
                    q.then_inc(in_mm, 1)
                    pe.drain().then_inc(w_used[s], 1)
            pe.wait_ge(lat_sq, 1)
            for c in range(QR):
                pe.matmul(M[0][:, 0:T], ones, dsq[:, c, :], start=c == 0, stop=c == QR - 1)
            for c in range(KVR):
                q = pe.matmul(M[0][:, T:2 * T], ones, dsq[:, QR + c, :], start=c == 0, stop=c == KVR - 1)
            q.then_inc(lat_ss, 1)
            pe.wait_ge(memv_ev, 2)
            for m in range(NT):
                q = pe.transpose(M[1][:, m * 32:(m + 1) * 32], z[0:32, Z_SMALL, m * P:(m + 1) * P], ident[0:32, 0:32])
            q.then_inc(tok_mm, 1)
            pe.wait_ge(sp_done, 1)
            for m in range(NT):
                q = pe.matmul(M[2][:, m * 8:(m + 1) * 8], tri, gdec[:, m * 8:(m + 1) * 8], start=True, stop=True)
            q.then_inc(gcum_mm, 1)
            pe.wait_ge(xconv, LRU_CH)
            for j in range(2 * LRU_CH):
                s, c = j // LRU_CH, j % LRU_CH
                if c == 0:
                    landed(s, R_DSA)
                bank = M[3 + j % 3]
                if j >= 3:
                    pe.wait_ge(lru_sig, j - 2)
                q = pe.matmul(bank[:, 0:T], wring[s][:, c * P:(c + 1) * P], xc[:, c, :], start=True, stop=True)
                q.then_inc(lru_mm, 1)
                if c == LRU_CH - 1:
                    pe.drain().then_inc(w_used[s], 1)
            pe.wait_ge(lat_n, 1)
            pe.wait_ge(lru_sig, 2 * LRU_CH)
            pe.wait_ge(gcum_ev, 1)
            e = 0

            def proj_bank():
                if e >= 4:
                    pe.wait_ge(prj_ev, e - 3)
                return M[e % 4]

            for s, r, chunks, kn, rhs in ((2, R_DSA, 4, QR, Z_CQ), (3, R_DSA, 8, KVR, Z_CKV),
                                          (0, R_DSA + 1, 4, QR, Z_CQ), (1, R_DSA + 1, 4, QR, Z_CQ)):
                landed(s, r)
                for c in range(chunks):
                    if c % 2 == 0:
                        bank = proj_bank()
                    q = chunk(bank[:, (c % 2) * T:(c % 2 + 1) * T], s, c * kn, kn, lambda k: z[:, rhs + k, :])
                    if c % 2:
                        q.then_inc(prj_mm, 1)
                        e += 1
                pe.drain().then_inc(w_used[s], 1)
            landed(2, R_DSA + 1)
            landed(3, R_DSA + 1)
            for m in range(NT):
                for half in range(2):
                    bank = proj_bank()
                    for k in range(KVR):
                        q = pe.matmul(bank[:], z[:, Z_CKV + k, m * P:(m + 1) * P],
                                      wring[2 + k][:, half * 512:(half + 1) * 512], start=k == 0, stop=k == KVR - 1)
                    q.then_inc(prj_mm, 1)
                    e += 1
            n_proj = e
            pe.drain().then_inc(w_used[2], 1)
            pe.drain().then_inc(w_used[3], 1)
            pe.wait_ge(prj_ev, n_proj)
            for m in range(NT):
                for h in range(HEADS):
                    e = m * HEADS + h
                    if e >= 4:
                        pe.wait_ge(idx_relu, e - 3)
                    o = IDX_DIM * (h % 2)
                    pe.matmul(M[e % 4][:, 0:T], qiF[o:o + IDX_DIM, h // 2, m * P:(m + 1) * P],
                              z[o:o + IDX_DIM, Z_KIDX, :], start=True, stop=True).then_inc(idx_mm, 1)

            def attention(first, pairs, keys):
                with pe.Fori(0, pairs) as i:
                    n = i * 2 + first
                    for u in range(2):
                        pe.wait_ge(a_stage, n + (u + 1))
                        pe.wait_ge(a_max, n + u + 1)
                        for m in range(NT):
                            q = pe.matmul(M[u][:, m * T:(m + 1) * T], att_q[u][:, m * P:(m + 1) * P],
                                          dyn(keys, i * 2 + u), start=True, stop=True)
                        q.then_inc(a_mm, 1)
                    for u in range(2):
                        pe.wait_ge(a_p, n + (u + 1))
                        for m in range(NT):
                            for k in range(NT):
                                q = pe.transpose(M[2 + u][:, k * T + m * P:k * T + (m + 1) * P],
                                                 att_s[u][:, m, k * P:(k + 1) * P], ident)
                        q.then_inc(a_tr, 1)
                    for u in range(2):
                        pe.wait_ge(a_pt, n + (u + 1))
                        for k in range(NT):
                            q = pe.matmul(M[4 + u][:, 0:T], att_v[u][:, k, :], att_pT[u][:, k, :],
                                          start=k == 0, stop=k == NT - 1)
                        q.then_inc(a_o, 1)

            pe.wait_ge(idx_relu, 2 * HEADS)
            attention(0, HEADS // 2, kF)

            y_of = {0: yA, 1: yB, 2: yC}

            def branch(n, slot0, base, r0, y, lo, hi):
                for b in range(lo, hi):
                    i = min(b // 16, 2)
                    s, r = (slot0 + i) % WSLOTS, r0 + (slot0 + i) // WSLOTS
                    if b == 0:
                        pe.wait_ge(b_exp, n + base + 1)
                    if b == 32:
                        pe.wait_ge(b_sum, n + base + 1)
                    if b in (0, 16, 32):
                        landed(s, r)
                    if b < 32:
                        k = b % 16
                        q = pe.matmul(G[0][:, i * T:(i + 1) * T], wring[s][:, k * P:(k + 1) * P], hT[:, k, :],
                                      start=k == 0, stop=k == 15)
                    else:
                        c, k = (b - 32) // 8, b % 8
                        q = pe.matmul(G[1][:, c * T:(c + 1) * T], wring[s][:, (c * 8 + k) * P:(c * 8 + k + 1) * P],
                                      y[:, k, :], start=k == 0, stop=k == 7)
                    if b in (15, 31, 47):
                        q.then_inc(w_used[s], 1)
                    if b == 31:
                        pe.drain().then_inc(b_gate, 1)
                    if b == 47:
                        pe.drain().then_inc(b_proj, 1)

            pe.wait_ge(a_ev, 1 + HEADS)
            pe.wait_ge(lru_done, 1)
            with pe.Fori(0, HEADS // 2) as it:
                def unit(j, lo, hi):
                    branch(it * 4, 3 * j, j, R_AB + it * 3, y_of[j // 2], lo, hi)

                pe.wait_ge(d["sq"], it + 1)
                for i in range(2):
                    q = pe.matmul(M[3 * i][:], ones, g_sq[:, i * 512:(i + 1) * 512], start=True, stop=True)
                q.then_inc(d["ss"], 1)
                pe.wait_ge(d["v2"], it + 1)
                for p in range(4):
                    q = pe.transpose(M[2][:, p * P:(p + 1) * P], g_v2[:, p * P:(p + 1) * P], ident)
                q.then_inc(d["vtr"], 1)
                unit(0, 0, 10)
                pe.wait_ge(d["rank1"], it + 1)
                pe.matmul(M[3][:], ones, g_ug, start=True, stop=True)
                pe.matmul(M[4][:], ones, g_db, start=True, stop=True).then_inc(d["bc"], 1)
                unit(0, 10, 18)
                pe.wait_ge(d["qk"], it + 1)
                for u in range(2):
                    pe.transpose(M[5][:, u * P:(u + 1) * P], g_k2[:, 2 * u * P:(2 * u + 1) * P], ident)
                for p in range(4):
                    ks = g_k2[:, p * P:(p + 1) * P]
                    pe.matmul(M[0][:, p * P:(p + 1) * P], ks, ks, start=True, stop=True)
                    q = pe.matmul(M[1][:, p * P:(p + 1) * P], ks, g_q2[:, p * P:(p + 1) * P], start=True, stop=True)
                q.then_inc(d["prod"], 1)
                unit(0, 18, 38)
                pe.wait_ge(d["e"], it * LEVELS + 1)
                pe.wait_ge(d["vt"], it + 1)
                for p in range(4):
                    q = pe.transpose(M[2][:, p * P:(p + 1) * P], g_e[0][:, p * P:(p + 1) * P], ident)
                q.then_inc(d["etr"], 1)
                fill = [(0, 38, 48), (1, 0, 10), (1, 10, 20), (1, 20, 30), (1, 30, 40), (1, 40, 48),
                        (2, 0, 10), (2, 10, 20), (2, 20, 30), (2, 30, 38), (2, 38, 48), (3, 0, 8), (3, 8, 16)]
                unit(*fill[0])
                for l in range(1, LEVELS):
                    e = g_e[l % EBUF]
                    pe.wait_ge(d["t"], it * LEVELS + l)
                    pe.wait_ge(d["e"], it * LEVELS + l + 1)
                    for p in range(4):
                        q = pe.matmul(M[3][:, p * P:(p + 1) * P], e[:, p * P:(p + 1) * P], g_t[:, p * P:(p + 1) * P],
                                      start=True, stop=True)
                    q.then_inc(d["m1"], 1)
                    unit(*fill[2 * l - 1])
                    pe.wait_ge(d["ms"], it * (LEVELS - 1) + l)
                    for p in range(4):
                        c = slice(p * P, (p + 1) * P)
                        if l < LEVELS - 1:
                            pe.matmul(M[4][:, c], g_tt[:, c], g_ms[:, c], start=True, stop=True)
                        q = pe.matmul(M[5][:, c], g_ms[:, c], g_tt[:, c], start=True, stop=True)
                    q.then_inc(d["x"], 1)
                    unit(*fill[2 * l])
                pe.wait_ge(d["tb"], it + 1)
                for u in range(2):
                    p = 2 * u
                    q = pe.matmul(M[0][:, u * P:(u + 1) * P], g_tb[:, p * P:(p + 1) * P], g_vt[:, p * P:(p + 1) * P],
                                  start=True, stop=True)
                q.then_inc(d["v0mm"], 1)
                unit(3, 16, 24)
                pe.wait_ge(d["v0"], it + 1)
                pe.wait_ge(d["kt"], it + 1)
                for u in range(2):
                    q = pe.matmul(M[2][:, u * P:(u + 1) * P], g_ktail[:, u * P:(u + 1) * P], g_v0[:, u * P:(u + 1) * P],
                                  start=True, stop=True)
                q.then_inc(d["smm"], 1)
                for u in range(2):
                    p = 2 * u
                    pe.matmul(M[1][:, p * P:(p + 1) * P], g_v0[:, u * P:(u + 1) * P], g_qk[:, p * P:(p + 1) * P],
                              start=True, stop=True)
                unit(3, 24, 32)
                pe.wait_ge(d["s"], it + 1)
                for u in range(2):
                    p = 2 * u + 1
                    q = pe.matmul(M[3][:, u * P:(u + 1) * P], g_kw[:, p * P:(p + 1) * P], g_s[:, u * P:(u + 1) * P],
                                  start=True, stop=True)
                q.then_inc(d["ksmm"], 1)
                unit(3, 32, 40)
                pe.wait_ge(d["r"], it + 1)
                for u in range(2):
                    p = 2 * u + 1
                    q = pe.matmul(M[4][:, u * P:(u + 1) * P], g_tb[:, p * P:(p + 1) * P], g_r[:, u * P:(u + 1) * P],
                                  start=True, stop=True)
                q.then_inc(d["v1mm"], 1)
                pe.wait_ge(d["v1"], it + 1)
                for u in range(2):
                    p = 2 * u + 1
                    pe.matmul(M[1][:, p * P:(p + 1) * P], g_s[:, u * P:(u + 1) * P], g_qd[:, p * P:(p + 1) * P],
                              start=True, stop=False)
                    q = pe.matmul(M[1][:, p * P:(p + 1) * P], g_v1[:, u * P:(u + 1) * P], g_qk[:, p * P:(p + 1) * P],
                                  start=False, stop=True)
                q.then_inc(d["o"], 1)
                unit(3, 40, 48)
                pe.wait_ge(d["osq"], it + 1)
                pe.matmul(M[2][:], ones, g_osq, start=True, stop=True).then_inc(d["oss"], 1)
            pe.wait_ge(d["y"], 1 + HEADS // 2)
            with pe.Fori(0, 2) as it:
                for j in range(4):
                    branch(it * 4, 3 * j, 16 + j, R_C + it * 3, yC, 0, 48)
            pe.wait_ge(b_sum, 1 + 24)
            with pe.Fori(0, KC // WSLOTS) as r:
                for s in range(WSLOTS):
                    landed(s, R_WO + r)
                    pe.wait_ge(o_ev, r * WSLOTS + s + 1)
                    chunk(G[s % 2][:, 0:T], s, 0, KC, lambda k: merged[:, k, :]).then_inc(o_mm, 1)
                    pe.drain().then_inc(w_used[s], 1)
            norm_sums(2)
            pe.wait_ge(n_h, 3 * KC)
            for s in range(WSLOTS):
                landed(s, R_X)
                if s >= 2:
                    pe.wait_ge(xq_ev, s - 1)
                chunk(G[s % 2][:, 0:T], s, 0, KC, lambda k: hT[:, k, :]).then_inc(xq_mm, 1)
                pe.drain().then_inc(w_used[s], 1)
            pe.wait_ge(xq_ev, 4)
            attention(HEADS, XHEADS // 2, mem_k)
            pe.wait_ge(a_ev, 1 + HEADS + XHEADS)
            for s in range(WSLOTS):
                landed(s, R_X + 1)
                for c in range(4):
                    n = 4 * s + c
                    if n >= 2:
                        pe.wait_ge(xo_ev, n - 1)
                    chunk(G[n % 2][:, 0:T], s, 4 * c, 4, lambda k: yX[:, k, :]).then_inc(xo_mm, 1)
                pe.drain().then_inc(w_used[s], 1)
            norm_sums(3)
            pe.wait_ge(n_h, 4 * KC)
            with pe.Fori(0, 2 * FF_CH // WSLOTS) as r:
                for s in range(WSLOTS):
                    landed(s, R_UP + r)
                    pe.wait_ge(up_conv, r * WSLOTS + s + 1)
                    chunk(G[s % 2][:, 0:T], s, 0, KC, lambda k: hT[:, k, :]).then_inc(up_mm, 1)
                    pe.drain().then_inc(w_used[s], 1)
            pe.wait_ge(up_h, FF_CH)
            with pe.Fori(0, 2 * KC // WSLOTS) as r:
                for s in range(WSLOTS):
                    landed(s, R_DOWN + r)
                    if s % 2 == 0:
                        pe.wait_ge(dn_ev, r * 2 + s // 2 + 1)
                    for k in range(DOWN_BLOCKS):
                        kk = (s % 2) * DOWN_BLOCKS + k
                        q = pe.matmul(G[s // 2][:, 0:T], wring[s][:, k * P:(k + 1) * P], ff[:, kk, :],
                                      start=kk == 0, stop=kk == FF_CH - 1)
                    q.then_inc(w_used[s], 1)
                    if s % 2:
                        pe.drain().then_inc(dn_mm, 1)
            norm_sums(4)

        @block.scalar
        def _(act):
            def hold(s, value):
                act.wait_ge(s, value)
                act.sem_inc(act_turns, 1)

            def norm(n, src):
                for q in range(4):
                    act.activation(flat(sq[:, 4 * q:4 * q + 4, :]), flat(src[:, 4 * q:4 * q + 4, :]),
                                   ACT.Square).then_inc(n_sq, 1)
                act.wait_ge(n_ss, n + 1)
                act.activation(rt, M[0][:, 0:T], ACT.Sqrt, bias=eps, scale=1.0 / D).then_inc(n_rt, 1)

            act.dma_start(mem_in, dr["mem"]).then_inc(mem_loaded, 16)
            act.dma_start(consts[:], dr["consts"]).then_inc(const_in, 16)
            act.dma_start(prm[:], dr["prm"]).then_inc(const_in, 16)
            act.dma_start(xT[:], dr["x"]).then_inc(x_in, 16)
            act.wait_ge(const_in, 32)
            act.wait_ge(mem_loaded, 16)
            norm(0, mem_in)
            act.wait_ge(x_in, 16)
            act.wait_ge(n_h, KC)
            norm(1, xT)
            for s in range(WSLOTS):
                act.wait_ge(memk_mm, s + 1)
                act.copy(mem_k[:, s, :], G[s % 2][:, 0:T]).then_inc(memk_ev, 1)
            act.wait_ge(memv_mm, 1)
            for m in range(NT):
                act.copy(mem_v[:, m, :], M[1 + m][:]).then_inc(memv_ev, 1)
            act.sem_inc(a_ev, 1)
            act.sem_inc(in_ev, 2)
            with act.Fori(0, Z_FLAT // WSLOTS) as r:
                for s in range(WSLOTS):
                    hold(in_mm, r * WSLOTS + s + 1)
                    act.copy(dyn(z, r * WSLOTS + s), G[s % 2][:, 0:T]).then_inc(in_ev, 1)
            with act.Fori(0, (Z_CH - Z_FLAT) // WSLOTS) as r:
                for s in range(WSLOTS):
                    c = r * WSLOTS + s
                    hold(in_mm, c + (Z_FLAT + 1))
                    act.copy(dyn(z, c + Z_FLAT), G[s % 2][:, 0:T]).then_inc(in_ev, 1)
                    hold(qconv, c + 1)
                    act.activation(dyn(z, c + Z_FLAT), ctmp[s % 2], ACT.Silu).then_inc(qsilu, 1)
            act.activation(flat(z[:, Z_GZ:Z_GZ + 8, :]), flat(z[:, Z_GZ:Z_GZ + 8, :]), ACT.Silu).then_inc(gates_act, 1)
            act.activation(flat(yA), flat(yA), ACT.Gelu_apprx_tanh).then_inc(gates_act, 1)
            act.activation(flat(dsq), flat(z[:, Z_CQ:Z_CQ + 6, :]), ACT.Square).then_inc(lat_sq, 1)
            act.wait_ge(lat_ss, 1)
            act.activation(drt[:, 0:T], M[0][:, 0:T], ACT.Sqrt, bias=eps, scale=1.0 / (QR * P)).then_inc(lat_rt, 1)
            act.activation(drt[:, T:2 * T], M[0][:, T:2 * T], ACT.Sqrt, bias=eps, scale=1.0 / (KVR * P)).then_inc(lat_rt, 1)
            act.wait_ge(sp_in, 1)
            act.activation(sp_e, sp_x, ACT.Abs)
            act.activation(ea, prm[:, PCOL["gdn_a_log"]:PCOL["gdn_a_log"] + 8], ACT.Exp)
            act.drain()
            act.activation(sp_e, sp_e, ACT.Exp, scale=-1.0).then_inc(sp_ex, 1)
            act.activation(beta.rearrange("p (m n) -> p m n", m=NT), tokc[:, :, 8:16], ACT.Sigmoid).then_inc(beta_done, 1)
            for j in range(2 * LRU_CH):
                c = j % LRU_CH
                act.wait_ge(lru_mm, j + 1)
                dst, b = (lr, "lru_ba") if j < LRU_CH else (li, "lru_bx")
                act.activation(dst[:, c, :], M[3 + j % 3][:, 0:T], ACT.Sigmoid, bias=col(b, c)).then_inc(lru_sig, 1)
            act.wait_ge(sp_done, 1)
            act.drain()
            for c in range(LRU_CH):
                act.activation(la[:, c, :], lr[:, c, :], ACT.Exp, scale=lam_n[:, c:c + 1])
                act.activation(lt[:, c, :], lr[:, c, :], ACT.Tanh, scale=lam_p[:, c:c + 1]).then_inc(lru_at, 1)
            act.wait_ge(lru_m2, 1)
            act.activation(flat(lr), flat(lt), ACT.Sqrt, scale=2.0).then_inc(lru_root, 1)
            act.wait_ge(lru_done, 1)
            dsts = ([flat(qiF[:, 2 * i:2 * i + 2, :]) for i in range(2)] + [flat(kF[:, 2 * i:2 * i + 2, :]) for i in range(4)]
                    + [flat(qF[:, 2 * i:2 * i + 2, :]) for i in range(4)]
                    + [vT[:, m, h * 512:(h + 1) * 512] for m in range(NT) for h in range(2)])
            for e, dst in enumerate(dsts):
                act.wait_ge(prj_mm, e + 1)
                act.copy(dst, M[e % 4][:]).then_inc(prj_ev, 1)
            for e in range(NT * HEADS):
                act.wait_ge(idx_mm, e + 1)
                if e >= 2:
                    act.wait_ge(idx_acc, e - 1)
                act.activation(rl[e % 2], M[e % 4][:, 0:T], ACT.Relu).then_inc(idx_relu, 1)

            def attention(first, pairs, dst):
                with act.Fori(0, pairs) as i:
                    n = i * 2 + first
                    for u in range(2):
                        act.wait_ge(a_max, n + (u + 3))
                        for m in range(NT):
                            q = act.activation(att_s[u][:, m, :], att_s[u][:, m, :], ACT.Exp, bias=amax[u][:, m:m + 1],
                                               accum_out=asum[u][:, m:m + 1])
                        q.then_inc(a_exp, 1)
                    for u in range(2):
                        act.wait_ge(a_tr, n + (u + 1))
                        act.copy(flat(att_pT[u]), M[2 + u][:]).then_inc(a_pt, 1)
                    for u in range(2):
                        hold(a_o, n + (u + 1))
                        act.copy(dyn(dst, i * 2 + u), M[4 + u][:, 0:T]).then_inc(a_ev, 1)

            attention(0, HEADS // 2, yB)

            def gate(n):
                act.wait_ge(b_gate, n + 1)
                act.wait_ge(b_sum, n + 1)
                act.activation(sg, G[0][:], ACT.Exp, scale=-1.0).then_inc(b_exp, 1)

            act.sem_inc(b_exp, 1)
            with act.Fori(0, HEADS // 2) as it:
                act.activation(g_sq[:, 0:512], dyn(z, it * 2 + Z_Q, 2), ACT.Square)
                act.activation(g_sq[:, 512:1024], dyn(z, it * 2 + Z_K, 2), ACT.Square).then_inc(d["sq"], 1)
                act.wait_ge(d["ss"], it + 1)
                for i in range(2):
                    q = act.activation(g_rt[:, i * 512:(i + 1) * 512], M[3 * i][:], ACT.Sqrt, bias=eps)
                q.then_inc(d["rt"], 1)
                act.wait_ge(d["vtr"], it + 1)
                act.copy(g_vt, M[2][:])
                act.wait_ge(d["diff"], it + 1)
                act.activation(g_eg, M[3][:], ACT.Exp)
                act.activation(g_dec, g_dec, ACT.Exp).then_inc(d["dec"], 1)
                act.wait_ge(d["prod"], it + 1)
                act.copy(g_kt, M[5][:, 0:2 * P]).then_inc(d["vt"], 1)
                gate(it * 4)
                for l in range(1, LEVELS):
                    act.wait_ge(d["m1"], it * (LEVELS - 1) + l)
                    act.copy(g_ms, M[3][:]).then_inc(d["ms"], 1)
                    if l == 3:
                        gate(it * 4 + 1)
                    if l == 5:
                        gate(it * 4 + 2)
                hold(d["t"], it * LEVELS + LEVELS)
                for u in range(2):
                    for m in range(NT):
                        c = slice((2 * u + m) * P, (2 * u + m + 1) * P)
                        q = act.activation(g_tb[:, c], g_tt[:, c], ACT.Copy,
                                           scale=beta[:, bass.ds(it * 2 + (u + 8 * m), 1)])
                q.then_inc(d["tb"], 1)
                act.wait_ge(d["smm"], it + 1)
                act.copy(g_s, M[2][:, 0:2 * P]).then_inc(d["s"], 1)
                gate(it * 4 + 3)
                act.wait_ge(d["o"], it + 1)
                act.activation(g_osq, M[1][:], ACT.Square).then_inc(d["osq"], 1)
                act.wait_ge(d["oss"], it + 1)
                act.activation(g_ort, M[2][:], ACT.Sqrt, bias=eps, scale=1.0 / P).then_inc(d["ort"], 1)
            with act.Fori(0, 8) as i:
                gate(i + 16)
            act.wait_ge(o_ev, 2 + KC)
            norm(2, xT)
            for s in range(WSLOTS):
                act.wait_ge(xq_mm, s + 1)
                act.copy(xqF[:, s, :], G[s % 2][:, 0:T]).then_inc(xq_ev, 1)
            attention(HEADS, XHEADS // 2, yX)
            act.wait_ge(xo_ev, KC)
            norm(3, xT)
            with act.Fori(0, FF_CH // 2) as i:
                for u in range(2):
                    act.wait_ge(up_conv, i * 4 + (2 * u + 4))
                    act.activation(wide(4 + u, 5 + u), wide(2 * u, 2 * u + 1), ACT.Silu).then_inc(up_silu, 1)
            act.wait_ge(dn_ev, 2 + KC)
            norm(4, xT)

        @block.vector
        def _(dve):
            def norm(n, src, gain):
                dve.wait_ge(n_rt, n + 1)
                dve.reciprocal(rt, rt)
                dve.drain()
                dst = mem_h if n == 0 else hT
                for c in range(KC):
                    dve.scalar_tensor_tensor(out=dst[:, c, :], in0=src[:, c, :], scalar=col(gain, c), in1=rt,
                                             op0=ALU.mult, op1=ALU.mult).then_inc(n_h, 1)

            def conv(dst, src, name, taps, chunks, c, bias=None):
                def w(k):
                    return prm[:, bass.ds(PCOL[name] + k * chunks + c, 1)]
                if bias is None:
                    dve.tensor_scalar(dst, src, w(taps - 1), None, ALU.mult)
                else:
                    dve.tensor_scalar(dst, src, w(taps - 1), bias, ALU.mult, ALU.add)
                for lag in range(1, taps):
                    dve.drain()
                    q = dve.scalar_tensor_tensor(out=dst[:, lag:T], in0=src[:, 0:T - lag], scalar=w(taps - 1 - lag),
                                                 in1=dst[:, lag:T], op0=ALU.mult, op1=ALU.add)
                return q

            dve.sem_inc(b_sum, 1)
            dve.sem_inc(a_max, 2)
            dve.sem_inc(d["y"], 1)
            dve.sem_inc(o_ev, 2)
            dve.sem_inc(dn_ev, 2)
            dve.sem_inc(up_conv, 2)
            dve.wait_ge(const_in, 32)
            norm(0, mem_in, "mem_norm")
            norm(1, xT, "ln_mix")
            with dve.Fori(0, LRU_CH) as c:
                dve.wait_ge(in_ev, c + (Z_AX + 3))
                conv(dyn(xc, c), dyn(z, c + Z_AX), "conv_a_w", 4, LRU_CH, c, bias=col("conv_a_b", c)).then_inc(xconv, 1)
            with dve.Fori(0, (Z_CH - Z_FLAT) // 2) as i:
                for u in range(2):
                    c = i * 2 + u
                    dve.wait_ge(in_ev, c + (Z_FLAT + 3))
                    conv(ctmp[u], dyn(z, c + Z_FLAT), "gdn_conv_w", 4, Z_CH - Z_FLAT, c).then_inc(qconv, 1)
            dve.wait_ge(lat_rt, 2)
            dve.reciprocal(drt, drt)
            dve.drain()
            for c in range(QR + KVR):
                name, cc, r = ("dsa_q_norm", c, drt[:, 0:T]) if c < QR else ("dsa_kv_norm", c - QR, drt[:, T:2 * T])
                q = dve.scalar_tensor_tensor(out=z[:, Z_CQ + c, :], in0=z[:, Z_CQ + c, :], scalar=col(name, cc), in1=r,
                                             op0=ALU.mult, op1=ALU.mult)
            q.then_inc(lat_n, 1)
            dve.wait_ge(tok_mm, 1)
            dve.tensor_copy(tokc, M[1][:, 0:64].rearrange("p (m n) -> p m n", m=NT)).then_inc(tok_ev, 1)
            lam = prm[:, PCOL["lru_lambda"]:PCOL["lru_lambda"] + 8]
            dtb = prm[:, PCOL["gdn_dt_bias"]:PCOL["gdn_dt_bias"] + 8]
            dve.tensor_scalar(sp_x[:, 0:8], lam, -1.0, None, ALU.mult)
            dve.drain()
            for m in range(NT):
                dve.tensor_tensor(sp_x[:, 8 + 8 * m:16 + 8 * m], tokc[:, m, 16:24], dtb, ALU.add)
            dve.tensor_scalar(widx, tokc[:, :, 0:8], float(HEADS ** -0.5 * IDX_DIM ** -0.5), None, ALU.mult)
            dve.drain().then_inc(sp_in, 1)
            dve.wait_ge(sp_ex, 1)
            dve.tensor_scalar(sp_s, sp_e, 2.0, None, ALU.add)
            dve.drain()
            dve.reciprocal(sp_s, sp_s)
            dve.drain()
            dve.tensor_tensor(sp_s, sp_s, sp_e, ALU.mult)
            dve.drain()
            dve.tensor_tensor(sp_z, sp_s, sp_s, ALU.mult)
            dve.drain()
            dve.tensor_scalar(sp_p, sp_z, 1.0 / 17, None, ALU.mult)
            for k in range(15, 1, -2):
                dve.drain()
                dve.scalar_tensor_tensor(out=sp_p, in0=sp_p, scalar=1.0 / k, in1=sp_z, op0=ALU.add, op1=ALU.mult)
            dve.drain()
            dve.scalar_tensor_tensor(out=sp_p, in0=sp_p, scalar=1.0, in1=sp_s, op0=ALU.add, op1=ALU.mult)
            dve.tensor_scalar(sp, sp_x, 0.0, None, ALU.max)
            dve.drain()
            dve.scalar_tensor_tensor(out=sp, in0=sp_p, scalar=2.0, in1=sp, op0=ALU.mult, op1=ALU.add)
            dve.drain()
            dve.tensor_scalar(lam_n, sp[:, 0:8], -LRU_C, None, ALU.mult)
            dve.tensor_scalar(lam_p, sp[:, 0:8], LRU_C, None, ALU.mult)
            for m in range(NT):
                dve.scalar_tensor_tensor(out=gdec[:, 8 * m:8 * m + 8], in0=sp[:, 8 + 8 * m:16 + 8 * m], scalar=-1.0,
                                         in1=ea, op0=ALU.mult, op1=ALU.mult)
            dve.drain().then_inc(sp_done, 1)
            dve.wait_ge(gcum_mm, 1)
            dve.tensor_copy(gcum, M[2][:, 0:16]).then_inc(gcum_ev, 1)
            dve.wait_ge(lru_at, LRU_CH)
            dve.tensor_scalar(flat(lr), flat(lt), 1.0, None, ALU.add)
            dve.drain()
            dve.reciprocal(flat(lr), flat(lr))
            dve.drain()
            dve.tensor_tensor(flat(lt), flat(lt), flat(lr), ALU.mult).then_inc(lru_m2, 1)
            dve.tensor_tensor(flat(li), flat(li), flat(xc), ALU.mult)
            dve.wait_ge(lru_root, 1)
            dve.memset(lr[:, :, 0:1], 1.0)
            dve.drain()
            dve.tensor_tensor(flat(li), flat(li), flat(lr), ALU.mult)
            dve.drain()
            for c in range(LRU_CH):
                dve.tensor_tensor_scan(lt[:, c, :], la[:, c, :], li[:, c, :], 0.0, ALU.mult, ALU.add)
            dve.drain()
            dve.wait_ge(gates_act, 2)
            dve.tensor_tensor(flat(yA), flat(yA), flat(lt), ALU.mult).then_inc(lru_done, 1)
            for m in range(NT):
                for h in range(HEADS):
                    e = m * HEADS + h
                    dve.drain()
                    dve.wait_ge(idx_relu, e + 1)
                    dve.scalar_tensor_tensor(out=score[:, m, :], in0=rl[e % 2], scalar=widx[:, m, h:h + 1],
                                             in1=negmask[:, m, :] if h == 0 else score[:, m, :],
                                             op0=ALU.mult, op1=ALU.add).then_inc(idx_acc, 1)
            with dve.Fori(0, TOPK // 8) as _:
                dve.drain()
                for m in range(NT):
                    dve.max(top8[:, m, :], score[:, m, :])
                dve.drain()
                for m in range(NT):
                    dve.match_replace(score[:, m, :], top8[:, m, :], score[:, m, :], TAKEN)
            dve.drain()
            dve.tensor_scalar(flat(sbias), flat(score), TAKEN, 1.0, ALU.is_equal, ALU.subtract)
            dve.drain()
            dve.scalar_tensor_tensor(out=flat(sbias), in0=flat(sbias), scalar=-NEG, in1=flat(negmask),
                                     op0=ALU.mult, op1=ALU.add)
            dve.drain()

            def attention(first, pairs, bias):
                scale = float(P ** -0.5)
                with dve.Fori(0, pairs) as i:
                    n = i * 2 + first
                    for u in range(2):
                        dve.wait_ge(a_mm, n + (u + 1))
                        if bias is None:
                            dve.tensor_scalar(flat(att_s[u]), M[u][:], scale, None, ALU.mult)
                        else:
                            dve.scalar_tensor_tensor(out=flat(att_s[u]), in0=M[u][:], scalar=scale, in1=flat(bias),
                                                     op0=ALU.mult, op1=ALU.add)
                        dve.drain()
                        dve.tensor_reduce(amax[u], att_s[u], AX.X, ALU.max)
                        dve.drain()
                        dve.tensor_scalar(amax[u], amax[u], -1.0, None, ALU.mult).then_inc(a_max, 1)
                    for u in range(2):
                        dve.wait_ge(a_exp, n + (u + 1))
                        dve.reciprocal(asum[u], asum[u])
                        dve.drain()
                        for m in range(NT):
                            q = dve.tensor_scalar(att_s[u][:, m, :], att_s[u][:, m, :], asum[u][:, m:m + 1], None, ALU.mult)
                        q.then_inc(a_p, 1)

            attention(0, HEADS // 2, sbias)

            def merge(n, c, first):
                dve.wait_ge(b_exp, n + 2)
                dve.tensor_scalar(sg, sg, 1.0, None, ALU.add)
                dve.drain()
                dve.reciprocal(sg, sg)
                dve.drain()
                dve.wait_ge(b_proj, n + 1)
                if first:
                    dve.tensor_tensor(dyn(merged, c, 2), G[1][:], sg, ALU.mult)
                else:
                    dve.tensor_tensor(gt, G[1][:], sg, ALU.mult)
                    dve.drain()
                    dve.tensor_tensor(dyn(merged, c, 2), dyn(merged, c, 2), gt, ALU.add)
                dve.drain().then_inc(b_sum, 1)

            def heads(ap):
                return ap.rearrange("p (q n) -> p q n", q=4)

            def over(ap):
                return ap.unsqueeze(1).broadcast_to([P, 4, P])

            with dve.Fori(0, HEADS // 2) as it:
                dve.wait_ge(d["rt"], it + 1)
                for u in range(2):
                    for m in range(NT):
                        c = slice((2 * u + m) * P, (2 * u + m + 1) * P)
                        at = it * 2 + (u + 8 * m)
                        dve.tensor_scalar(g_ug[:, c], tri, gdec[:, bass.ds(at, 1)], None, ALU.mult)
                        q = dve.tensor_scalar(g_db[:, c], ident, beta[:, bass.ds(at, 1)], None, ALU.mult)
                q.then_inc(d["rank1"], 1)
                dve.reciprocal(g_rt, g_rt)
                dve.drain()
                dve.scalar_tensor_tensor(out=g_q2, in0=dyn(z, it * 2 + Z_Q, 2), scalar=float(P ** -0.5),
                                         in1=g_rt[:, 0:512], op0=ALU.mult, op1=ALU.mult)
                dve.tensor_tensor(g_k2, dyn(z, it * 2 + Z_K, 2), g_rt[:, 512:1024], ALU.mult).then_inc(d["qk"], 1)
                dve.drain()
                dve.wait_ge(d["bc"], it + 1)
                for u in range(2):
                    for m in range(NT):
                        c = slice((2 * u + m) * P, (2 * u + m + 1) * P)
                        q = dve.tensor_scalar(g_dec[:, c], M[3][:, c], gcum[:, bass.ds(it * 2 + (u + 8 * m), 1)], 0.0,
                                              ALU.subtract, ALU.min)
                q.then_inc(d["diff"], 1)
                dve.wait_ge(d["dec"], it + 1)
                dve.tensor_tensor(heads(g_dec), heads(g_dec), over(tri), ALU.mult)
                dve.drain()
                dve.wait_ge(d["prod"], it + 1)
                dve.tensor_tensor(g_bd, g_dec, M[4][:], ALU.mult)
                dve.drain()
                dve.tensor_tensor(g_at, g_bd, M[0][:], ALU.mult).then_inc(d["at"], 1)
                dve.tensor_tensor(g_qk, g_dec, M[1][:], ALU.mult)
                dve.tensor_tensor(g_kw, g_k2, g_eg, ALU.mult)
                dve.tensor_tensor(g_qd, g_q2, g_eg, ALU.mult)
                dve.wait_ge(d["vt"], it + 1)
                for u in range(2):
                    last = (2 * u + 1) * P - 1
                    q = dve.tensor_scalar(g_ktail[:, u * P:(u + 1) * P], g_kt[:, u * P:(u + 1) * P],
                                          g_dec[:, last:last + 1], None, ALU.mult)
                q.then_inc(d["kt"], 1)
                dve.wait_ge(d["etr"], it + 1)
                dve.tensor_tensor(heads(g_t), over(ident), heads(M[2][:]), ALU.subtract)
                dve.tensor_tensor(heads(g_tt), over(ident), heads(g_e[0]), ALU.subtract).then_inc(d["t"], 1)
                merge(it * 4, it * 4, True)
                for l in range(1, LEVELS):
                    dve.drain()
                    dve.wait_ge(d["x"], it * (LEVELS - 1) + l)
                    if l < LEVELS - 1:
                        dve.tensor_tensor(g_t, g_t, M[4][:], ALU.subtract)
                    dve.tensor_tensor(g_tt, g_tt, M[5][:], ALU.subtract).then_inc(d["t"], 1)
                    if l == 3:
                        merge(it * 4 + 1, it * 4 + 2, True)
                dve.wait_ge(d["v0mm"], it + 1)
                dve.tensor_copy(g_v0, M[0][:, 0:2 * P]).then_inc(d["v0"], 1)
                merge(it * 4 + 2, it * 4, False)
                dve.wait_ge(d["ksmm"], it + 1)
                for u in range(2):
                    q = dve.tensor_tensor(g_r[:, u * P:(u + 1) * P], g_vt[:, (2 * u + 1) * P:(2 * u + 2) * P],
                                          M[3][:, u * P:(u + 1) * P], ALU.subtract)
                q.then_inc(d["r"], 1)
                dve.wait_ge(d["v1mm"], it + 1)
                dve.tensor_copy(g_v1, M[4][:, 0:2 * P]).then_inc(d["v1"], 1)
                merge(it * 4 + 3, it * 4 + 2, False)
                dve.wait_ge(d["ort"], it + 1)
                dve.reciprocal(g_ort, g_ort)
                dve.drain()
                dve.scalar_tensor_tensor(out=g_ort, in0=M[1][:], scalar=col("gdn_o_norm", 0), in1=g_ort,
                                         op0=ALU.mult, op1=ALU.mult)
                dve.drain()
                dve.tensor_tensor(dyn(yC, it * 2, 2), dyn(yC, it * 2, 2), g_ort, ALU.mult).then_inc(d["y"], 1)
            with dve.Fori(0, 8) as i:
                merge(i + 16, i * 2, False)
            with dve.Fori(0, KC // 2) as i:
                for u in range(2):
                    dve.wait_ge(o_mm, i * 2 + (u + 1))
                    c = i * 2 + u
                    dve.tensor_tensor(dyn(xT, c), dyn(xT, c), G[u][:, 0:T], ALU.add).then_inc(o_ev, 1)
            norm(2, xT, "ln_mem")
            attention(HEADS, XHEADS // 2, None)
            for c in range(KC):
                dve.wait_ge(xo_mm, c + 1)
                dve.tensor_tensor(xT[:, c, :], xT[:, c, :], G[c % 2][:, 0:T], ALU.add).then_inc(xo_ev, 1)
            norm(3, xT, "ln_ffn")
            with dve.Fori(0, FF_CH // 2) as i:
                for u in range(2):
                    tg, tu = wide(2 * u, 2 * u + 1), wide(2 * u + 1, 2 * u + 2)
                    c = i * 2 + u
                    dve.wait_ge(up_mm, i * 4 + (2 * u + 1))
                    conv(tg, G[0][:, 0:T], "ffn_conv_w", 3, 2 * FF_CH, c).then_inc(up_conv, 1)
                    dve.wait_ge(up_mm, i * 4 + (2 * u + 2))
                    conv(tu, G[1][:, 0:T], "ffn_conv_w", 3, 2 * FF_CH, c + FF_CH).then_inc(up_conv, 1)
                    dve.drain()
                    dve.wait_ge(up_silu, c + 1)
                    dve.tensor_tensor(dyn(ff, c), wide(4 + u, 5 + u), tu, ALU.mult).then_inc(up_h, 1)
            with dve.Fori(0, KC // 2) as i:
                for u in range(2):
                    c = i * 2 + u
                    dve.wait_ge(dn_mm, c + 1)
                    dve.tensor_tensor(dyn(xT, c), dyn(xT, c), G[u][:, 0:T], ALU.add).then_inc(dn_ev, 1)
            norm(4, xT, "ln_f")

        @block.gpsimd
        def _(pool):
            def attention(first, pairs, queries, values):
                with pool.Fori(0, pairs) as i:
                    n = i * 2 + first
                    for u in range(2):
                        pool.wait_ge(a_ev, n + 1)
                        pool.tensor_copy(att_q[u], dyn(queries, i * 2 + u))
                        pool.tensor_copy(att_v[u], values[:, :, bass.ds((i * 2 + u) * P, P)])
                        pool.drain().then_inc(a_stage, 1)

            pool.wait_ge(prj_ev, 14)
            attention(0, HEADS // 2, qF, vT)
            pool.wait_ge(a_ev, 1 + HEADS)
            with pool.Fori(0, HEADS // 2) as it:
                pool.wait_ge(d["y"], it + 1)
                pool.tensor_copy(g_v2, dyn(z, it * 2 + Z_V, 2)).then_inc(d["v2"], 1)
                pool.wait_ge(d["at"], it + 1)
                for l in range(LEVELS):
                    if l >= EBUF:
                        if l == EBUF:
                            pool.wait_ge(d["t"], it * LEVELS + 1)
                        else:
                            pool.wait_ge(d["m1"], it * (LEVELS - 1) + l - EBUF)
                    pool.tensor_tensor(g_e[l % EBUF].rearrange("p (q n) -> p q n", q=4),
                                       g_at.rearrange("p (q n) -> p q n", q=4),
                                       level_mask(l).unsqueeze(1).broadcast_to([P, 4, P]), ALU.mult).then_inc(d["e"], 1)
            pool.wait_ge(xq_ev, 4)
            attention(HEADS, XHEADS // 2, xqF, mem_v)


def _chunks(w):
    k, m = w.shape
    return np.ascontiguousarray(w.reshape(k // P, P, m // P, P).transpose(2, 1, 0, 3).reshape(m // P, P, k))


def _group(jobs, n):
    j, p, c = jobs.shape
    return np.ascontiguousarray(jobs.reshape(j // n, n, p, c).transpose(0, 2, 1, 3).reshape(j // n, p, n * c))


def _cols(v):
    return np.asarray(v).reshape(-1, P).T


def _feature_major(x):
    t, dd = x.shape
    return np.ascontiguousarray(x.T.reshape(dd // P, P, t).transpose(1, 0, 2))


def _constants():
    c = np.zeros((P, C_N), np.float32)
    i = np.arange(P)
    c[:, C_ID:C_ID + P] = np.eye(P)
    c[:, C_ONE:C_ONE + P] = 1.0
    c[:, C_TRI:C_TRI + P] = i[:, None] <= i[None, :]
    for l in range(LEVELS):
        b = 1 << l
        row, colm = i[None, :], i[:, None]
        c[:, C_MASK + l * P:C_MASK + (l + 1) * P] = (
            (row // (2 * b) == colm // (2 * b)) & (row // b % 2 == 1) & (colm // b % 2 == 0))
    for m in range(NT):
        c[:, C_NEG + m * T:C_NEG + (m + 1) * T] = np.where(np.arange(T)[None, :] > m * P + i[:, None], NEG, 0.0)
    c[:, C_EPS] = EPS
    return c


def kernel(**inp):
    import concourse.bacc as bacc
    from concourse.bass_utils import run_bass_kernel_spmd

    a = {k: np.asarray(v) for k, v in inp.items()}
    one = {k: v[0] for k, v in a.items() if k not in ("ln_f",)}
    w_in = one["w_in"]
    o = np.cumsum([0, 1024, 1024, 512, 256, 64, 8, 1024, 1024, 1024, 8, 8, 1024, 6144])
    part = [w_in[:, o[i]:o[i + 1]] for i in range(13)]
    a_x, a_gate, c_q, c_kv, k_idx, w_idx, g_q, g_k, g_v, g_b, g_a, g_z, gates = part
    pad = np.zeros((D, P - 24), np.float32)
    host = {
        "x_wk": _chunks(one["x_wkv"][:, 0:512]),
        "x_wv": np.ascontiguousarray(one["x_wkv"][:, 512:].reshape(4, 4, P, 512).transpose(0, 2, 1, 3).reshape(4, P, D)),
        "w_in": _chunks(np.concatenate([g_z, a_gate, a_x, c_q, c_kv, k_idx, k_idx, w_idx, g_b, g_a, pad, g_q, g_k, g_v], 1)),
        "w_gate": _chunks(gates),
        "lru_wa": np.ascontiguousarray(one["lru_wa"].transpose(1, 0, 2).reshape(P, LRU_CH * P)),
        "lru_wx": np.ascontiguousarray(one["lru_wx"].transpose(1, 0, 2).reshape(P, LRU_CH * P)),
        "w_uqi": _group(_chunks(one["dsa_w_uqi"].reshape(QR * P, -1)), 4)[0],
        "w_uk": _group(_chunks(one["dsa_w_uk"].reshape(KVR * P, -1)), 8)[0],
        "w_uq": _group(_chunks(one["dsa_w_uq"].reshape(QR * P, -1)), 4),
        "w_uv": np.ascontiguousarray(one["dsa_w_uv"].reshape(KVR, P, HEADS * P)),
        "p_a": _group(_chunks(one["p_a"]), 2),
        "p_b": _group(_chunks(one["p_b"]), 2),
        "p_c": _group(_chunks(one["p_c"]), 2),
        "w_o": _chunks(one["w_o"]),
        "x_wq": _chunks(one["x_wq"]),
        "x_wo": _group(_chunks(one["x_wo"]), 4),
        "w_up": _chunks(one["ffn_w_up"]),
        "w_down": _chunks(one["ffn_w_down"]),
        "x": _feature_major(one["x"]),
        "mem": _feature_major(one["mem"]),
        "consts": _constants(),
    }
    one["ln_f"] = a["ln_f"]
    cols = []
    for name, width in PARAMS:
        v = one[name]
        cols.append(np.broadcast_to(v, (P, 8)) if name in ("gdn_a_log", "gdn_dt_bias") else _cols(v))
        assert cols[-1].shape[1] == width
    host["prm"] = np.ascontiguousarray(np.concatenate(cols, 1))

    nc = bacc.Bacc("TRN2", target_bir_lowering=False, num_devices=1)
    dr = {k: nc.dram_tensor("in_" + k, v.shape, F32, kind="ExternalInput").ap() for k, v in host.items()}
    out = nc.dram_tensor("out_0", (P, KC, T), F32, kind="ExternalOutput").ap()
    build(nc, dr, out)
    r = run_bass_kernel_spmd(nc, [{"in_" + k: v for k, v in host.items()}], core_ids=[0])
    y = r.results[0]["out_0"]
    return np.ascontiguousarray(y.transpose(2, 1, 0).reshape(1, T, D))
```

```python
from contextlib import ExitStack

import numpy as np

import concourse.bass as bass
from concourse import mybir

F32 = mybir.dt.float32
F32R = mybir.dt.float32r
ALU = mybir.AluOpType
ACT = mybir.ActivationFunctionType
AX = mybir.AxisListType

P = 128
T = 256
NT = T // P
D = 2048
KC = D // P
N_MEM = 256
EPS = 1e-6
LRU_CH = 8
LRU_C = 8.0
QR, KVR = 4, 2
HEADS = 8
IDX_DIM = 64
TOPK = min(256, T // 4)
XHEADS = 4
FF_CH = 44
DOWN_BLOCKS = 11
PIECE = 8
LEVELS = 7
WSLOTS = 4
NEG = -1.0e30
TAKEN = -float(2.0 ** 127)

Z_GZ, Z_AGATE, Z_AX, Z_CQ, Z_CKV, Z_KIDX, Z_SMALL, Z_Q, Z_K, Z_V = 0, 8, 16, 24, 28, 30, 31, 32, 40, 48
Z_CH = 56
Z_FLAT = 32

C_ONE, C_EPS, C_N = 0, 128, 136
C_ID, C_TRI, C_MASK = 0, 128, 256
C_MN = C_MASK + LEVELS * P

PARAMS = [("ln_mix", 16), ("mem_norm", 16), ("ln_mem", 16), ("ln_ffn", 16), ("ln_f", 16),
          ("conv_a_w", 4 * 8), ("conv_a_b", 8), ("lru_ba", 8), ("lru_bx", 8), ("lru_lambda", 8),
          ("dsa_q_norm", 4), ("dsa_kv_norm", 2), ("gdn_conv_w", 4 * 24), ("gdn_o_norm", 1),
          ("ffn_conv_w", 3 * 88), ("gdn_a_log", 8), ("gdn_dt_bias", 8)]
PCOL, _at = {}, 0
for _n, _w in PARAMS:
    PCOL[_n] = _at
    _at += _w
P_N = _at

R_IN = 0
R_DSA = R_IN + Z_CH // WSLOTS
R_AB = R_DSA + 8 // WSLOTS
R_C = R_AB + 48 // WSLOTS
R_WO = R_C + 24 // WSLOTS
R_MEM = R_WO + KC // WSLOTS
R_X = R_MEM + 8 // WSLOTS
R_UP = R_X + 8 // WSLOTS
R_DOWN = R_UP + 2 * FF_CH // WSLOTS
R_END = R_DOWN + 4 * KC // WSLOTS

G_IN = 0
G_AB = G_IN + Z_CH
G_C = G_AB + 32
G_WO = G_C + 16
G_MEM = G_WO + KC
G_XQ = G_MEM + 8
G_UP = G_XQ + 4
G_DOWN = G_UP + 2 * FF_CH


def build(nc, dr, out):
    ctx = ExitStack()
    with ctx:
        def sb(name, shape):
            return ctx.enter_context(nc.sbuf_tensor(name, shape, F32))

        def sem(name):
            return ctx.enter_context(nc.semaphore(name))

        consts = sb("consts", [P, C_N])
        prm = sb("prm", [P, P_N])
        tiny = sb("tiny", [P, 328])
        xT = sb("xT", [P, KC, T])
        wring = [sb(f"wring{s}", [P, D]) for s in range(WSLOTS)]

        def sbr(name, shape, stack=None):
            return (stack or ctx).enter_context(nc.sbuf_tensor(name, shape, F32R))

        w_hi = [sbr(f"w_hi{i}", [P, PIECE * P]) for i in range(4)]
        w_lo = [sbr(f"w_lo{i}", [P, PIECE * P]) for i in range(4)]
        h_hi, h_lo = sbr("h_hi", [P, KC, T]), sbr("h_lo", [P, KC, T])
        with ExitStack() as mixers:
            z = mixers.enter_context(nc.sbuf_tensor("z", [P, Z_CH, T], F32))
            V = mixers.enter_context(nc.sbuf_tensor("V", [P, 31, T], F32))
            masks = mixers.enter_context(nc.sbuf_tensor("masks", [P, C_MN], F32))
        with ExitStack() as memory:
            m_hi = sbr("m_hi", [P, KC, T], memory)
            memory.enter_context(nc.sbuf_tensor("beside_memory", [P, 32, T], F32))
            m_lo = sbr("m_lo", [P, KC, T], memory)
        with ExitStack() as mlp:
            ff_hi, ff_lo = sbr("ff_hi", [P, FF_CH, T], mlp), sbr("ff_lo", [P, FF_CH, T], mlp)
            ff_t = mlp.enter_context(nc.sbuf_tensor("ff_t", [P, 3, T], F32))
        G = [ctx.enter_context(nc.psum_tensor(f"G{i}", [P, 512], F32)) for i in range(2)]
        M = [ctx.enter_context(nc.psum_tensor(f"M{i}", [P, 512], F32)) for i in range(6)]
        X = xT

        ident = masks[:, C_ID:C_ID + P]
        ones = consts[:, C_ONE:C_ONE + P]
        tri = masks[:, C_TRI:C_TRI + P]
        eps = consts[:, C_EPS:C_EPS + 1]

        def level_mask(l):
            return masks[:, C_MASK + l * P:C_MASK + (l + 1) * P]

        def col(name, c):
            return prm[:, bass.ds(PCOL[name] + c, 1)]

        def flat(ap):
            return ap.rearrange("p c t -> p (c t)")

        def xs(lo, hi):
            return flat(X[:, lo:hi, :])

        def vs(lo, hi):
            return flat(V[:, lo:hi, :])

        def tiles(ap):
            return ap.rearrange("p (m n) -> p m n", m=NT)

        hf = z[:, 16:32, :]
        rt = vs(9, 10)
        ctmp = [vs(29, 30), vs(30, 31)]
        negmask = V[:, 27:29, :]
        xc, lr, li, la, lt = X[:, 0:8, :], X[:, 8:16, :], V[:, 0:8, :], V[:, 8:16, :], z[:, 16:24, :]
        dsq, drt = V[:, 16:22, :], vs(22, 24)
        qF, kF, qiF = z[:, 16:24, :], X[:, 0:8, :], V[:, 0:4, :]
        vT = tiles(xs(8, 16))
        score = V[:, 4:6, :]
        rl = [vs(6, 7), vs(7, 8)]
        sbias = V[:, 8:10, :]
        att_s = [V[:, 10:12, :], V[:, 12:14, :]]
        att_pT = [V[:, 14:16, :], V[:, 16:18, :]]
        att_q = [vs(18, 19), vs(19, 20)]
        att_v = [tiles(vs(20, 21)), tiles(vs(21, 22))]
        yB = V[:, 22:30, :]
        yA = z[:, Z_AGATE:Z_AGATE + 8, :]
        yC = z[:, Z_GZ:Z_GZ + 8, :]
        merged = z[:, 16:32, :]
        mem_in = z[:, 32:48, :]
        xqF, mem_k = z[:, 40:44, :], z[:, 32:36, :]
        mem_v = tiles(flat(z[:, 36:40, :]))
        yX = V[:, 22:26, :]

        g_sq, g_rt = xs(0, 4), xs(4, 8)
        g_ug, g_db = xs(0, 2), xs(2, 4)
        g_bd, g_at = xs(0, 2), xs(2, 4)
        g_dec, g_qk = xs(4, 6), xs(6, 8)
        g_q2, g_k2, g_v2, g_eg = xs(8, 10), xs(10, 12), xs(12, 14), xs(14, 16)
        g_t = g_v2
        g_vt, g_kt, g_ktail, g_kw, g_qd = vs(0, 2), vs(2, 3), vs(3, 4), vs(4, 6), vs(6, 8)
        g_v0 = g_kt
        EBUF = 3
        g_e = [vs(8, 10), vs(10, 12), vs(12, 14)]
        g_osq, g_ort = g_e[0], g_e[1]
        g_tt, g_ms = vs(14, 16), vs(16, 18)
        g_tb = g_ms
        g_s, g_r, g_v1 = vs(18, 19), vs(19, 20), vs(30, 31)
        sg = vs(20, 22)

        _t = [0]

        def small(n):
            _t[0] += n
            return tiny[:, _t[0] - n:_t[0]]

        tokc = tiles(small(64))
        widx = tiles(small(16))
        beta = small(16)
        gdec = small(16)
        gcum = small(16)
        sp_x, sp_e, sp_s, sp_z, sp_p = (small(24) for _ in range(5))
        sp = small(24)
        ea = small(8)
        lam_n, lam_p = small(8), small(8)
        top8 = tiles(small(16))
        amax = [small(2), small(2)]
        asum = [small(2), small(2)]

        w_landed = [sem(f"w_landed{s}") for s in range(WSLOTS)]
        w_used = [sem(f"w_used{s}") for s in range(WSLOTS)]
        hi_done = sem("hi_done")
        lo_first = sem("lo_first")
        piece_used = sem("piece_used")
        const_in, x_in = sem("const_in"), [sem(f"x_in{q}") for q in range(4)]
        x_back, mem_loaded = sem("x_back"), sem("mem_loaded")
        n_sq, n_ss, n_rt, n_f, n_hi, n_h = ({k: sem(f"{w}_{k}") for k in ("mix", "mem", "xat", "ffn", "out")}
                                            for w in ("sq", "ss", "rt", "hf", "hh", "h"))
        mg_hi, mg_h = sem("mg_hi"), sem("mg_h")
        memk_ev, memv_ev = sem("memk_ev"), sem("memv_ev")
        in_ev = sem("in_ev")
        xconv, qconv, qsilu = sem("xconv"), sem("qconv"), sem("qsilu")
        lat_sq, lat_ss, lat_rt, lat_n = sem("lat_sq"), sem("lat_ss"), sem("lat_rt"), sem("lat_n")
        tok_mm, tok_ev, sp_in, sp_ex, sp_done, beta_done = (sem(n) for n in
            ("tok_mm", "tok_ev", "sp_in", "sp_ex", "sp_done", "beta_done"))
        gcum_mm, gcum_ev = sem("gcum_mm"), sem("gcum_ev")
        lru_mm, lru_sig, lru_at, lru_m2, lru_root, gates_act, lru_done = (sem(n) for n in
            ("lru_mm", "lru_sig", "lru_at", "lru_m2", "lru_root", "gates_act", "lru_done"))
        prj_mm, prj_ev = sem("prj_mm"), sem("prj_ev")
        idx_mm, idx_relu, idx_acc, sel_done = sem("idx_mm"), sem("idx_relu"), sem("idx_acc"), sem("sel_done")
        a_stage, a_mm, a_max, a_exp, a_p, a_tr, a_pt, a_o, a_ev = (sem(n) for n in
            ("a_stage", "a_mm", "a_max", "a_exp", "a_p", "a_tr", "a_pt", "a_o", "a_ev"))
        d = {n: sem("d_" + n) for n in (
            "sq", "ss", "rt", "v2", "rank1", "qk", "bc", "vtr", "prod", "diff", "dec", "vt", "at", "kt",
            "e", "etr", "t", "m1", "ms", "x", "tb", "v0mm", "v0", "smm", "s", "ksmm", "r", "v1mm", "v1",
            "o", "osq", "oss", "ort", "y")}
        b_exp, b_sum = sem("b_exp"), sem("b_sum")
        o_ev = sem("o_ev")
        xq_ev, xo_mm, xo_ev = sem("xq_ev"), sem("xo_mm"), sem("xo_ev")
        up_conv, up_silu, up_f, up_hi, up_h = sem("up_conv"), sem("up_silu"), sem("up_f"), sem("up_hi"), sem("up_h")
        dn_ev = sem("dn_ev")
        act_turns, stored = sem("act_turns"), sem("stored")

        block = ctx.enter_context(nc.Block())

        def dyn(ap, i, n=1):
            return ap[:, bass.ds(i, n), :].rearrange("p c t -> p (c t)")

        @block.sync
        def _(sp_eng):
            def load(s, r, src, cols):
                sp_eng.wait_ge(w_used[s], r)
                sp_eng.dma_start(wring[s][:, 0:cols], src).then_inc(w_landed[s], 16)

            def job(name, i):
                return dr[name][bass.ds(i, 1)].rearrange("a p c -> p (a c)")

            for s in range(WSLOTS):
                sp_eng.dma_start(wring[s][:], job("w_in", s)).then_inc(w_landed[s], 16)
            with sp_eng.Fori(1, Z_CH // WSLOTS) as r:
                for s in range(WSLOTS):
                    load(s, R_IN + r, job("w_in", r * WSLOTS + s), D)
            load(0, R_DSA, dr["lru_wa"], LRU_CH * P)
            load(1, R_DSA, dr["lru_wx"], LRU_CH * P)
            load(2, R_DSA, dr["w_uqi"], 16 * P)
            load(3, R_DSA, dr["w_uk"], 16 * P)
            load(0, R_DSA + 1, job("w_uq", 0), D)
            load(1, R_DSA + 1, job("w_uq", 1), D)
            load(2, R_DSA + 1, job("w_uv", 0), 8 * P)
            load(3, R_DSA + 1, job("w_uv", 1), 8 * P)
            with sp_eng.Fori(0, 4) as it:
                for j in range(4):
                    br, pair = j // 2, it * 2 + j % 2
                    for i in range(3):
                        n = 3 * j + i
                        src = job("w_gate", br * KC + pair * 2 + i) if i < 2 else job("p_ab"[0:2] + "ab"[br], pair)
                        load(n % WSLOTS, R_AB + it * 3 + n // WSLOTS, src, D)
            with sp_eng.Fori(0, 2) as it:
                for j in range(4):
                    pair = it * 4 + j
                    for i in range(3):
                        n = 3 * j + i
                        src = job("w_gate", 2 * KC + pair * 2 + i) if i < 2 else job("p_c", pair)
                        load(n % WSLOTS, R_C + it * 3 + n // WSLOTS, src, D)
            with sp_eng.Fori(0, KC // WSLOTS) as r:
                for s in range(WSLOTS):
                    load(s, R_WO + r, job("w_o", r * WSLOTS + s), D)
            for s in range(WSLOTS):
                load(s, R_MEM, job("x_wk", s), D)
            for s in range(WSLOTS):
                load(s, R_MEM + 1, job("x_wv", s), D)
            for s in range(WSLOTS):
                load(s, R_X, job("x_wq", s), D)
            for s in range(WSLOTS):
                load(s, R_X + 1, job("x_wo", s), D)
            with sp_eng.Fori(0, 2 * FF_CH // WSLOTS) as r:
                for s in range(WSLOTS):
                    load(s, R_UP + r, job("w_up", (s % 2) * FF_CH + r * 2 + s // 2), D)
            with sp_eng.Fori(0, KC) as r:
                src = dr["w_down"][bass.ds(r, 1)].rearrange("a p c -> p (a c)")
                n = DOWN_BLOCKS * P
                for s in range(WSLOTS):
                    load(s, R_DOWN + r, src[:, s * n:(s + 1) * n], n)
            for q in range(4):
                sp_eng.wait_ge(n_f["out"], 4 * q + 4)
                sp_eng.dma_start(out[:, 4 * q:4 * q + 4, :], hf[:, 4 * q:4 * q + 4, :]).then_inc(stored, 16)
            sp_eng.wait_ge(stored, 64)

        @block.tensor
        def _(pe):
            def landed(s, r):
                pe.wait_ge(w_landed[s], (r + 1) * 16)

            def norm_sums(k):
                for c in range(KC):
                    if c % 4 == 0:
                        pe.wait_ge(n_sq[k], c // 4 + 1)
                    q = pe.matmul(M[0][:, 0:T], ones, hf[:, c, :], start=c == 0, stop=c == KC - 1)
                q.then_inc(n_ss[k], 1)

            def chunk(dst, s, first, count, rhs):
                for k in range(count):
                    q = pe.matmul(dst, wring[s][:, (first + k) * P:(first + k + 1) * P], rhs(k),
                                  start=k == 0, stop=k == count - 1)
                return q

            def piece_ready(q, s, g, r):
                if q == 0:
                    pe.wait_ge(lo_first, g + 1)
                else:
                    pe.wait_ge(w_used[s], r + 1)

            def piece(dst, b, q, s, g, r, blocks, hi, lo, k0=0, kn=KC, ready=None):
                piece_ready(q, s, g, r)
                wh, wl = w_hi[2 * b + q], w_lo[2 * b + q]
                for k in range(blocks):
                    if ready is not None:
                        pe.wait_ge(ready, k0 + k + 1)
                    c = slice(k * P, (k + 1) * P)
                    pe.matmul(dst, wh[:, c], hi[:, k0 + k, :], start=k0 + k == 0, stop=False)
                    pe.matmul(dst, wh[:, c], lo[:, k0 + k, :], start=False, stop=False)
                    e = pe.matmul(dst, wl[:, c], hi[:, k0 + k, :], start=False, stop=k0 + k == kn - 1)
                e.then_inc(piece_used, 1)

            def split_chunk(dst, s, g, r, hi, lo, ready=None):
                for q in range(2):
                    piece(dst, s % 2, q, s, g, r, PIECE, hi, lo, k0=q * PIECE, ready=ready)

            pe.wait_ge(const_in, 32)
            norm_sums("mix")
            with pe.Fori(0, Z_CH // WSLOTS) as r:
                for s in range(WSLOTS):
                    pe.wait_ge(in_ev, r * WSLOTS + s + 1)
                    split_chunk(G[s % 2][:, 0:T], s, G_IN + r * WSLOTS + s, R_IN + r, h_hi, h_lo,
                                n_h["mix"] if s == 0 else None)
            pe.wait_ge(lat_sq, 1)
            for c in range(QR):
                pe.matmul(M[0][:, 0:T], ones, dsq[:, c, :], start=c == 0, stop=c == QR - 1)
            for c in range(KVR):
                q = pe.matmul(M[0][:, T:2 * T], ones, dsq[:, QR + c, :], start=c == 0, stop=c == KVR - 1)
            q.then_inc(lat_ss, 1)
            for m in range(NT):
                q = pe.transpose(M[1][:, m * 32:(m + 1) * 32], z[0:32, Z_SMALL, m * P:(m + 1) * P], ident[0:32, 0:32])
            q.then_inc(tok_mm, 1)
            pe.wait_ge(sp_done, 1)
            for m in range(NT):
                q = pe.matmul(M[2][:, m * 8:(m + 1) * 8], tri, gdec[:, m * 8:(m + 1) * 8], start=True, stop=True)
            q.then_inc(gcum_mm, 1)
            pe.wait_ge(xconv, LRU_CH)
            for j in range(2 * LRU_CH):
                s, c = j // LRU_CH, j % LRU_CH
                if c == 0:
                    landed(s, R_DSA)
                bank = M[3 + j % 3]
                if j >= 3:
                    pe.wait_ge(lru_sig, j - 2)
                q = pe.matmul(bank[:, 0:T], wring[s][:, c * P:(c + 1) * P], xc[:, c, :], start=True, stop=True)
                q.then_inc(lru_mm, 1)
                if c == LRU_CH - 1:
                    pe.drain().then_inc(w_used[s], 1)
            pe.wait_ge(lat_n, 1)
            pe.wait_ge(lru_sig, 2 * LRU_CH)
            pe.wait_ge(gcum_ev, 1)
            e = 0

            def proj_bank():
                if e >= 4:
                    pe.wait_ge(prj_ev, e - 3)
                return M[e % 4]

            for s, r, chunks, kn, rhs in ((2, R_DSA, 4, QR, Z_CQ), (3, R_DSA, 8, KVR, Z_CKV),
                                          (0, R_DSA + 1, 4, QR, Z_CQ), (1, R_DSA + 1, 4, QR, Z_CQ)):
                landed(s, r)
                for c in range(chunks):
                    if c % 2 == 0:
                        bank = proj_bank()
                    q = chunk(bank[:, (c % 2) * T:(c % 2 + 1) * T], s, c * kn, kn, lambda k: z[:, rhs + k, :])
                    if c % 2:
                        q.then_inc(prj_mm, 1)
                        e += 1
                pe.drain().then_inc(w_used[s], 1)
            landed(2, R_DSA + 1)
            landed(3, R_DSA + 1)
            for m in range(NT):
                for half in range(2):
                    bank = proj_bank()
                    for k in range(KVR):
                        q = pe.matmul(bank[:], z[:, Z_CKV + k, m * P:(m + 1) * P],
                                      wring[2 + k][:, half * 512:(half + 1) * 512], start=k == 0, stop=k == KVR - 1)
                    q.then_inc(prj_mm, 1)
                    e += 1
            n_proj = e
            pe.drain().then_inc(w_used[2], 1)
            pe.drain().then_inc(w_used[3], 1)
            pe.wait_ge(prj_ev, n_proj)
            for m in range(NT):
                for h in range(HEADS):
                    e = m * HEADS + h
                    if e >= 4:
                        pe.wait_ge(idx_relu, e - 3)
                    o = IDX_DIM * (h % 2)
                    pe.matmul(M[e % 4][:, 0:T], qiF[o:o + IDX_DIM, h // 2, m * P:(m + 1) * P],
                              z[o:o + IDX_DIM, Z_KIDX, :], start=True, stop=True).then_inc(idx_mm, 1)

            def attention(first, pairs, keys):
                with pe.Fori(0, pairs) as i:
                    n = i * 2 + first
                    for u in range(2):
                        pe.wait_ge(a_stage, n + (u + 1))
                        pe.wait_ge(a_max, n + u + 1)
                        for m in range(NT):
                            q = pe.matmul(M[u][:, m * T:(m + 1) * T], att_q[u][:, m * P:(m + 1) * P],
                                          dyn(keys, i * 2 + u), start=True, stop=True)
                        q.then_inc(a_mm, 1)
                    for u in range(2):
                        pe.wait_ge(a_p, n + (u + 1))
                        for m in range(NT):
                            for k in range(NT):
                                q = pe.transpose(M[2 + u][:, k * T + m * P:k * T + (m + 1) * P],
                                                 att_s[u][:, m, k * P:(k + 1) * P], ident)
                        q.then_inc(a_tr, 1)
                    for u in range(2):
                        pe.wait_ge(a_pt, n + (u + 1))
                        for k in range(NT):
                            q = pe.matmul(M[4 + u][:, 0:T], att_v[u][:, k, :], att_pT[u][:, k, :],
                                          start=k == 0, stop=k == NT - 1)
                        q.then_inc(a_o, 1)

            pe.wait_ge(idx_relu, 2 * HEADS)
            attention(0, HEADS // 2, kF)

            y_of = {0: yA, 1: yB, 2: yC}

            def gate_piece(n, j, q, g0, r0):
                i = q // 2
                at = 3 * j + i
                if q == 0:
                    pe.wait_ge(b_exp, n + 1)
                piece(G[0][:, i * T:(i + 1) * T], i, q % 2, at % WSLOTS, g0 + 2 * j + i, r0 + at // WSLOTS, PIECE,
                      h_hi, h_lo, k0=(q % 2) * PIECE)

            def proj_piece(n, j, c, r0, y):
                at = 3 * j + 2
                s = at % WSLOTS
                if c == 0:
                    pe.wait_ge(b_sum, n + 1)
                    landed(s, r0 + at // WSLOTS)
                e = chunk(G[1][:, c * T:(c + 1) * T], s, 8 * c, 8, lambda k: y[:, k, :])
                if c == 1:
                    e.then_inc(w_used[s], 1)

            pe.wait_ge(a_ev, 1 + HEADS)
            pe.wait_ge(lru_done, 1)
            with pe.Fori(0, HEADS // 2) as it:
                def gp(j, q):
                    gate_piece(it * 4 + j, j, q, it * 8 + G_AB, it * 3 + R_AB)

                def pp(j, c):
                    proj_piece(it * 4 + j, j, c, it * 3 + R_AB, y_of[j // 2])

                pe.wait_ge(d["sq"], it + 1)
                for i in range(2):
                    q = pe.matmul(M[3 * i][:], ones, g_sq[:, i * 512:(i + 1) * 512], start=True, stop=True)
                q.then_inc(d["ss"], 1)
                pe.wait_ge(d["v2"], it + 1)
                for p in range(4):
                    q = pe.transpose(M[2][:, p * P:(p + 1) * P], g_v2[:, p * P:(p + 1) * P], ident)
                q.then_inc(d["vtr"], 1)
                gp(0, 0)
                pe.wait_ge(d["rank1"], it + 1)
                pe.matmul(M[3][:], ones, g_ug, start=True, stop=True)
                pe.matmul(M[4][:], ones, g_db, start=True, stop=True).then_inc(d["bc"], 1)
                gp(0, 1)
                pe.wait_ge(d["qk"], it + 1)
                for u in range(2):
                    pe.transpose(M[5][:, u * P:(u + 1) * P], g_k2[:, 2 * u * P:(2 * u + 1) * P], ident)
                for p in range(4):
                    ks = g_k2[:, p * P:(p + 1) * P]
                    pe.matmul(M[0][:, p * P:(p + 1) * P], ks, ks, start=True, stop=True)
                    q = pe.matmul(M[1][:, p * P:(p + 1) * P], ks, g_q2[:, p * P:(p + 1) * P], start=True, stop=True)
                q.then_inc(d["prod"], 1)
                gp(0, 2)
                gp(0, 3)
                pe.wait_ge(d["e"], it * LEVELS + 1)
                pe.wait_ge(d["vt"], it + 1)
                for p in range(4):
                    q = pe.transpose(M[2][:, p * P:(p + 1) * P], g_e[0][:, p * P:(p + 1) * P], ident)
                q.then_inc(d["etr"], 1)
                pp(0, 0)
                fill = [(pp, 0, 1), (gp, 1, 0), (gp, 1, 1), (gp, 1, 2), (gp, 1, 3), (pp, 1, 0), (pp, 1, 1), (gp, 2, 0),
                        (gp, 2, 1), (gp, 2, 2), (gp, 2, 3), (pp, 2, 0)]
                for l in range(1, LEVELS):
                    e = g_e[l % EBUF]
                    pe.wait_ge(d["t"], it * LEVELS + l)
                    pe.wait_ge(d["e"], it * LEVELS + l + 1)
                    for p in range(4):
                        q = pe.matmul(M[3][:, p * P:(p + 1) * P], e[:, p * P:(p + 1) * P], g_t[:, p * P:(p + 1) * P],
                                      start=True, stop=True)
                    q.then_inc(d["m1"], 1)
                    fill[2 * l - 2][0](*fill[2 * l - 2][1:])
                    pe.wait_ge(d["ms"], it * (LEVELS - 1) + l)
                    for p in range(4):
                        c = slice(p * P, (p + 1) * P)
                        if l < LEVELS - 1:
                            pe.matmul(M[4][:, c], g_tt[:, c], g_ms[:, c], start=True, stop=True)
                        q = pe.matmul(M[5][:, c], g_ms[:, c], g_tt[:, c], start=True, stop=True)
                    q.then_inc(d["x"], 1)
                    fill[2 * l - 1][0](*fill[2 * l - 1][1:])
                pe.wait_ge(d["tb"], it + 1)
                for u in range(2):
                    p = 2 * u
                    q = pe.matmul(M[0][:, u * P:(u + 1) * P], g_tb[:, p * P:(p + 1) * P], g_vt[:, p * P:(p + 1) * P],
                                  start=True, stop=True)
                q.then_inc(d["v0mm"], 1)
                pp(2, 1)
                pe.wait_ge(d["v0"], it + 1)
                pe.wait_ge(d["kt"], it + 1)
                for u in range(2):
                    q = pe.matmul(M[2][:, u * P:(u + 1) * P], g_ktail[:, u * P:(u + 1) * P], g_v0[:, u * P:(u + 1) * P],
                                  start=True, stop=True)
                q.then_inc(d["smm"], 1)
                for u in range(2):
                    p = 2 * u
                    pe.matmul(M[1][:, p * P:(p + 1) * P], g_v0[:, u * P:(u + 1) * P], g_qk[:, p * P:(p + 1) * P],
                              start=True, stop=True)
                gp(3, 0)
                pe.wait_ge(d["s"], it + 1)
                for u in range(2):
                    p = 2 * u + 1
                    q = pe.matmul(M[3][:, u * P:(u + 1) * P], g_kw[:, p * P:(p + 1) * P], g_s[:, u * P:(u + 1) * P],
                                  start=True, stop=True)
                q.then_inc(d["ksmm"], 1)
                gp(3, 1)
                pe.wait_ge(d["r"], it + 1)
                for u in range(2):
                    p = 2 * u + 1
                    q = pe.matmul(M[4][:, u * P:(u + 1) * P], g_tb[:, p * P:(p + 1) * P], g_r[:, u * P:(u + 1) * P],
                                  start=True, stop=True)
                q.then_inc(d["v1mm"], 1)
                gp(3, 2)
                pe.wait_ge(d["v1"], it + 1)
                for u in range(2):
                    p = 2 * u + 1
                    pe.matmul(M[1][:, p * P:(p + 1) * P], g_s[:, u * P:(u + 1) * P], g_qd[:, p * P:(p + 1) * P],
                              start=True, stop=False)
                    q = pe.matmul(M[1][:, p * P:(p + 1) * P], g_v1[:, u * P:(u + 1) * P], g_qk[:, p * P:(p + 1) * P],
                                  start=False, stop=True)
                q.then_inc(d["o"], 1)
                gp(3, 3)
                pe.wait_ge(d["osq"], it + 1)
                pe.matmul(M[2][:], ones, g_osq, start=True, stop=True).then_inc(d["oss"], 1)
                pp(3, 0)
                pp(3, 1)
            pe.wait_ge(d["y"], 1 + HEADS // 2)
            with pe.Fori(0, 2) as it:
                for j in range(4):
                    for q in range(4):
                        gate_piece(it * 4 + (16 + j), j, q, it * 8 + G_C, it * 3 + R_C)
                    for c in range(2):
                        proj_piece(it * 4 + (16 + j), j, c, it * 3 + R_C, yC)
            pe.wait_ge(b_exp, 1 + 24)
            pe.wait_ge(b_sum, 1 + 24)
            with pe.Fori(0, KC // WSLOTS) as r:
                for s in range(WSLOTS):
                    pe.wait_ge(o_ev, r * WSLOTS + s + 1)
                    split_chunk(G[s % 2][:, 0:T], s, G_WO + r * WSLOTS + s, R_WO + r, h_hi, h_lo,
                                mg_h if s == 0 else None)
            norm_sums("mem")
            pe.wait_ge(o_ev, 2 + KC)
            for s in range(WSLOTS):
                if s >= 2:
                    pe.wait_ge(memk_ev, s - 1)
                split_chunk(G[s % 2][:, 0:T], s, G_MEM + s, R_MEM, m_hi, m_lo, n_h["mem"] if s == 0 else None)
            for s in range(WSLOTS):
                for q in range(2):
                    piece_ready(q, s, G_MEM + 4 + s, R_MEM + 1)
                    wh, wl = w_hi[2 * (s % 2) + q], w_lo[2 * (s % 2) + q]
                    for kk in range(2):
                        k = 4 * s + 2 * q + kk
                        c = slice(kk * 512, (kk + 1) * 512)
                        for m in range(NT):
                            t = slice(m * P, (m + 1) * P)
                            pe.matmul(M[1 + m][:], m_hi[:, k, t], wh[:, c], start=k == 0, stop=False)
                            pe.matmul(M[1 + m][:], m_hi[:, k, t], wl[:, c], start=False, stop=False)
                            e = pe.matmul(M[1 + m][:], m_lo[:, k, t], wh[:, c], start=False, stop=k == KC - 1)
                    e.then_inc(piece_used, 1)
            norm_sums("xat")
            pe.wait_ge(memk_ev, 4)
            for s in range(WSLOTS):
                if s >= 2:
                    pe.wait_ge(xq_ev, s - 1)
                split_chunk(G[s % 2][:, 0:T], s, G_XQ + s, R_X, h_hi, h_lo, n_h["xat"] if s == 0 else None)
            pe.wait_ge(xq_ev, 4)
            attention(HEADS, XHEADS // 2, mem_k)
            pe.wait_ge(a_ev, 1 + HEADS + XHEADS)
            for s in range(WSLOTS):
                landed(s, R_X + 1)
                for c in range(4):
                    n = 4 * s + c
                    if n >= 2:
                        pe.wait_ge(xo_ev, n - 1)
                    chunk(G[n % 2][:, 0:T], s, 4 * c, 4, lambda k: yX[:, k, :]).then_inc(xo_mm, 1)
                pe.drain().then_inc(w_used[s], 1)
            norm_sums("ffn")
            with pe.Fori(0, 2 * FF_CH // WSLOTS) as r:
                for s in range(WSLOTS):
                    pe.wait_ge(up_conv, r * WSLOTS + s + 1)
                    split_chunk(G[s % 2][:, 0:T], s, G_UP + r * WSLOTS + s, R_UP + r, h_hi, h_lo,
                                n_h["ffn"] if s == 0 else None)
            pe.wait_ge(up_h, FF_CH)
            with pe.Fori(0, KC // 2) as i:
                for u in range(2):
                    pe.wait_ge(dn_ev, i * 2 + (u + 1))
                    for s in range(WSLOTS):
                        r = i * 2 + (R_DOWN + u)
                        g = i * 8 + (G_DOWN + 4 * u + s)
                        piece(G[u][:, 0:T], s % 2, 0, s, g, r, PIECE, ff_hi, ff_lo, s * DOWN_BLOCKS, FF_CH)
                        piece(G[u][:, 0:T], s % 2, 1, s, g, r, DOWN_BLOCKS - PIECE, ff_hi, ff_lo,
                              s * DOWN_BLOCKS + PIECE, FF_CH)
            norm_sums("out")

        @block.scalar
        def _(act):
            def hold(s, value):
                act.wait_ge(s, value)
                act.sem_inc(act_turns, 1)

            def hi(b, q, s, g, r, blocks=PIECE):
                if q == 0:
                    act.wait_ge(w_landed[s], (r + 1) * 16)
                if not isinstance(g, int) or g >= 2:
                    act.wait_ge(piece_used, g * 2 + (q - 3))
                n = blocks * P
                act.copy(w_hi[2 * b + q][:, 0:n], wring[s][:, q * PIECE * P:q * PIECE * P + n]).then_inc(hi_done, 1)

            def hi_job(s, g, r, last=PIECE):
                hi(s % 2, 0, s, g, r)
                hi(s % 2, 1, s, g, r, last)

            def squares(k, src, waits=None):
                for q in range(4):
                    if waits:
                        act.wait_ge(waits[q], 16)
                    act.activation(flat(hf[:, 4 * q:4 * q + 4, :]), flat(src[:, 4 * q:4 * q + 4, :]),
                                   ACT.Square).then_inc(n_sq[k], 1)

            def root(k):
                act.wait_ge(n_ss[k], 1)
                act.activation(rt, M[0][:, 0:T], ACT.Sqrt, bias=eps, scale=1.0 / D).then_inc(n_rt[k], 1)

            def round_chunks(ready, done, dst):
                for c in range(KC):
                    act.wait_ge(ready, c + 1)
                    act.copy(dst[:, c, :], hf[:, c, :]).then_inc(done, 1)

            for q in range(4):
                act.dma_start(xT[:, 4 * q:4 * q + 4, :], dr["x"][:, 4 * q:4 * q + 4, :]).then_inc(x_in[q], 16)
                if q == 0:
                    act.dma_start(consts[:], dr["consts"]).then_inc(const_in, 16)
                    act.dma_start(prm[:], dr["prm"]).then_inc(const_in, 16)
            act.dma_start(masks[:], dr["masks"]).then_inc(const_in, 16)
            act.dma_start(negmask, dr["negmask"]).then_inc(const_in, 16)
            act.sem_inc(a_ev, 1)
            act.sem_inc(in_ev, 2)
            act.wait_ge(const_in, 64)
            squares("mix", xT, x_in)
            for g in range(2):
                hi_job(g, g, R_IN)
            root("mix")
            round_chunks(n_f["mix"], n_hi["mix"], h_hi)

            def in_round(r, silu, ahead):
                for s in range(WSLOTS):
                    c = r * WSLOTS + s
                    hold(piece_used, c * 2 + (2 * G_IN + 2))
                    act.copy(dyn(z, c), G[s % 2][:, 0:T]).then_inc(in_ev, 1)
                    if s < ahead:
                        hi_job((s + 2) % WSLOTS, c + (G_IN + 2), r + (R_IN + (s + 2) // WSLOTS))
                    if silu:
                        hold(qconv, c - (Z_FLAT - 1))
                        act.activation(dyn(z, c), ctmp[s % 2], ACT.Silu).then_inc(qsilu, 1)

            with act.Fori(0, Z_FLAT // WSLOTS) as r:
                in_round(r, False, WSLOTS)
            with act.Fori(Z_FLAT // WSLOTS, Z_CH // WSLOTS - 1) as r:
                in_round(r, True, WSLOTS)
            in_round(Z_CH // WSLOTS - 1, True, 2)
            act.activation(flat(z[:, Z_GZ:Z_GZ + 8, :]), flat(z[:, Z_GZ:Z_GZ + 8, :]), ACT.Silu).then_inc(gates_act, 1)
            act.activation(flat(yA), flat(yA), ACT.Gelu_apprx_tanh).then_inc(gates_act, 1)
            act.activation(flat(dsq), flat(z[:, Z_CQ:Z_CQ + 6, :]), ACT.Square).then_inc(lat_sq, 1)
            act.wait_ge(lat_ss, 1)
            act.activation(drt[:, 0:T], M[0][:, 0:T], ACT.Sqrt, bias=eps, scale=1.0 / (QR * P)).then_inc(lat_rt, 1)
            act.activation(drt[:, T:2 * T], M[0][:, T:2 * T], ACT.Sqrt, bias=eps, scale=1.0 / (KVR * P)).then_inc(lat_rt, 1)
            act.wait_ge(sp_in, 1)
            act.activation(sp_e, sp_x, ACT.Abs)
            act.activation(ea, prm[:, PCOL["gdn_a_log"]:PCOL["gdn_a_log"] + 8], ACT.Exp)
            act.drain()
            act.activation(sp_e, sp_e, ACT.Exp, scale=-1.0).then_inc(sp_ex, 1)
            act.activation(beta.rearrange("p (m n) -> p m n", m=NT), tokc[:, :, 8:16], ACT.Sigmoid).then_inc(beta_done, 1)
            for j in range(2 * LRU_CH):
                c = j % LRU_CH
                act.wait_ge(lru_mm, j + 1)
                dst, b = (lr, "lru_ba") if j < LRU_CH else (li, "lru_bx")
                act.activation(dst[:, c, :], M[3 + j % 3][:, 0:T], ACT.Sigmoid, bias=col(b, c)).then_inc(lru_sig, 1)
            act.wait_ge(sp_done, 1)
            act.drain()
            for c in range(LRU_CH):
                act.activation(la[:, c, :], lr[:, c, :], ACT.Exp, scale=lam_n[:, c:c + 1])
                act.activation(lt[:, c, :], lr[:, c, :], ACT.Tanh, scale=lam_p[:, c:c + 1]).then_inc(lru_at, 1)
            act.wait_ge(lru_m2, 1)
            act.activation(flat(lr), flat(lt), ACT.Sqrt, scale=2.0).then_inc(lru_root, 1)
            act.wait_ge(lru_done, 1)
            dsts = ([flat(qiF[:, 2 * i:2 * i + 2, :]) for i in range(2)] + [flat(kF[:, 2 * i:2 * i + 2, :]) for i in range(4)]
                    + [flat(qF[:, 2 * i:2 * i + 2, :]) for i in range(4)]
                    + [vT[:, m, h * 512:(h + 1) * 512] for m in range(NT) for h in range(2)])
            for e, dst in enumerate(dsts):
                act.wait_ge(prj_mm, e + 1)
                act.copy(dst, M[e % 4][:]).then_inc(prj_ev, 1)
            for e in range(NT * HEADS):
                act.wait_ge(idx_mm, e + 1)
                if e >= 2:
                    act.wait_ge(idx_acc, e - 1)
                act.activation(rl[e % 2], M[e % 4][:, 0:T], ACT.Relu).then_inc(idx_relu, 1)

            def attention(first, pairs, dst):
                with act.Fori(0, pairs) as i:
                    n = i * 2 + first
                    for u in range(2):
                        act.wait_ge(a_max, n + (u + 3))
                        for m in range(NT):
                            q = act.activation(att_s[u][:, m, :], att_s[u][:, m, :], ACT.Exp, bias=amax[u][:, m:m + 1],
                                               accum_out=asum[u][:, m:m + 1])
                        q.then_inc(a_exp, 1)
                    for u in range(2):
                        act.wait_ge(a_tr, n + (u + 1))
                        act.copy(flat(att_pT[u]), M[2 + u][:]).then_inc(a_pt, 1)
                    for u in range(2):
                        hold(a_o, n + (u + 1))
                        act.copy(dyn(dst, i * 2 + u), M[4 + u][:, 0:T]).then_inc(a_ev, 1)

            attention(0, HEADS // 2, yB)

            def gate(n, g):
                act.wait_ge(b_sum, n + 1)
                act.wait_ge(piece_used, g * 2 + 2)
                act.activation(sg, G[0][:], ACT.Exp, scale=-1.0).then_inc(b_exp, 1)

            def hi_unit(j, q, g0, r0):
                at = 3 * j + q // 2
                hi(q // 2, q % 2, at % WSLOTS, g0 + (2 * j + q // 2), r0 + at // WSLOTS)

            act.sem_inc(b_exp, 1)
            for q in range(4):
                hi_unit(0, q, G_AB, R_AB)
            with act.Fori(0, HEADS // 2) as it:
                def hi_of(j, q):
                    hi_unit(j, q, it * 8 + G_AB, it * 3 + R_AB)

                act.activation(g_sq[:, 0:512], dyn(z, it * 2 + Z_Q, 2), ACT.Square)
                act.activation(g_sq[:, 512:1024], dyn(z, it * 2 + Z_K, 2), ACT.Square).then_inc(d["sq"], 1)
                act.wait_ge(d["ss"], it + 1)
                for i in range(2):
                    q = act.activation(g_rt[:, i * 512:(i + 1) * 512], M[3 * i][:], ACT.Sqrt, bias=eps)
                q.then_inc(d["rt"], 1)
                act.wait_ge(d["vtr"], it + 1)
                act.copy(g_vt, M[2][:])
                hi_of(1, 0)
                act.wait_ge(d["diff"], it + 1)
                act.activation(g_eg, M[3][:], ACT.Exp)
                act.activation(g_dec, g_dec, ACT.Exp).then_inc(d["dec"], 1)
                hi_of(1, 1)
                act.wait_ge(d["prod"], it + 1)
                act.copy(g_kt, M[5][:, 0:2 * P]).then_inc(d["vt"], 1)
                gate(it * 4, it * 8 + (G_AB + 1))
                hi_of(1, 2)
                hi_of(1, 3)
                after = {2: [(2, 0)], 3: [(2, 1), (2, 2)], 4: [(2, 3)], 5: [(3, 0)], 6: [(3, 1), (3, 2)]}
                for l in range(1, LEVELS):
                    act.wait_ge(d["m1"], it * (LEVELS - 1) + l)
                    act.copy(g_ms, M[3][:]).then_inc(d["ms"], 1)
                    if l == 3:
                        gate(it * 4 + 1, it * 8 + (G_AB + 3))
                    if l == 6:
                        gate(it * 4 + 2, it * 8 + (G_AB + 5))
                    for j, q in after.get(l, ()):
                        hi_of(j, q)
                hold(d["t"], it * LEVELS + LEVELS)
                for u in range(2):
                    for m in range(NT):
                        c = slice((2 * u + m) * P, (2 * u + m + 1) * P)
                        q = act.activation(g_tb[:, c], g_tt[:, c], ACT.Copy,
                                           scale=beta[:, bass.ds(it * 2 + (u + 8 * m), 1)])
                q.then_inc(d["tb"], 1)
                hi_of(3, 3)
                act.wait_ge(d["smm"], it + 1)
                act.copy(g_s, M[2][:, 0:2 * P]).then_inc(d["s"], 1)
                hi_of(4, 0)
                hi_of(4, 1)
                act.wait_ge(d["o"], it + 1)
                act.activation(g_osq, M[1][:], ACT.Square).then_inc(d["osq"], 1)
                hi_of(4, 2)
                hi_of(4, 3)
                gate(it * 4 + 3, it * 8 + (G_AB + 7))
                act.wait_ge(d["oss"], it + 1)
                act.activation(g_ort, M[2][:], ACT.Sqrt, bias=eps, scale=1.0 / P).then_inc(d["ort"], 1)
            act.wait_ge(d["y"], 1 + HEADS // 2)
            act.dma_start(xT[:], dr["x"]).then_inc(x_back, 16)
            act.dma_start(mem_in, dr["mem"]).then_inc(mem_loaded, 16)

            def c_unit(it, j, ahead=True):
                n = it * 4 + (16 + j)
                g = it * 8 + (G_C + 2 * j)
                act.wait_ge(piece_used, g * 2 + 4)
                gate(n, g + 1)
                if ahead:
                    for q in range(4):
                        hi_unit(j + 1, q, it * 8 + G_C, it * 3 + R_C)

            with act.Fori(0, 2) as it:
                for j in range(4):
                    c_unit(it, j)
            act.wait_ge(b_sum, 1 + 24)
            for c in range(KC):
                act.copy(h_hi[:, c, :], merged[:, c, :]).then_inc(mg_hi, 1)

            def o_round(r):
                for s in range(WSLOTS):
                    hi_job((s + 2) % WSLOTS, r * WSLOTS + (s + G_WO + 2), r + (R_WO + (s + 2) // WSLOTS))

            o_round(0)
            act.wait_ge(mem_loaded, 16)
            act.wait_ge(mg_h, KC)
            squares("mem", mem_in)
            with act.Fori(1, KC // WSLOTS) as r:
                o_round(r)
            root("mem")
            round_chunks(n_f["mem"], n_hi["mem"], m_hi)
            for s in range(WSLOTS):
                act.wait_ge(piece_used, 2 * (G_MEM + s) + 2)
                act.copy(mem_k[:, s, :], G[s % 2][:, 0:T]).then_inc(memk_ev, 1)
                hi_job((s + 2) % WSLOTS, G_MEM + s + 2, R_MEM + (s + 2) // WSLOTS)
            act.wait_ge(o_ev, 2 + KC)
            squares("xat", xT)
            for s in range(WSLOTS):
                hi_job((s + 2) % WSLOTS, G_MEM + s + 6, R_MEM + 1 + (s + 2) // WSLOTS)
            for m in range(NT):
                act.copy(mem_v[:, m, :], M[1 + m][:]).then_inc(memv_ev, 1)
            root("xat")
            round_chunks(n_f["xat"], n_hi["xat"], h_hi)
            for s in range(WSLOTS):
                act.wait_ge(piece_used, 2 * (G_XQ + s) + 2)
                act.copy(xqF[:, s, :], G[s % 2][:, 0:T]).then_inc(xq_ev, 1)
                if s < 2:
                    hi_job(s + 2, G_XQ + s + 2, R_X)
            attention(HEADS, XHEADS // 2, yX)
            act.wait_ge(xo_ev, KC)
            squares("ffn", xT)
            for s in range(2):
                hi_job(s, G_UP + s, R_UP)
            root("ffn")
            round_chunks(n_f["ffn"], n_hi["ffn"], h_hi)

            def up_round(r, last):
                for s in range(WSLOTS):
                    u = s // 2
                    c = r * 2 + u
                    if s % 2 == 0:
                        act.wait_ge(up_conv, r * WSLOTS + (s + 3))
                        act.activation(flat(ff_t[:, u:u + 1, :]), flat(ff_t[:, u:u + 1, :]), ACT.Silu).then_inc(up_silu, 1)
                    down = last and s >= 2
                    hi_job((s + 2) % WSLOTS, r * WSLOTS + (s + G_UP + 2), r + (R_UP + (s + 2) // WSLOTS),
                           DOWN_BLOCKS - PIECE if down else PIECE)
                    if s % 2:
                        hold(up_f, c + 1)
                        act.copy(dyn(ff_hi, c), flat(ff_t[:, u:u + 1, :])).then_inc(up_hi, 1)

            rounds = 2 * FF_CH // WSLOTS
            with act.Fori(0, rounds - 1) as r:
                up_round(r, False)
            up_round(rounds - 1, True)
            with act.Fori(0, KC - 1) as r:
                for s in range(WSLOTS):
                    hi_job((s + 2) % WSLOTS, r * WSLOTS + (s + G_DOWN + 2), r + (R_DOWN + (s + 2) // WSLOTS),
                           DOWN_BLOCKS - PIECE)
            for s in range(2):
                hi_job(s + 2, G_DOWN + 4 * (KC - 1) + s + 2, R_DOWN + KC - 1, DOWN_BLOCKS - PIECE)
            act.wait_ge(dn_ev, 2 + KC)
            squares("out", xT)
            root("out")

        @block.vector
        def _(dve):
            def lo(b, q, s, g, blocks=PIECE):
                dve.wait_ge(hi_done, g * 2 + (q + 1))
                n = blocks * P
                dve.tensor_tensor(w_lo[2 * b + q][:, 0:n], wring[s][:, q * PIECE * P:q * PIECE * P + n],
                                  w_hi[2 * b + q][:, 0:n].bitcast(F32), ALU.subtract).then_inc(w_used[s] if q else lo_first, 1)

            def lo_job(s, g, last=PIECE):
                lo(s % 2, 0, s, g)
                lo(s % 2, 1, s, g, last)

            def norm(k, src, gain, hi=None, lo=None):
                dve.wait_ge(n_rt[k], 1)
                dve.reciprocal(rt, rt)
                dve.drain()
                for c in range(KC + 2):
                    if c < KC:
                        dve.scalar_tensor_tensor(out=hf[:, c, :], in0=src[:, c, :], scalar=col(gain, c), in1=rt,
                                                 op0=ALU.mult, op1=ALU.mult).then_inc(n_f[k], 1)
                    if c >= 2 and hi is not None:
                        dve.wait_ge(n_hi[k], c - 1)
                        dve.tensor_tensor(lo[:, c - 2, :], hf[:, c - 2, :], hi[:, c - 2, :].bitcast(F32),
                                          ALU.subtract).then_inc(n_h[k], 1)

            def conv(dst, src, name, taps, chunks, c, bias=None):
                def w(k):
                    return prm[:, bass.ds(PCOL[name] + k * chunks + c, 1)]
                if bias is None:
                    dve.tensor_scalar(dst, src, w(taps - 1), None, ALU.mult)
                else:
                    dve.tensor_scalar(dst, src, w(taps - 1), bias, ALU.mult, ALU.add)
                for lag in range(1, taps):
                    dve.drain()
                    q = dve.scalar_tensor_tensor(out=dst[:, lag:T], in0=src[:, 0:T - lag], scalar=w(taps - 1 - lag),
                                                 in1=dst[:, lag:T], op0=ALU.mult, op1=ALU.add)
                return q

            dve.sem_inc(b_sum, 1)
            dve.sem_inc(a_max, 2)
            dve.sem_inc(d["y"], 1)
            dve.sem_inc(o_ev, 2)
            dve.sem_inc(dn_ev, 2)
            dve.sem_inc(up_conv, 2)
            dve.wait_ge(const_in, 64)
            for g in range(2):
                lo_job(g, g)
            norm("mix", xT, "ln_mix", h_hi, h_lo)

            def in_round(r, kind, ahead):
                for s in range(WSLOTS):
                    c = r * WSLOTS + s
                    if s < ahead:
                        lo_job((s + 2) % WSLOTS, c + (G_IN + 2))
                    if kind:
                        dve.wait_ge(in_ev, c + 3)
                    if kind == "x":
                        conv(dyn(xc, c - Z_AX), dyn(z, c), "conv_a_w", 4, LRU_CH, c - Z_AX,
                             bias=col("conv_a_b", c - Z_AX)).then_inc(xconv, 1)
                    if kind == "q":
                        conv(ctmp[s % 2], dyn(z, c), "gdn_conv_w", 4, Z_CH - Z_FLAT, c - Z_FLAT).then_inc(qconv, 1)

            for kind, a, b in ((None, 0, Z_AX), ("x", Z_AX, Z_CQ), (None, Z_CQ, Z_FLAT), ("q", Z_FLAT, Z_CH - WSLOTS)):
                with dve.Fori(a // WSLOTS, b // WSLOTS) as r:
                    in_round(r, kind, WSLOTS)
            in_round(Z_CH // WSLOTS - 1, "q", 2)
            dve.wait_ge(lat_rt, 2)
            dve.reciprocal(drt, drt)
            dve.drain()
            for c in range(QR + KVR):
                name, cc, r = ("dsa_q_norm", c, drt[:, 0:T]) if c < QR else ("dsa_kv_norm", c - QR, drt[:, T:2 * T])
                q = dve.scalar_tensor_tensor(out=z[:, Z_CQ + c, :], in0=z[:, Z_CQ + c, :], scalar=col(name, cc), in1=r,
                                             op0=ALU.mult, op1=ALU.mult)
            q.then_inc(lat_n, 1)
            dve.wait_ge(tok_mm, 1)
            dve.tensor_copy(tokc, M[1][:, 0:64].rearrange("p (m n) -> p m n", m=NT)).then_inc(tok_ev, 1)
            lam = prm[:, PCOL["lru_lambda"]:PCOL["lru_lambda"] + 8]
            dtb = prm[:, PCOL["gdn_dt_bias"]:PCOL["gdn_dt_bias"] + 8]
            dve.tensor_scalar(sp_x[:, 0:8], lam, -1.0, None, ALU.mult)
            dve.drain()
            for m in range(NT):
                dve.tensor_tensor(sp_x[:, 8 + 8 * m:16 + 8 * m], tokc[:, m, 16:24], dtb, ALU.add)
            dve.tensor_scalar(widx, tokc[:, :, 0:8], float(HEADS ** -0.5 * IDX_DIM ** -0.5), None, ALU.mult)
            dve.drain().then_inc(sp_in, 1)
            dve.wait_ge(sp_ex, 1)
            dve.tensor_scalar(sp_s, sp_e, 2.0, None, ALU.add)
            dve.drain()
            dve.reciprocal(sp_s, sp_s)
            dve.drain()
            dve.tensor_tensor(sp_s, sp_s, sp_e, ALU.mult)
            dve.drain()
            dve.tensor_tensor(sp_z, sp_s, sp_s, ALU.mult)
            dve.drain()
            dve.tensor_scalar(sp_p, sp_z, 1.0 / 17, None, ALU.mult)
            for k in range(15, 1, -2):
                dve.drain()
                dve.scalar_tensor_tensor(out=sp_p, in0=sp_p, scalar=1.0 / k, in1=sp_z, op0=ALU.add, op1=ALU.mult)
            dve.drain()
            dve.scalar_tensor_tensor(out=sp_p, in0=sp_p, scalar=1.0, in1=sp_s, op0=ALU.add, op1=ALU.mult)
            dve.tensor_scalar(sp, sp_x, 0.0, None, ALU.max)
            dve.drain()
            dve.scalar_tensor_tensor(out=sp, in0=sp_p, scalar=2.0, in1=sp, op0=ALU.mult, op1=ALU.add)
            dve.drain()
            dve.tensor_scalar(lam_n, sp[:, 0:8], -LRU_C, None, ALU.mult)
            dve.tensor_scalar(lam_p, sp[:, 0:8], LRU_C, None, ALU.mult)
            for m in range(NT):
                dve.scalar_tensor_tensor(out=gdec[:, 8 * m:8 * m + 8], in0=sp[:, 8 + 8 * m:16 + 8 * m], scalar=-1.0,
                                         in1=ea, op0=ALU.mult, op1=ALU.mult)
            dve.drain().then_inc(sp_done, 1)
            dve.wait_ge(gcum_mm, 1)
            dve.tensor_copy(gcum, M[2][:, 0:16]).then_inc(gcum_ev, 1)
            dve.wait_ge(lru_at, LRU_CH)
            dve.tensor_scalar(flat(lr), flat(lt), 1.0, None, ALU.add)
            dve.drain()
            dve.reciprocal(flat(lr), flat(lr))
            dve.drain()
            dve.tensor_tensor(flat(lt), flat(lt), flat(lr), ALU.mult).then_inc(lru_m2, 1)
            dve.tensor_tensor(flat(li), flat(li), flat(xc), ALU.mult)
            dve.wait_ge(lru_root, 1)
            dve.memset(lr[:, :, 0:1], 1.0)
            dve.drain()
            dve.tensor_tensor(flat(li), flat(li), flat(lr), ALU.mult)
            dve.drain()
            for c in range(LRU_CH):
                dve.tensor_tensor_scan(lt[:, c, :], la[:, c, :], li[:, c, :], 0.0, ALU.mult, ALU.add)
            dve.drain()
            dve.wait_ge(gates_act, 2)
            dve.tensor_tensor(flat(yA), flat(yA), flat(lt), ALU.mult).then_inc(lru_done, 1)
            for m in range(NT):
                for h in range(HEADS):
                    e = m * HEADS + h
                    dve.drain()
                    dve.wait_ge(idx_relu, e + 1)
                    dve.scalar_tensor_tensor(out=score[:, m, :], in0=rl[e % 2], scalar=widx[:, m, h:h + 1],
                                             in1=negmask[:, m, :] if h == 0 else score[:, m, :],
                                             op0=ALU.mult, op1=ALU.add).then_inc(idx_acc, 1)
            with dve.Fori(0, TOPK // 8) as _:
                dve.drain()
                for m in range(NT):
                    dve.max(top8[:, m, :], score[:, m, :])
                dve.drain()
                for m in range(NT):
                    dve.match_replace(score[:, m, :], top8[:, m, :], score[:, m, :], TAKEN)
            dve.drain()
            dve.tensor_scalar(flat(sbias), flat(score), TAKEN, 1.0, ALU.is_equal, ALU.subtract)
            dve.drain()
            dve.scalar_tensor_tensor(out=flat(sbias), in0=flat(sbias), scalar=-NEG, in1=flat(negmask),
                                     op0=ALU.mult, op1=ALU.add)
            dve.drain()

            def attention(first, pairs, bias):
                scale = float(P ** -0.5)
                with dve.Fori(0, pairs) as i:
                    n = i * 2 + first
                    for u in range(2):
                        dve.wait_ge(a_mm, n + (u + 1))
                        if bias is None:
                            dve.tensor_scalar(flat(att_s[u]), M[u][:], scale, None, ALU.mult)
                        else:
                            dve.scalar_tensor_tensor(out=flat(att_s[u]), in0=M[u][:], scalar=scale, in1=flat(bias),
                                                     op0=ALU.mult, op1=ALU.add)
                        dve.drain()
                        dve.tensor_reduce(amax[u], att_s[u], AX.X, ALU.max)
                        dve.drain()
                        dve.tensor_scalar(amax[u], amax[u], -1.0, None, ALU.mult).then_inc(a_max, 1)
                    for u in range(2):
                        dve.wait_ge(a_exp, n + (u + 1))
                        dve.reciprocal(asum[u], asum[u])
                        dve.drain()
                        for m in range(NT):
                            q = dve.tensor_scalar(att_s[u][:, m, :], att_s[u][:, m, :], asum[u][:, m:m + 1], None, ALU.mult)
                        q.then_inc(a_p, 1)

            attention(0, HEADS // 2, sbias)

            def merge(n, c, j, r0, first):
                dve.wait_ge(b_exp, n + 2)
                dve.tensor_scalar(sg, sg, 1.0, None, ALU.add)
                dve.drain()
                dve.reciprocal(sg, sg)
                dve.drain()
                at = 3 * j + 2
                dve.wait_ge(w_used[at % WSLOTS], r0 + (at // WSLOTS + 1))
                if first:
                    dve.tensor_tensor(dyn(merged, c, 2), G[1][:], sg, ALU.mult)
                else:
                    dve.tensor_tensor(sg, G[1][:], sg, ALU.mult)
                    dve.drain()
                    dve.tensor_tensor(dyn(merged, c, 2), dyn(merged, c, 2), sg, ALU.add)
                dve.drain().then_inc(b_sum, 1)

            def lo_unit(j, q, g0):
                at = 3 * j + q // 2
                lo(q // 2, q % 2, at % WSLOTS, g0 + (2 * j + q // 2))

            for q in range(4):
                lo_unit(0, q, G_AB)

            def heads(ap):
                return ap.rearrange("p (q n) -> p q n", q=4)

            def over(ap):
                return ap.unsqueeze(1).broadcast_to([P, 4, P])

            with dve.Fori(0, HEADS // 2) as it:
                def lo_of(j, q):
                    lo_unit(j, q, it * 8 + G_AB)

                def merge_ab(j):
                    merge(it * 4 + j, it * 4 + 2 * (j % 2), j, it * 3 + R_AB, j < 2)

                dve.wait_ge(d["rt"], it + 1)
                for u in range(2):
                    for m in range(NT):
                        c = slice((2 * u + m) * P, (2 * u + m + 1) * P)
                        at = it * 2 + (u + 8 * m)
                        dve.tensor_scalar(g_ug[:, c], tri, gdec[:, bass.ds(at, 1)], None, ALU.mult)
                        q = dve.tensor_scalar(g_db[:, c], ident, beta[:, bass.ds(at, 1)], None, ALU.mult)
                q.then_inc(d["rank1"], 1)
                dve.reciprocal(g_rt, g_rt)
                dve.drain()
                dve.scalar_tensor_tensor(out=g_q2, in0=dyn(z, it * 2 + Z_Q, 2), scalar=float(P ** -0.5),
                                         in1=g_rt[:, 0:512], op0=ALU.mult, op1=ALU.mult)
                dve.tensor_tensor(g_k2, dyn(z, it * 2 + Z_K, 2), g_rt[:, 512:1024], ALU.mult).then_inc(d["qk"], 1)
                dve.drain()
                dve.wait_ge(d["bc"], it + 1)
                for u in range(2):
                    for m in range(NT):
                        c = slice((2 * u + m) * P, (2 * u + m + 1) * P)
                        q = dve.tensor_scalar(g_dec[:, c], M[3][:, c], gcum[:, bass.ds(it * 2 + (u + 8 * m), 1)], 0.0,
                                              ALU.subtract, ALU.min)
                q.then_inc(d["diff"], 1)
                lo_of(1, 0)
                dve.wait_ge(d["dec"], it + 1)
                dve.tensor_tensor(heads(g_dec), heads(g_dec), over(tri), ALU.mult)
                lo_of(1, 1)
                dve.drain()
                dve.wait_ge(d["prod"], it + 1)
                dve.tensor_tensor(g_bd, g_dec, M[4][:], ALU.mult)
                dve.drain()
                dve.tensor_tensor(g_at, g_bd, M[0][:], ALU.mult).then_inc(d["at"], 1)
                dve.tensor_tensor(g_qk, g_dec, M[1][:], ALU.mult)
                dve.tensor_tensor(g_kw, g_k2, g_eg, ALU.mult)
                dve.tensor_tensor(g_qd, g_q2, g_eg, ALU.mult)
                dve.wait_ge(d["vt"], it + 1)
                for u in range(2):
                    last = (2 * u + 1) * P - 1
                    q = dve.tensor_scalar(g_ktail[:, u * P:(u + 1) * P], g_kt[:, u * P:(u + 1) * P],
                                          g_dec[:, last:last + 1], None, ALU.mult)
                q.then_inc(d["kt"], 1)
                lo_of(1, 2)
                dve.wait_ge(d["etr"], it + 1)
                dve.tensor_tensor(heads(g_t), over(ident), heads(M[2][:]), ALU.subtract)
                dve.tensor_tensor(heads(g_tt), over(ident), heads(g_e[0]), ALU.subtract).then_inc(d["t"], 1)
                lo_of(1, 3)
                merge_ab(0)
                after = {2: [(2, 0)], 3: [(2, 1), (2, 2)], 4: [(2, 3)], 5: [(3, 0)], 6: [(3, 1), (3, 2)]}
                for l in range(1, LEVELS):
                    dve.drain()
                    dve.wait_ge(d["x"], it * (LEVELS - 1) + l)
                    if l < LEVELS - 1:
                        dve.tensor_tensor(g_t, g_t, M[4][:], ALU.subtract)
                    dve.tensor_tensor(g_tt, g_tt, M[5][:], ALU.subtract).then_inc(d["t"], 1)
                    for j, q in after.get(l, ()):
                        lo_of(j, q)
                    if l == 4:
                        merge_ab(1)
                dve.wait_ge(d["v0mm"], it + 1)
                dve.tensor_copy(g_v0, M[0][:, 0:2 * P]).then_inc(d["v0"], 1)
                merge_ab(2)
                lo_of(3, 3)
                dve.wait_ge(d["ksmm"], it + 1)
                for u in range(2):
                    q = dve.tensor_tensor(g_r[:, u * P:(u + 1) * P], g_vt[:, (2 * u + 1) * P:(2 * u + 2) * P],
                                          M[3][:, u * P:(u + 1) * P], ALU.subtract)
                q.then_inc(d["r"], 1)
                dve.wait_ge(d["v1mm"], it + 1)
                dve.tensor_copy(g_v1, M[4][:, 0:2 * P]).then_inc(d["v1"], 1)
                for q in range(4):
                    lo_of(4, q)
                dve.wait_ge(d["ort"], it + 1)
                dve.reciprocal(g_ort, g_ort)
                dve.drain()
                dve.scalar_tensor_tensor(out=g_ort, in0=M[1][:], scalar=col("gdn_o_norm", 0), in1=g_ort,
                                         op0=ALU.mult, op1=ALU.mult)
                dve.drain()
                dve.tensor_tensor(dyn(yC, it * 2, 2), dyn(yC, it * 2, 2), g_ort, ALU.mult).then_inc(d["y"], 1)
                merge_ab(3)
            with dve.Fori(0, 2) as it:
                for j in range(4):
                    for q in range(4):
                        lo_unit(j + 1, q, it * 8 + G_C)
                    merge(it * 4 + (16 + j), it * 8 + 2 * j, j, it * 3 + R_C, False)
            for c in range(KC):
                dve.wait_ge(mg_hi, c + 1)
                dve.tensor_tensor(h_lo[:, c, :], merged[:, c, :], h_hi[:, c, :].bitcast(F32), ALU.subtract).then_inc(mg_h, 1)
            dve.wait_ge(x_back, 16)
            with dve.Fori(0, KC // WSLOTS) as r:
                for s in range(WSLOTS):
                    c = r * WSLOTS + s
                    lo_job((s + 2) % WSLOTS, c + (G_WO + 2))
                    dve.wait_ge(piece_used, c * 2 + (2 * G_WO + 2))
                    dve.tensor_tensor(dyn(xT, c), dyn(xT, c), G[s % 2][:, 0:T], ALU.add).then_inc(o_ev, 1)
            norm("mem", mem_in, "mem_norm", m_hi, m_lo)
            for s in range(WSLOTS):
                lo_job((s + 2) % WSLOTS, G_MEM + s + 2)
            for s in range(WSLOTS):
                lo_job((s + 2) % WSLOTS, G_MEM + s + 6)
            norm("xat", xT, "ln_mem", h_hi, h_lo)
            for s in range(2):
                lo_job(s + 2, G_XQ + s + 2)
            attention(HEADS, XHEADS // 2, None)
            for c in range(KC):
                dve.wait_ge(xo_mm, c + 1)
                dve.tensor_tensor(xT[:, c, :], xT[:, c, :], G[c % 2][:, 0:T], ALU.add).then_inc(xo_ev, 1)
            for s in range(2):
                lo_job(s, G_UP + s)
            norm("ffn", xT, "ln_ffn", h_hi, h_lo)

            def up_round(r, last):
                for s in range(WSLOTS):
                    u = s // 2
                    c = r * 2 + u
                    dve.wait_ge(piece_used, r * 8 + (2 * (G_UP + s) + 2))
                    dst = flat(ff_t[:, u:u + 1, :]) if s % 2 == 0 else flat(ff_t[:, 2:3, :])
                    conv(dst, G[s % 2][:, 0:T], "ffn_conv_w", 3, 2 * FF_CH, c + (s % 2) * FF_CH).then_inc(up_conv, 1)
                    if s % 2:
                        dve.drain()
                        dve.wait_ge(up_silu, c + 1)
                        dve.tensor_tensor(flat(ff_t[:, u:u + 1, :]), flat(ff_t[:, u:u + 1, :]), dst, ALU.mult).then_inc(up_f, 1)
                    down = last and s >= 2
                    lo_job((s + 2) % WSLOTS, r * WSLOTS + (s + G_UP + 2), DOWN_BLOCKS - PIECE if down else PIECE)
                    if s % 2:
                        dve.wait_ge(up_hi, c + 1)
                        dve.tensor_tensor(dyn(ff_lo, c), flat(ff_t[:, u:u + 1, :]), dyn(ff_hi, c).bitcast(F32),
                                          ALU.subtract).then_inc(up_h, 1)

            rounds = 2 * FF_CH // WSLOTS
            with dve.Fori(0, rounds - 1) as r:
                up_round(r, False)
            up_round(rounds - 1, True)

            def down_chunk(c, u, ahead):
                for s in range(ahead):
                    lo_job((s + 2) % WSLOTS, c * WSLOTS + (s + G_DOWN + 2), DOWN_BLOCKS - PIECE)
                dve.wait_ge(piece_used, c * 8 + (2 * G_DOWN + 8))
                dve.tensor_tensor(dyn(xT, c), dyn(xT, c), G[u][:, 0:T], ALU.add).then_inc(dn_ev, 1)

            with dve.Fori(0, KC // 2 - 1) as i:
                for u in range(2):
                    down_chunk(i * 2 + u, u, WSLOTS)
            down_chunk(KC - 2, 0, WSLOTS)
            down_chunk(KC - 1, 1, 2)
            norm("out", xT, "ln_f")

        @block.gpsimd
        def _(pool):
            def attention(first, pairs, queries, values):
                with pool.Fori(0, pairs) as i:
                    n = i * 2 + first
                    for u in range(2):
                        pool.wait_ge(a_ev, n + 1)
                        pool.tensor_copy(att_q[u], dyn(queries, i * 2 + u))
                        pool.tensor_copy(att_v[u], values[:, :, bass.ds((i * 2 + u) * P, P)])
                        pool.drain().then_inc(a_stage, 1)

            pool.wait_ge(prj_ev, 14)
            attention(0, HEADS // 2, qF, vT)
            pool.wait_ge(a_ev, 1 + HEADS)
            with pool.Fori(0, HEADS // 2) as it:
                pool.wait_ge(d["y"], it + 1)
                pool.tensor_copy(g_v2, dyn(z, it * 2 + Z_V, 2)).then_inc(d["v2"], 1)
                pool.wait_ge(d["at"], it + 1)
                for l in range(LEVELS):
                    if l >= EBUF:
                        if l == EBUF:
                            pool.wait_ge(d["t"], it * LEVELS + 1)
                        else:
                            pool.wait_ge(d["m1"], it * (LEVELS - 1) + (l - EBUF))
                    pool.tensor_tensor(g_e[l % EBUF].rearrange("p (q n) -> p q n", q=4),
                                       g_at.rearrange("p (q n) -> p q n", q=4),
                                       level_mask(l).unsqueeze(1).broadcast_to([P, 4, P]), ALU.mult).then_inc(d["e"], 1)
            pool.wait_ge(memv_ev, 2)
            pool.wait_ge(xq_ev, 4)
            attention(HEADS, XHEADS // 2, xqF, mem_v)


def _chunks(w):
    k, m = w.shape
    return np.ascontiguousarray(w.reshape(k // P, P, m // P, P).transpose(2, 1, 0, 3).reshape(m // P, P, k))


def _group(jobs, n):
    j, p, c = jobs.shape
    return np.ascontiguousarray(jobs.reshape(j // n, n, p, c).transpose(0, 2, 1, 3).reshape(j // n, p, n * c))


def _cols(v):
    return np.asarray(v).reshape(-1, P).T


def _feature_major(x):
    t, dd = x.shape
    return np.ascontiguousarray(x.T.reshape(dd // P, P, t).transpose(1, 0, 2))


def _constants():
    c = np.zeros((P, C_N), np.float32)
    c[:, C_ONE:C_ONE + P] = 1.0
    c[:, C_EPS] = EPS
    i = np.arange(P)
    m = np.zeros((P, C_MN), np.float32)
    m[:, C_ID:C_ID + P] = np.eye(P)
    m[:, C_TRI:C_TRI + P] = i[:, None] <= i[None, :]
    for l in range(LEVELS):
        b = 1 << l
        row, colm = i[None, :], i[:, None]
        m[:, C_MASK + l * P:C_MASK + (l + 1) * P] = (
            (row // (2 * b) == colm // (2 * b)) & (row // b % 2 == 1) & (colm // b % 2 == 0))
    neg = np.stack([np.where(np.arange(T)[None, :] > t * P + i[:, None], NEG, 0.0) for t in range(NT)], 1)
    return c, m, neg.astype(np.float32)


def kernel(**inp):
    import concourse.bacc as bacc
    from concourse.bass_utils import run_bass_kernel_spmd

    a = {k: np.asarray(v) for k, v in inp.items()}
    one = {k: v[0] for k, v in a.items() if k not in ("ln_f",)}
    w_in = one["w_in"]
    o = np.cumsum([0, 1024, 1024, 512, 256, 64, 8, 1024, 1024, 1024, 8, 8, 1024, 6144])
    part = [w_in[:, o[i]:o[i + 1]] for i in range(13)]
    a_x, a_gate, c_q, c_kv, k_idx, w_idx, g_q, g_k, g_v, g_b, g_a, g_z, gates = part
    pad = np.zeros((D, P - 24), np.float32)
    host = {
        "x_wk": _chunks(one["x_wkv"][:, 0:512]),
        "x_wv": np.ascontiguousarray(one["x_wkv"][:, 512:].reshape(4, 4, P, 512).transpose(0, 2, 1, 3).reshape(4, P, D)),
        "w_in": _chunks(np.concatenate([g_z, a_gate, a_x, c_q, c_kv, k_idx, k_idx, w_idx, g_b, g_a, pad, g_q, g_k, g_v], 1)),
        "w_gate": _chunks(gates),
        "lru_wa": np.ascontiguousarray(one["lru_wa"].transpose(1, 0, 2).reshape(P, LRU_CH * P)),
        "lru_wx": np.ascontiguousarray(one["lru_wx"].transpose(1, 0, 2).reshape(P, LRU_CH * P)),
        "w_uqi": _group(_chunks(one["dsa_w_uqi"].reshape(QR * P, -1)), 4)[0],
        "w_uk": _group(_chunks(one["dsa_w_uk"].reshape(KVR * P, -1)), 8)[0],
        "w_uq": _group(_chunks(one["dsa_w_uq"].reshape(QR * P, -1)), 4),
        "w_uv": np.ascontiguousarray(one["dsa_w_uv"].reshape(KVR, P, HEADS * P)),
        "p_a": _group(_chunks(one["p_a"]), 2),
        "p_b": _group(_chunks(one["p_b"]), 2),
        "p_c": _group(_chunks(one["p_c"]), 2),
        "w_o": _chunks(one["w_o"]),
        "x_wq": _chunks(one["x_wq"]),
        "x_wo": _group(_chunks(one["x_wo"]), 4),
        "w_up": _chunks(one["ffn_w_up"]),
        "w_down": _chunks(one["ffn_w_down"]),
        "x": _feature_major(one["x"]),
        "mem": _feature_major(one["mem"]),
        **dict(zip(("consts", "masks", "negmask"), _constants())),
    }
    one["ln_f"] = a["ln_f"]
    cols = []
    for name, width in PARAMS:
        v = one[name]
        cols.append(np.broadcast_to(v, (P, 8)) if name in ("gdn_a_log", "gdn_dt_bias") else _cols(v))
        assert cols[-1].shape[1] == width
    host["prm"] = np.ascontiguousarray(np.concatenate(cols, 1))

    nc = bacc.Bacc("TRN2", target_bir_lowering=False, num_devices=1)
    dr = {k: nc.dram_tensor("in_" + k, v.shape, F32, kind="ExternalInput").ap() for k, v in host.items()}
    out = nc.dram_tensor("out_0", (P, KC, T), F32, kind="ExternalOutput").ap()
    build(nc, dr, out)
    r = run_bass_kernel_spmd(nc, [{"in_" + k: v for k, v in host.items()}], core_ids=[0])
    y = r.results[0]["out_0"]
    return np.ascontiguousarray(y.transpose(2, 1, 0).reshape(1, T, D))
```

```python
from contextlib import ExitStack

import numpy as np

import concourse.bass as bass
from concourse import mybir

F32 = mybir.dt.float32
F32R = mybir.dt.float32r
ALU = mybir.AluOpType
ACT = mybir.ActivationFunctionType
AX = mybir.AxisListType

P = 128
T = 256
NT = T // P
D = 2048
KC = D // P
N_MEM = 256
EPS = 1e-6
LRU_CH = 8
LRU_C = 8.0
QR, KVR = 4, 2
HEADS = 8
IDX_DIM = 64
TOPK = min(256, T // 4)
XHEADS = 4
FF_CH = 44
DOWN_BLOCKS = 11
PIECE = 8
QKV_AHEAD = {4: (0, 0), 7: (0, 1), 10: (1, 0), 13: (1, 1)}
LEVELS = 7
WSLOTS = 4
NEG = -1.0e30
TAKEN = -float(2.0 ** 127)

Z_GZ, Z_AGATE, Z_AX, Z_CQ, Z_CKV, Z_KIDX, Z_SMALL, Z_Q, Z_K, Z_V = 0, 8, 16, 24, 28, 30, 31, 32, 40, 48
Z_CH = 56
J_AGATE, J_GZ, J_QKV, J_LOOP = 16, 24, 32, 40

C_ONE, C_EPS, C_N = 0, 128, 136
C_ID, C_TRI, C_MASK = 0, 128, 256
C_MN = C_MASK + LEVELS * P

PARAMS = [("ln_mix", 16), ("mem_norm", 16), ("ln_mem", 16), ("ln_ffn", 16), ("ln_f", 16),
          ("conv_a_w", 4 * 8), ("conv_a_b", 8), ("lru_ba", 8), ("lru_bx", 8), ("lru_lambda", 8),
          ("dsa_q_norm", 4), ("dsa_kv_norm", 2), ("gdn_conv_w", 4 * 24), ("gdn_o_norm", 1),
          ("ffn_conv_w", 3 * 88), ("gdn_a_log", 8), ("gdn_dt_bias", 8)]
PCOL, _at = {}, 0
for _n, _w in PARAMS:
    PCOL[_n] = _at
    _at += _w
P_N = _at

R_IN = 0
R_DSA_A = 6
R_F1 = 7
R_DSA_B = 9
R_F3 = 10
R_AB = R_F3 + 6
R_C = R_AB + 48 // WSLOTS
R_WO = R_C + 24 // WSLOTS
R_MEM = R_WO + KC // WSLOTS
R_X = R_MEM + 8 // WSLOTS
R_UP = R_X + 8 // WSLOTS
R_DOWN = R_UP + 2 * FF_CH // WSLOTS
R_END = R_DOWN + 4 * KC // WSLOTS

G_IN = 0
G_AB = G_IN + Z_CH
G_C = G_AB + 32
G_WO = G_C + 24
G_MEM = G_WO + KC
G_XQ = G_MEM + 8
G_XO = G_XQ + 4
G_UP = G_XO + 4
G_DOWN = G_UP + 2 * FF_CH


def build(nc, dr, out):
    ctx = ExitStack()
    with ctx:
        def sb(name, shape):
            return ctx.enter_context(nc.sbuf_tensor(name, shape, F32))

        def sem(name):
            return ctx.enter_context(nc.semaphore(name))

        consts = sb("consts", [P, C_N])
        prm = sb("prm", [P, P_N])
        tiny = sb("tiny", [P, 328])
        xT = sb("xT", [P, KC, T])
        wring = [sb(f"wring{s}", [P, D]) for s in range(WSLOTS)]

        def sbr(name, shape, stack=None):
            return (stack or ctx).enter_context(nc.sbuf_tensor(name, shape, F32R))

        w_hi = [sbr(f"w_hi{i}", [P, PIECE * P]) for i in range(4)]
        w_lo = [sbr(f"w_lo{i}", [P, PIECE * P]) for i in range(4)]
        h_hi, h_lo = sbr("h_hi", [P, KC, T]), sbr("h_lo", [P, KC, T])
        with ExitStack() as mixers:
            z = mixers.enter_context(nc.sbuf_tensor("z", [P, Z_CH, T], F32))
            V = mixers.enter_context(nc.sbuf_tensor("V", [P, 31, T], F32))
            masks = mixers.enter_context(nc.sbuf_tensor("masks", [P, C_MN], F32))
        with ExitStack() as branch_c:
            branch_c.enter_context(nc.sbuf_tensor("before_branch_c", [P, Z_CH, T], F32))
            yC_hi = sbr("yC_hi", [P, 8, T], branch_c)
            yC_lo = sbr("yC_lo", [P, 8, T], branch_c)
        with ExitStack() as cross:
            cross.enter_context(nc.sbuf_tensor("before_cross", [P, Z_CH + 18, T], F32))
            yX_hi = sbr("yX_hi", [P, XHEADS, T], cross)
            yX_lo = sbr("yX_lo", [P, XHEADS, T], cross)
        with ExitStack() as memory:
            m_hi = sbr("m_hi", [P, KC, T], memory)
            memory.enter_context(nc.sbuf_tensor("beside_memory", [P, 32, T], F32))
            m_lo = sbr("m_lo", [P, KC, T], memory)
        with ExitStack() as mlp:
            ff_hi, ff_lo = sbr("ff_hi", [P, FF_CH, T], mlp), sbr("ff_lo", [P, FF_CH, T], mlp)
            ff_t = mlp.enter_context(nc.sbuf_tensor("ff_t", [P, 3, T], F32))
        G = [ctx.enter_context(nc.psum_tensor(f"G{i}", [P, 512], F32)) for i in range(2)]
        M = [ctx.enter_context(nc.psum_tensor(f"M{i}", [P, 512], F32)) for i in range(6)]
        X = xT

        xo_bank = [G[0], G[1], M[4], M[5]]

        ident = masks[:, C_ID:C_ID + P]
        ones = consts[:, C_ONE:C_ONE + P]
        tri = masks[:, C_TRI:C_TRI + P]
        eps = consts[:, C_EPS:C_EPS + 1]

        def level_mask(l):
            return masks[:, C_MASK + l * P:C_MASK + (l + 1) * P]

        def col(name, c):
            return prm[:, bass.ds(PCOL[name] + c, 1)]

        def flat(ap):
            return ap.rearrange("p c t -> p (c t)")

        def xs(lo, hi):
            return flat(X[:, lo:hi, :])

        def vs(lo, hi):
            return flat(V[:, lo:hi, :])

        def tiles(ap):
            return ap.rearrange("p (m n) -> p m n", m=NT)

        hf = z[:, 16:32, :]
        rt = vs(9, 10)
        ctmp = [vs(16, 17), vs(17, 18)]
        negmask = V[:, 27:29, :]
        xc, lr, li, la, lt = X[:, 0:8, :], X[:, 8:16, :], z[:, 40:48, :], z[:, 48:56, :], z[:, 32:40, :]
        dsq, drt = V[:, 16:22, :], vs(22, 24)
        qF, kF, qiF = z[:, 16:24, :], V[:, 0:8, :], V[:, 16:20, :]
        vT = tiles(vs(8, 16))
        score, rl, sbias = X[:, 0:2, :], [xs(2, 3), xs(3, 4)], X[:, 4:6, :]
        self_att = ([X[:, 6:8, :], X[:, 8:10, :]], [X[:, 10:12, :], X[:, 12:14, :]], [xs(14, 15), xs(15, 16)],
                    [tiles(vs(20, 21)), tiles(vs(21, 22))])
        x_s, x_pT = ([V[:, c + 2 * h:c + 2 * h + 2, :] for h in range(XHEADS)] for c in (10, 0))
        yB = V[:, 22:30, :]
        yA = z[:, Z_AGATE:Z_AGATE + 8, :]
        yC = z[:, Z_GZ:Z_GZ + 8, :]
        merged = z[:, 16:32, :]
        mem_in = z[:, 32:48, :]
        xqF, mem_k = z[:, 40:44, :], z[:, 32:36, :]
        mem_v = tiles(flat(z[:, 36:40, :]))
        sq_acc = {"mem": hf[:, 0, :], "xat": V[:, 26, :], "ffn": V[:, 26, :], "out": ff_t[:, 0, :]}
        sq_new = {"xat": [V[:, 27, :], V[:, 28, :]], "ffn": [V[:, 27 + u, :] for u in range(4)],
                  "out": [ff_t[:, 1, :], ff_t[:, 2, :]]}

        g_sq, g_rt = xs(0, 4), xs(4, 8)
        g_ug, g_db = xs(0, 2), xs(2, 4)
        g_bd, g_at = xs(0, 2), xs(2, 4)
        g_dec, g_qk = xs(4, 6), xs(6, 8)
        g_q2, g_k2, g_v2, g_eg = xs(8, 10), xs(10, 12), xs(12, 14), xs(14, 16)
        g_t = g_v2
        g_vt, g_kt, g_ktail, g_kw, g_qd = vs(0, 2), vs(2, 3), vs(3, 4), vs(4, 6), vs(6, 8)
        g_v0 = g_kt
        EBUF = 3
        g_e = [vs(8, 10), vs(10, 12), vs(12, 14)]
        g_osq, g_ort = g_e[0], g_e[1]
        g_tt, g_ms = vs(14, 16), vs(16, 18)
        g_tb = g_ms
        g_s, g_r, g_v1 = vs(18, 19), vs(19, 20), vs(30, 31)
        sg = vs(20, 22)

        _t = [0]

        def small(n):
            _t[0] += n
            return tiny[:, _t[0] - n:_t[0]]

        tokc = tiles(small(64))
        widx = tiles(small(16))
        beta = small(16)
        gdec = small(16)
        gcum = small(16)
        sp_x, sp_e, sp_s, sp_z, sp_p = (small(24) for _ in range(5))
        sp = small(24)
        ea = small(8)
        lam_n, lam_p = small(8), small(8)
        top8 = tiles(small(16))
        amax = [small(2), small(2)]
        asum = [small(2), small(2)]
        x_max, x_sum = amax + [small(2), small(2)], asum + [small(2), small(2)]

        w_landed = [sem(f"w_landed{s}") for s in range(WSLOTS)]
        w_used = [sem(f"w_used{s}") for s in range(WSLOTS)]
        hi_done = sem("hi_done")
        lo_first = sem("lo_first")
        piece_used = sem("piece_used")
        const_in, masks_in, x_in = sem("const_in"), sem("masks_in"), [sem(f"x_in{q}") for q in range(4)]
        x_back, mem_loaded = sem("x_back"), sem("mem_loaded")
        n_sq, n_acc, n_ss, n_rt, n_f, n_hi, n_h = ({k: sem(f"{w}_{k}") for k in ("mix", "mem", "xat", "ffn", "out")}
                                            for w in ("sq", "acc", "ss", "rt", "hf", "hh", "h"))
        mg_hi, mg_h = sem("mg_hi"), sem("mg_h")
        memk_ev, memv_ev = sem("memk_ev"), sem("memv_ev")
        in_ev = sem("in_ev")
        xconv, qconv, qsilu = sem("xconv"), sem("qconv"), sem("qsilu")
        lat_sq, lat_ss, lat_rt, lat_n = sem("lat_sq"), sem("lat_ss"), sem("lat_rt"), sem("lat_n")
        tok_mm, tok_ev, sp_in, sp_ex, sp_done, beta_done = (sem(n) for n in
            ("tok_mm", "tok_ev", "sp_in", "sp_ex", "sp_done", "beta_done"))
        gcum_mm, gcum_ev = sem("gcum_mm"), sem("gcum_ev")
        lru_mm, lru_sig, lru_at, lru_m2, lru_root, gates_act, lru_done = (sem(n) for n in
            ("lru_mm", "lru_sig", "lru_at", "lru_m2", "lru_root", "gates_act", "lru_done"))
        prj_mm, prj_ev = sem("prj_mm"), sem("prj_ev")
        idx_mm, idx_relu, idx_acc, sel_done = sem("idx_mm"), sem("idx_relu"), sem("idx_acc"), sem("sel_done")
        a_stage, a_mm, a_max, a_exp, a_p, a_tr, a_pt, a_o, a_ev = (sem(n) for n in
            ("a_stage", "a_mm", "a_max", "a_exp", "a_p", "a_tr", "a_pt", "a_o", "a_ev"))
        d = {n: sem("d_" + n) for n in (
            "sq", "ss", "rt", "v2", "rank1", "qk", "bc", "vtr", "prod", "diff", "dec", "vt", "at", "kt",
            "e", "etr", "t", "m1", "ms", "x", "tb", "v0mm", "v0", "smm", "s", "ksmm", "r", "v1mm", "v1",
            "o", "osq", "oss", "ort", "y")}
        b_exp, b_sum = sem("b_exp"), sem("b_sum")
        yc_hi, yc_lo = sem("yc_hi"), sem("yc_lo")
        o_ev = sem("o_ev")
        xq_ev, yx_lo, sq_added, xo_mm, xo_ev = sem("xq_ev"), sem("yx_lo"), sem("sq_added"), sem("xo_mm"), sem("xo_ev")
        up_conv, up_silu, up_f, up_hi, up_h = sem("up_conv"), sem("up_silu"), sem("up_f"), sem("up_hi"), sem("up_h")
        dn_ev = sem("dn_ev")
        act_turns, stored = sem("act_turns"), sem("stored")

        block = ctx.enter_context(nc.Block())

        def dyn(ap, i, n=1):
            return ap[:, bass.ds(i, n), :].rearrange("p c t -> p (c t)")

        @block.sync
        def _(sp_eng):
            def load(s, r, src, cols):
                sp_eng.wait_ge(w_used[s], r)
                sp_eng.dma_start(wring[s][:, 0:cols], src).then_inc(w_landed[s], 16)

            def job(name, i):
                return dr[name][bass.ds(i, 1)].rearrange("a p c -> p (a c)")

            def in_round(r, first):
                for s in range(WSLOTS):
                    load(s, r, job("w_in", first + s), D)

            for q in range(0, 4, 2):
                sp_eng.dma_start(xT[:, 4 * q:4 * q + 4, :], dr["x"][:, 4 * q:4 * q + 4, :]).then_inc(x_in[q], 16)
            sp_eng.wait_ge(x_in[2], 16)
            for s in range(WSLOTS):
                sp_eng.dma_start(wring[s][:], job("w_in", s)).then_inc(w_landed[s], 16)
            with sp_eng.Fori(1, R_DSA_A) as r:
                in_round(r, r * WSLOTS)
            load(0, R_DSA_A, dr["lru_wa"], LRU_CH * P)
            load(1, R_DSA_A, dr["lru_wx"], LRU_CH * P)
            load(2, R_DSA_A, dr["w_uqi"], 16 * P)
            load(3, R_DSA_A, dr["w_uk"], 16 * P)
            for r in range(2):
                in_round(R_F1 + r, J_GZ + r * WSLOTS)
            load(0, R_DSA_B, job("w_uq", 0), D)
            load(1, R_DSA_B, job("w_uq", 1), D)
            load(2, R_DSA_B, job("w_uv", 0), 8 * P)
            load(3, R_DSA_B, job("w_uv", 1), 8 * P)
            with sp_eng.Fori(0, 6) as r:
                in_round(r + R_F3, r * WSLOTS + J_QKV)
            with sp_eng.Fori(0, 4) as it:
                for j in range(4):
                    br, pair = j // 2, it * 2 + j % 2
                    for i in range(3):
                        n = 3 * j + i
                        src = job("w_gate", br * KC + pair * 2 + i) if i < 2 else job("p_ab"[0:2] + "ab"[br], pair)
                        load(n % WSLOTS, R_AB + it * 3 + n // WSLOTS, src, D)
            with sp_eng.Fori(0, 2) as it:
                for j in range(4):
                    pair = it * 4 + j
                    for i in range(3):
                        n = 3 * j + i
                        src = job("w_gate", 2 * KC + pair * 2 + i) if i < 2 else job("p_c", pair)
                        load(n % WSLOTS, R_C + it * 3 + n // WSLOTS, src, D)
            with sp_eng.Fori(0, KC // WSLOTS) as r:
                for s in range(WSLOTS):
                    load(s, R_WO + r, job("w_o", r * WSLOTS + s), D)
            for s in range(WSLOTS):
                load(s, R_MEM, job("x_wk", s), D)
            for s in range(WSLOTS):
                load(s, R_MEM + 1, job("x_wv", s), D)
            for s in range(WSLOTS):
                load(s, R_X, job("x_wq", s), D)
            for s in range(WSLOTS):
                load(s, R_X + 1, job("x_wo", s), D)
            with sp_eng.Fori(0, 2 * FF_CH // WSLOTS) as r:
                for s in range(WSLOTS):
                    load(s, R_UP + r, job("w_up", (s % 2) * FF_CH + r * 2 + s // 2), D)
            with sp_eng.Fori(0, KC) as r:
                src = dr["w_down"][bass.ds(r, 1)].rearrange("a p c -> p (a c)")
                n = DOWN_BLOCKS * P
                for s in range(WSLOTS):
                    load(s, R_DOWN + r, src[:, s * n:(s + 1) * n], n)
            for q in range(4):
                sp_eng.wait_ge(n_f["out"], 4 * q + 4)
                sp_eng.dma_start(out[:, 4 * q:4 * q + 4, :], hf[:, 4 * q:4 * q + 4, :]).then_inc(stored, 16)
            sp_eng.wait_ge(stored, 64)

        @block.tensor
        def _(pe):
            def landed(s, r):
                pe.wait_ge(w_landed[s], (r + 1) * 16)

            def norm_sum(k):
                pe.wait_ge(n_acc[k], 1)
                pe.matmul(M[0][:, 0:T], ones, sq_acc[k], start=True, stop=True).then_inc(n_ss[k], 1)

            def chunk(dst, s, first, count, rhs):
                for k in range(count):
                    q = pe.matmul(dst, wring[s][:, (first + k) * P:(first + k + 1) * P], rhs(k),
                                  start=k == 0, stop=k == count - 1)
                return q

            def piece_ready(q, s, g, r):
                if q == 0:
                    pe.wait_ge(lo_first, g + 1)
                else:
                    pe.wait_ge(w_used[s], r + 1)

            def piece(dst, b, q, s, g, r, blocks, hi, lo, k0=0, kn=KC, ready=None, half=None):
                if half != 1:
                    piece_ready(q, s, g, r)
                wh, wl = w_hi[2 * b + q], w_lo[2 * b + q]
                for k in range(blocks) if half is None else range(half * blocks // 2, (half + 1) * blocks // 2):
                    if ready is not None:
                        pe.wait_ge(ready, k0 + k + 1)
                    c = slice(k * P, (k + 1) * P)
                    pe.matmul(dst, wh[:, c], hi[:, k0 + k, :], start=k0 + k == 0, stop=False)
                    pe.matmul(dst, wh[:, c], lo[:, k0 + k, :], start=False, stop=False)
                    e = pe.matmul(dst, wl[:, c], hi[:, k0 + k, :], start=False, stop=k0 + k == kn - 1)
                if half != 0:
                    e.then_inc(piece_used, 1)

            def split_chunk(dst, s, g, r, hi, lo, ready=None):
                for q in range(2):
                    piece(dst, s % 2, q, s, g, r, PIECE, hi, lo, k0=q * PIECE, ready=ready)

            pe.wait_ge(const_in, 32)
            for q in range(4):
                pe.wait_ge(n_acc["mix"], q + 1)
                e = pe.matmul(M[0][:, 0:T], ones, hf[:, 4 * q, :], start=q == 0, stop=q == 3)
            e.then_inc(n_ss["mix"], 1)

            def in_job(c, s, r, ready=None):
                pe.wait_ge(in_ev, c + 1)
                split_chunk(G[s % 2][:, 0:T], s, G_IN + c, r, h_hi, h_lo, ready)

            with pe.Fori(0, R_DSA_A) as r:
                for s in range(WSLOTS):
                    in_job(r * WSLOTS + s, s, r, n_h["mix"] if s == 0 else None)
            pe.wait_ge(lat_sq, 1)
            for c in range(QR):
                pe.matmul(M[0][:, 0:T], ones, dsq[:, c, :], start=c == 0, stop=c == QR - 1)
            for c in range(KVR):
                q = pe.matmul(M[0][:, T:2 * T], ones, dsq[:, QR + c, :], start=c == 0, stop=c == KVR - 1)
            q.then_inc(lat_ss, 1)
            pe.wait_ge(masks_in, 32)
            for m in range(NT):
                q = pe.transpose(M[1][:, m * 32:(m + 1) * 32], z[0:32, Z_SMALL, m * P:(m + 1) * P], ident[0:32, 0:32])
            q.then_inc(tok_mm, 1)
            pe.wait_ge(xconv, LRU_CH)
            for j in range(2 * LRU_CH):
                s, c = j // LRU_CH, j % LRU_CH
                if c == 0:
                    landed(s, R_DSA_A)
                bank = M[3 + j % 3]
                if j >= 3:
                    pe.wait_ge(lru_sig, j - 2)
                q = pe.matmul(bank[:, 0:T], wring[s][:, c * P:(c + 1) * P], xc[:, c, :], start=True, stop=True)
                q.then_inc(lru_mm, 1)
                if c == LRU_CH - 1:
                    pe.drain().then_inc(w_used[s], 1)
            pe.wait_ge(lat_n, 1)
            pe.wait_ge(lru_sig, 2 * LRU_CH)
            pe.wait_ge(tok_ev, 1)

            def proj_bank(e):
                if e >= 4:
                    pe.wait_ge(prj_ev, e - 3)
                return M[e % 4]

            def project(e, s, r, chunks, kn, first):
                landed(s, r)
                for c in range(chunks):
                    if c % 2 == 0:
                        bank = proj_bank(e + c // 2)
                    q = chunk(bank[:, (c % 2) * T:(c % 2 + 1) * T], s, c * kn, kn, lambda k: z[:, first + k, :])
                    if c % 2:
                        q.then_inc(prj_mm, 1)
                pe.drain().then_inc(w_used[s], 1)

            project(0, 2, R_DSA_A, 4, QR, Z_CQ)
            project(2, 3, R_DSA_A, 8, KVR, Z_CKV)
            for s in range(WSLOTS):
                in_job(J_GZ + s, s, R_F1)
            pe.wait_ge(sp_done, 1)
            pe.wait_ge(prj_ev, 6)
            for m in range(NT):
                q = pe.matmul(M[2][:, m * 8:(m + 1) * 8], tri, gdec[:, m * 8:(m + 1) * 8], start=True, stop=True)
            q.then_inc(gcum_mm, 1)
            for s in range(WSLOTS):
                in_job(J_GZ + WSLOTS + s, s, R_F1 + 1)
            pe.wait_ge(gcum_ev, 1)
            project(6, 0, R_DSA_B, 4, QR, Z_CQ)
            project(8, 1, R_DSA_B, 4, QR, Z_CQ)
            landed(2, R_DSA_B)
            landed(3, R_DSA_B)
            for m in range(NT):
                for half in range(2):
                    bank = proj_bank(10 + 2 * m + half)
                    for k in range(KVR):
                        q = pe.matmul(bank[:], z[:, Z_CKV + k, m * P:(m + 1) * P],
                                      wring[2 + k][:, half * 512:(half + 1) * 512], start=k == 0, stop=k == KVR - 1)
                    q.then_inc(prj_mm, 1)
            pe.drain().then_inc(w_used[2], 1)
            pe.drain().then_inc(w_used[3], 1)
            pe.wait_ge(prj_ev, 14)
            for m in range(NT):
                for h in range(HEADS):
                    e = m * HEADS + h
                    if e >= 4:
                        pe.wait_ge(idx_relu, e - 3)
                    o = IDX_DIM * (h % 2)
                    pe.matmul(M[e % 4][:, 0:T], qiF[o:o + IDX_DIM, h // 2, m * P:(m + 1) * P],
                              z[o:o + IDX_DIM, Z_KIDX, :], start=True, stop=True).then_inc(idx_mm, 1)
            for r in range(2):
                for s in range(WSLOTS):
                    in_job(J_QKV + r * WSLOTS + s, s, R_F3 + r)

            def attention(first, pairs, keys, bufs, between):
                att_s, att_pT, att_q, att_v = bufs
                with pe.Fori(0, pairs) as i:
                    n = i * 2 + first
                    for u in range(2):
                        pe.wait_ge(a_stage, n + (u + 1))
                        pe.wait_ge(a_max, n + u + 1)
                        for m in range(NT):
                            q = pe.matmul(M[u][:, m * T:(m + 1) * T], att_q[u][:, m * P:(m + 1) * P],
                                          dyn(keys, i * 2 + u), start=True, stop=True)
                        q.then_inc(a_mm, 1)
                    between(i, 0)
                    for u in range(2):
                        pe.wait_ge(a_p, n + (u + 1))
                        for m in range(NT):
                            for k in range(NT):
                                q = pe.transpose(M[2 + u][:, k * T + m * P:k * T + (m + 1) * P],
                                                 att_s[u][:, m, k * P:(k + 1) * P], ident)
                        q.then_inc(a_tr, 1)
                    between(i, 1)
                    for u in range(2):
                        pe.wait_ge(a_pt, n + (u + 1))
                        for k in range(NT):
                            q = pe.matmul(M[4 + u][:, 0:T], att_v[u][:, k, :], att_pT[u][:, k, :],
                                          start=k == 0, stop=k == NT - 1)
                        q.then_inc(a_o, 1)
                    between(i, 2)

            def qkv_jobs(i, at):
                for s in ((0, 1), (2,), (3,))[at]:
                    in_job(i * WSLOTS + (J_LOOP + s), s, i + (R_F3 + 2))

            pe.wait_ge(idx_relu, 2 * HEADS)
            attention(0, HEADS // 2, kF, self_att, qkv_jobs)

            y_of = {0: yA, 1: yB}

            def gate_piece(n, j, q, g0, r0, half=None):
                i = q // 2
                at = 3 * j + i
                if q == 0 and half != 1:
                    pe.wait_ge(b_exp, n + 1)
                piece(G[0][:, i * T:(i + 1) * T], i, q % 2, at % WSLOTS, g0 + 2 * j + i, r0 + at // WSLOTS, PIECE,
                      h_hi, h_lo, k0=(q % 2) * PIECE, half=half)

            def proj_piece(n, j, c, r0, y, half=None):
                at = 3 * j + 2
                s = at % WSLOTS
                if c == 0 and half != 1:
                    pe.wait_ge(b_sum, n + 1)
                    landed(s, r0 + at // WSLOTS)
                for k in range(8) if half is None else range(4 * half, 4 * half + 4):
                    e = pe.matmul(G[1][:, c * T:(c + 1) * T], wring[s][:, (8 * c + k) * P:(8 * c + k + 1) * P],
                                  y[:, k, :], start=k == 0, stop=k == 7)
                if c == 1 and half != 0:
                    e.then_inc(w_used[s], 1)

            pe.wait_ge(a_ev, 1 + HEADS)
            pe.wait_ge(lru_done, 1)
            with pe.Fori(0, HEADS // 2) as it:
                def gp(j, q, half=None):
                    gate_piece(it * 4 + j, j, q, it * 8 + G_AB, it * 3 + R_AB, half)

                def pp(j, c, half=None):
                    proj_piece(it * 4 + j, j, c, it * 3 + R_AB, y_of[j // 2], half)

                gp(0, 0)
                pe.wait_ge(d["sq"], it + 1)
                for i in range(2):
                    q = pe.matmul(M[3 * i][:], ones, g_sq[:, i * 512:(i + 1) * 512], start=True, stop=True)
                q.then_inc(d["ss"], 1)
                pe.wait_ge(d["v2"], it + 1)
                for p in range(4):
                    q = pe.transpose(M[2][:, p * P:(p + 1) * P], g_v2[:, p * P:(p + 1) * P], ident)
                q.then_inc(d["vtr"], 1)
                gp(0, 1)
                gp(0, 2)
                pe.wait_ge(d["rank1"], it + 1)
                pe.matmul(M[3][:], ones, g_ug, start=True, stop=True)
                pe.matmul(M[4][:], ones, g_db, start=True, stop=True).then_inc(d["bc"], 1)
                gp(0, 3)
                pp(0, 0)
                pe.wait_ge(d["qk"], it + 1)
                for u in range(2):
                    pe.transpose(M[5][:, u * P:(u + 1) * P], g_k2[:, 2 * u * P:(2 * u + 1) * P], ident)
                for p in range(4):
                    ks = g_k2[:, p * P:(p + 1) * P]
                    pe.matmul(M[0][:, p * P:(p + 1) * P], ks, ks, start=True, stop=True)
                    q = pe.matmul(M[1][:, p * P:(p + 1) * P], ks, g_q2[:, p * P:(p + 1) * P], start=True, stop=True)
                q.then_inc(d["prod"], 1)
                pp(0, 1)
                gp(1, 0)
                pe.wait_ge(d["e"], it * LEVELS + 1)
                pe.wait_ge(d["vt"], it + 1)
                for p in range(4):
                    q = pe.transpose(M[2][:, p * P:(p + 1) * P], g_e[0][:, p * P:(p + 1) * P], ident)
                q.then_inc(d["etr"], 1)
                gp(1, 1)
                fill = [(f, j, q, half) for f, j, q in ((gp, 1, 2), (gp, 1, 3), (pp, 1, 0), (pp, 1, 1), (gp, 2, 0), (gp, 2, 1),
                                                        (gp, 2, 2), (gp, 2, 3), (pp, 2, 0)) for half in range(2)]
                for l in range(1, LEVELS):
                    e = g_e[l % EBUF]
                    pe.wait_ge(d["t"], it * LEVELS + l)
                    pe.wait_ge(d["e"], it * LEVELS + l + 1)
                    for p in range(4):
                        q = pe.matmul(M[3][:, p * P:(p + 1) * P], e[:, p * P:(p + 1) * P], g_t[:, p * P:(p + 1) * P],
                                      start=True, stop=True)
                    q.then_inc(d["m1"], 1)
                    f, j, q, half = fill[3 * l - 3]
                    f(j, q, half)
                    pe.wait_ge(d["ms"], it * (LEVELS - 1) + l)
                    for p in range(4):
                        c = slice(p * P, (p + 1) * P)
                        if l < LEVELS - 1:
                            pe.matmul(M[4][:, c], g_tt[:, c], g_ms[:, c], start=True, stop=True)
                        q = pe.matmul(M[5][:, c], g_ms[:, c], g_tt[:, c], start=True, stop=True)
                    q.then_inc(d["x"], 1)
                    for f, j, q, half in fill[3 * l - 2:3 * l]:
                        f(j, q, half)
                pe.wait_ge(d["tb"], it + 1)
                for u in range(2):
                    p = 2 * u
                    q = pe.matmul(M[0][:, u * P:(u + 1) * P], g_tb[:, p * P:(p + 1) * P], g_vt[:, p * P:(p + 1) * P],
                                  start=True, stop=True)
                q.then_inc(d["v0mm"], 1)
                pp(2, 1)
                pe.wait_ge(d["v0"], it + 1)
                pe.wait_ge(d["kt"], it + 1)
                for u in range(2):
                    q = pe.matmul(M[2][:, u * P:(u + 1) * P], g_ktail[:, u * P:(u + 1) * P], g_v0[:, u * P:(u + 1) * P],
                                  start=True, stop=True)
                q.then_inc(d["smm"], 1)
                for u in range(2):
                    p = 2 * u
                    pe.matmul(M[1][:, p * P:(p + 1) * P], g_v0[:, u * P:(u + 1) * P], g_qk[:, p * P:(p + 1) * P],
                              start=True, stop=True)
                gp(3, 0)
                pe.wait_ge(d["s"], it + 1)
                for u in range(2):
                    p = 2 * u + 1
                    q = pe.matmul(M[3][:, u * P:(u + 1) * P], g_kw[:, p * P:(p + 1) * P], g_s[:, u * P:(u + 1) * P],
                                  start=True, stop=True)
                q.then_inc(d["ksmm"], 1)
                gp(3, 1)
                pe.wait_ge(d["r"], it + 1)
                for u in range(2):
                    p = 2 * u + 1
                    q = pe.matmul(M[4][:, u * P:(u + 1) * P], g_tb[:, p * P:(p + 1) * P], g_r[:, u * P:(u + 1) * P],
                                  start=True, stop=True)
                q.then_inc(d["v1mm"], 1)
                gp(3, 2)
                pe.wait_ge(d["v1"], it + 1)
                for u in range(2):
                    p = 2 * u + 1
                    pe.matmul(M[1][:, p * P:(p + 1) * P], g_s[:, u * P:(u + 1) * P], g_qd[:, p * P:(p + 1) * P],
                              start=True, stop=False)
                    q = pe.matmul(M[1][:, p * P:(p + 1) * P], g_v1[:, u * P:(u + 1) * P], g_qk[:, p * P:(p + 1) * P],
                                  start=False, stop=True)
                q.then_inc(d["o"], 1)
                gp(3, 3)
                pe.wait_ge(d["osq"], it + 1)
                pe.matmul(M[2][:], ones, g_osq, start=True, stop=True).then_inc(d["oss"], 1)
                pp(3, 0)
                pp(3, 1)
            def c_piece(dst, job, q, hi, lo, k0, kn):
                piece(dst, job % 2, q, job % WSLOTS, G_C + job, R_C + job // WSLOTS, PIECE, hi, lo, k0, kn)

            for u in range(8):
                pe.wait_ge(b_exp, 16 + u + 1)
                for i in range(2):
                    for q in range(2):
                        c_piece(G[0][:, i * T:(i + 1) * T], 3 * u + i, q, h_hi, h_lo, q * PIECE, KC)
                if u == 0:
                    pe.wait_ge(yc_lo, 4)
                pe.wait_ge(b_sum, 16 + u + 1)
                for q in range(2):
                    c_piece(G[1][:, q * T:(q + 1) * T], 3 * u + 2, q, yC_hi, yC_lo, 0, PIECE)
            pe.wait_ge(b_exp, 1 + 24)
            pe.wait_ge(b_sum, 1 + 24)
            def o_round(r):
                for s in range(WSLOTS):
                    pe.wait_ge(o_ev, r * WSLOTS + s + 1)
                    split_chunk(G[s % 2][:, 0:T], s, G_WO + r * WSLOTS + s, R_WO + r, h_hi, h_lo,
                                mg_h if isinstance(r, int) and r + s == 0 else None)

            o_round(0)
            o_round(1)
            norm_sum("mem")
            with pe.Fori(2, KC // WSLOTS) as r:
                o_round(r)
            for s in range(WSLOTS):
                if s < 2:
                    pe.wait_ge(o_ev, 1 + KC + s)
                if s >= 2:
                    pe.wait_ge(memk_ev, s - 1)
                split_chunk(G[s % 2][:, 0:T], s, G_MEM + s, R_MEM, m_hi, m_lo, n_h["mem"] if s == 0 else None)
                if s == 0:
                    norm_sum("xat")
            for s in range(WSLOTS):
                for q in range(2):
                    piece_ready(q, s, G_MEM + 4 + s, R_MEM + 1)
                    wh, wl = w_hi[2 * (s % 2) + q], w_lo[2 * (s % 2) + q]
                    for kk in range(2):
                        k = 4 * s + 2 * q + kk
                        c = slice(kk * 512, (kk + 1) * 512)
                        for m in range(NT):
                            t = slice(m * P, (m + 1) * P)
                            pe.matmul(M[1 + m][:], m_hi[:, k, t], wh[:, c], start=k == 0, stop=False)
                            pe.matmul(M[1 + m][:], m_hi[:, k, t], wl[:, c], start=False, stop=False)
                            e = pe.matmul(M[1 + m][:], m_lo[:, k, t], wh[:, c], start=False, stop=k == KC - 1)
                    e.then_inc(piece_used, 1)
            pe.wait_ge(memk_ev, 4)
            for s in range(WSLOTS):
                if s >= 2:
                    pe.wait_ge(xq_ev, s - 1)
                split_chunk(G[s % 2][:, 0:T], s, G_XQ + s, R_X, h_hi, h_lo, n_h["xat"] if s == 0 else None)
            pe.wait_ge(xq_ev, 4)
            pe.wait_ge(memv_ev, NT)
            x_t = [M[4], M[5], G[0], G[1]]

            def x_scores(h):
                for m in range(NT):
                    q = pe.matmul(M[h][:, m * T:(m + 1) * T], xqF[:, h, m * P:(m + 1) * P], mem_k[:, h, :],
                                  start=True, stop=True)
                q.then_inc(a_mm, 1)

            def x_transpose(h):
                pe.wait_ge(a_p, HEADS + h + 1)
                for m in range(NT):
                    for k in range(NT):
                        q = pe.transpose(x_t[h][:, k * T + m * P:k * T + (m + 1) * P], x_s[h][:, m, k * P:(k + 1) * P],
                                         ident)
                q.then_inc(a_tr, 1)

            def x_values(h):
                pe.wait_ge(a_pt, HEADS + h + 1)
                for k in range(NT):
                    q = pe.matmul(M[h][:, 0:T], mem_v[:, k, h * P:(h + 1) * P], x_pT[h][:, k, :],
                                  start=k == 0, stop=k == NT - 1)
                q.then_inc(a_o, 1)

            for h in range(XHEADS):
                x_scores(h)
            for h in range(XHEADS + 1):
                if h < XHEADS:
                    x_transpose(h)
                if h:
                    x_values(h - 1)
            for c in range(KC):
                s, q = c // 4, c // 2 % 2
                if c >= 4:
                    pe.wait_ge(xo_ev, c - 3)
                if c % 2 == 0:
                    piece_ready(q, s, G_XO + s, R_X + 1)
                for k in range(XHEADS):
                    if c == 0:
                        pe.wait_ge(yx_lo, k + 1)
                    w = slice((c % 2 * 4 + k) * P, (c % 2 * 4 + k + 1) * P)
                    wh, wl = w_hi[2 * (s % 2) + q], w_lo[2 * (s % 2) + q]
                    pe.matmul(xo_bank[c % 4][:, 0:T], wh[:, w], yX_hi[:, k, :], start=k == 0, stop=False)
                    pe.matmul(xo_bank[c % 4][:, 0:T], wh[:, w], yX_lo[:, k, :], start=False, stop=False)
                    e = pe.matmul(xo_bank[c % 4][:, 0:T], wl[:, w], yX_hi[:, k, :], start=False,
                                  stop=k == XHEADS - 1)
                e.then_inc(piece_used if c % 2 else xo_mm, 1)
            norm_sum("ffn")
            with pe.Fori(0, 2 * FF_CH // WSLOTS) as r:
                for s in range(WSLOTS):
                    pe.wait_ge(up_conv, r * WSLOTS + s + 1)
                    split_chunk(G[s % 2][:, 0:T], s, G_UP + r * WSLOTS + s, R_UP + r, h_hi, h_lo,
                                n_h["ffn"] if s == 0 else None)
            with pe.Fori(0, KC // 2) as i:
                for u in range(2):
                    pe.wait_ge(dn_ev, i * 2 + (u + 1))
                    pe.wait_ge(up_conv, 1 + 2 * FF_CH + u)
                    for s in range(WSLOTS):
                        pe.wait_ge(up_h, (s + 1) * DOWN_BLOCKS)
                        r = i * 2 + (R_DOWN + u)
                        g = i * 8 + (G_DOWN + 4 * u + s)
                        piece(G[u][:, 0:T], s % 2, 0, s, g, r, PIECE, ff_hi, ff_lo, s * DOWN_BLOCKS, FF_CH)
                        piece(G[u][:, 0:T], s % 2, 1, s, g, r, DOWN_BLOCKS - PIECE, ff_hi, ff_lo,
                              s * DOWN_BLOCKS + PIECE, FF_CH)
            norm_sum("out")

        @block.scalar
        def _(act):
            def hold(s, value):
                act.wait_ge(s, value)
                act.sem_inc(act_turns, 1)

            def hi(b, q, s, g, r, blocks=PIECE):
                if q == 0:
                    act.wait_ge(w_landed[s], (r + 1) * 16)
                if not isinstance(g, int) or g >= 2:
                    act.wait_ge(piece_used, g * 2 + (q - 3))
                n = blocks * P
                act.copy(w_hi[2 * b + q][:, 0:n], wring[s][:, q * PIECE * P:q * PIECE * P + n]).then_inc(hi_done, 1)

            def hi_job(s, g, r, last=PIECE, b=None):
                for q in range(2):
                    hi(s % 2 if b is None else b, q, s, g, r, last if q else PIECE)

            def squares(k, src, q):
                act.activation(flat(hf[:, 4 * q:4 * q + 4, :]), flat(src[:, 4 * q:4 * q + 4, :]),
                               ACT.Square).then_inc(n_sq[k], 1)

            def root(k):
                act.wait_ge(n_ss[k], 1)
                act.activation(rt, M[0][:, 0:T], ACT.Sqrt, bias=eps, scale=1.0 / D).then_inc(n_rt[k], 1)

            def square(k, c, u, added, credits=0):
                hold(added, c + (credits + 1))
                act.activation(sq_new[k][u], dyn(xT, c), ACT.Square).then_inc(n_sq[k], 1)

            def round_chunks(ready, done, dst, first=0, last=KC):
                for c in range(first, last):
                    act.wait_ge(ready, c + 1)
                    act.copy(dst[:, c, :], hf[:, c, :]).then_inc(done, 1)

            for q in range(1, 4, 2):
                act.dma_start(xT[:, 4 * q:4 * q + 4, :], dr["x"][:, 4 * q:4 * q + 4, :]).then_inc(x_in[q], 16)
                if q == 1:
                    act.dma_start(consts[:], dr["consts"]).then_inc(const_in, 16)
                    act.dma_start(prm[:], dr["prm"]).then_inc(const_in, 16)
            for q in range(4):
                act.wait_ge(x_in[q], 16)
            act.dma_start(masks[:], dr["masks"]).then_inc(masks_in, 16)
            act.dma_start(negmask, dr["negmask"]).then_inc(masks_in, 16)
            act.sem_inc(a_ev, 1)
            act.sem_inc(b_exp, 1)
            act.sem_inc(in_ev, 2)
            act.wait_ge(const_in, 32)
            for q in range(4):
                act.wait_ge(x_in[q], 16)
                squares("mix", xT, q)
            for g in range(2):
                hi_job(g, g, R_IN)
            root("mix")
            round_chunks(n_f["mix"], n_hi["mix"], h_hi)

            def evac(c, s, zc):
                hold(piece_used, c * 2 + (2 * G_IN + 2))
                act.copy(dyn(z, zc), G[s % 2][:, 0:T]).then_inc(in_ev, 1)

            def silu(c, u):
                hold(qconv, c - (J_QKV - 1))
                act.activation(dyn(z, c), ctmp[u], ACT.Silu).then_inc(qsilu, 1)

            def in_round(r, to_z, ahead=WSLOTS):
                for s in range(WSLOTS):
                    c = r * WSLOTS + s
                    evac(c, s, c + to_z)
                    if s < ahead:
                        hi_job((s + 2) % WSLOTS, c + (G_IN + 2), r + (R_IN + (s + 2) // WSLOTS))

            with act.Fori(0, J_AGATE // WSLOTS) as r:
                in_round(r, Z_AX)
            act.activation(flat(dsq), flat(z[:, Z_CQ:Z_CQ + 6, :]), ACT.Square).then_inc(lat_sq, 1)
            in_round(J_AGATE // WSLOTS, Z_AGATE - J_AGATE)
            in_round(J_AGATE // WSLOTS + 1, Z_AGATE - J_AGATE, 2)
            act.wait_ge(lat_ss, 1)
            act.activation(drt[:, 0:T], M[0][:, 0:T], ACT.Sqrt, bias=eps, scale=1.0 / (QR * P)).then_inc(lat_rt, 1)
            act.activation(drt[:, T:2 * T], M[0][:, T:2 * T], ACT.Sqrt, bias=eps, scale=1.0 / (KVR * P)).then_inc(lat_rt, 1)
            for j in range(2 * LRU_CH):
                c = j % LRU_CH
                act.wait_ge(lru_mm, j + 1)
                dst, b = (lr, "lru_ba") if j < LRU_CH else (li, "lru_bx")
                act.activation(dst[:, c, :], M[3 + j % 3][:, 0:T], ACT.Sigmoid, bias=col(b, c)).then_inc(lru_sig, 1)
            for s in range(2):
                hi_job(s, G_IN + J_GZ + s, R_F1)
            act.wait_ge(sp_in, 1)
            act.activation(beta.rearrange("p (m n) -> p m n", m=NT), tokc[:, :, 8:16], ACT.Sigmoid).then_inc(beta_done, 1)
            act.activation(sp_e, sp_x, ACT.Abs)
            act.activation(ea, prm[:, PCOL["gdn_a_log"]:PCOL["gdn_a_log"] + 8], ACT.Exp)
            act.drain()
            act.activation(sp_e, sp_e, ACT.Exp, scale=-1.0).then_inc(sp_ex, 1)
            dsts = ([flat(qiF[:, 2 * i:2 * i + 2, :]) for i in range(2)] + [flat(kF[:, 2 * i:2 * i + 2, :]) for i in range(4)]
                    + [flat(qF[:, 2 * i:2 * i + 2, :]) for i in range(4)]
                    + [vT[:, m, h * 512:(h + 1) * 512] for m in range(NT) for h in range(2)])

            def proj_out(a, b):
                for e in range(a, b):
                    act.wait_ge(prj_mm, e + 1)
                    act.copy(dsts[e], M[e % 4][:]).then_inc(prj_ev, 1)

            proj_out(0, 6)
            act.wait_ge(sp_done, 1)
            for s in range(WSLOTS):
                evac(J_GZ + s, s, Z_GZ + s)
                hi_job((s + 2) % WSLOTS, G_IN + J_GZ + s + 2, R_F1 + (s + 2) // WSLOTS)
                for c in (2 * s, 2 * s + 1):
                    act.activation(la[:, c, :], lr[:, c, :], ACT.Exp, scale=lam_n[:, c:c + 1])
                    act.activation(lt[:, c, :], lr[:, c, :], ACT.Tanh, scale=lam_p[:, c:c + 1]).then_inc(lru_at, 1)
            for s in range(WSLOTS):
                evac(J_GZ + WSLOTS + s, s, Z_GZ + WSLOTS + s)
                if s < 2:
                    hi_job(s + 2, G_IN + J_GZ + s + 6, R_F1 + 1)
                if s == 1:
                    act.wait_ge(lru_m2, 1)
                    act.activation(flat(lr), flat(lt), ACT.Sqrt).then_inc(lru_root, 1)
                if s == 2:
                    act.activation(flat(yA), flat(yA), ACT.Gelu_apprx_tanh).then_inc(gates_act, 1)
            proj_out(6, 14)
            act.wait_ge(lru_done, 1)
            for e in range(NT * HEADS):
                act.wait_ge(idx_mm, e + 1)
                if e >= 2:
                    act.wait_ge(idx_acc, e - 1)
                act.activation(rl[e % 2], M[e % 4][:, 0:T], ACT.Relu).then_inc(idx_relu, 1)
                if e in QKV_AHEAD:
                    s, q = QKV_AHEAD[e]
                    hi(s, q, s, G_IN + J_QKV + s, R_F3)
            act.activation(flat(z[:, Z_GZ:Z_GZ + 8, :]), flat(z[:, Z_GZ:Z_GZ + 8, :]), ACT.Silu).then_inc(gates_act, 1)

            def qkv_job(c, s, r):
                evac(c, s, c)
                hi_job((s + 2) % WSLOTS, c + (G_IN + 2), r + (s + 2) // WSLOTS)
                if not isinstance(c, int) or c > J_QKV:
                    silu(c - 1, (s + 1) % 2)

            for c in range(J_QKV, J_LOOP):
                qkv_job(c, c % WSLOTS, R_F3 + (c - J_QKV) // WSLOTS)

            def attention(first, pairs, dst, bufs, between):
                att_s, att_pT = bufs[0:2]
                with act.Fori(0, pairs) as i:
                    n = i * 2 + first
                    for u in range(2):
                        act.wait_ge(a_max, n + (u + 3))
                        for m in range(NT):
                            q = act.activation(att_s[u][:, m, :], att_s[u][:, m, :], ACT.Exp, bias=amax[u][:, m:m + 1],
                                               accum_out=asum[u][:, m:m + 1])
                        q.then_inc(a_exp, 1)
                    between(i, 0)
                    for u in range(2):
                        act.wait_ge(a_tr, n + (u + 1))
                        act.copy(flat(att_pT[u]), M[2 + u][:]).then_inc(a_pt, 1)
                    between(i, 1)
                    for u in range(2):
                        hold(a_o, n + (u + 1))
                        act.copy(dyn(dst, i * 2 + u), M[4 + u][:, 0:T]).then_inc(a_ev, 1)
                    between(i, 2)

            def qkv_jobs(i, at):
                for s in ((0, 1), (2,), (3,))[at]:
                    qkv_job(i * WSLOTS + (J_LOOP + s), s, i + (R_F3 + 2))

            attention(0, HEADS // 2, yB, self_att, qkv_jobs)

            def head_squares(pair):
                act.activation(g_sq[:, 0:512], dyn(z, pair * 2 + Z_Q, 2), ACT.Square)
                act.activation(g_sq[:, 512:1024], dyn(z, pair * 2 + Z_K, 2), ACT.Square).then_inc(d["sq"], 1)

            head_squares(0)
            silu(Z_CH - 1, 1)

            def gate(n, g, func=ACT.Exp):
                act.wait_ge(b_sum, n + 1)
                act.wait_ge(piece_used, g * 2 + 2)
                act.activation(sg, G[0][:], func, scale=-1.0 if func == ACT.Exp else 1.0).then_inc(b_exp, 1)

            def hi_unit(j, q, g0, r0):
                at = 3 * j + q // 2
                hi(q // 2, q % 2, at % WSLOTS, g0 + (2 * j + q // 2), r0 + at // WSLOTS)

            with act.Fori(0, HEADS // 2) as it:
                def hi_of(j, q):
                    hi_unit(j, q, it * 8 + G_AB, it * 3 + R_AB)

                act.wait_ge(d["ss"], it + 1)
                for i in range(2):
                    q = act.activation(g_rt[:, i * 512:(i + 1) * 512], M[3 * i][:], ACT.Sqrt, bias=eps)
                q.then_inc(d["rt"], 1)
                act.wait_ge(d["vtr"], it + 1)
                act.copy(g_vt, M[2][:])
                hi_of(1, 0)
                act.wait_ge(d["diff"], it + 1)
                act.activation(g_eg, M[3][:], ACT.Exp)
                act.activation(g_dec, g_dec, ACT.Exp).then_inc(d["dec"], 1)
                hi_of(1, 1)
                act.wait_ge(d["prod"], it + 1)
                act.copy(g_kt, M[5][:, 0:2 * P]).then_inc(d["vt"], 1)
                gate(it * 4, it * 8 + (G_AB + 1))
                hi_of(1, 2)
                hi_of(1, 3)
                after = {2: [(2, 0)], 3: [(2, 1), (2, 2)], 4: [(2, 3)], 5: [(3, 0)], 6: [(3, 1), (3, 2)]}
                for l in range(1, LEVELS):
                    act.wait_ge(d["m1"], it * (LEVELS - 1) + l)
                    act.copy(g_ms, M[3][:]).then_inc(d["ms"], 1)
                    if l == 3:
                        gate(it * 4 + 1, it * 8 + (G_AB + 3))
                    if l == 6:
                        gate(it * 4 + 2, it * 8 + (G_AB + 5))
                    for j, q in after.get(l, ()):
                        hi_of(j, q)
                hold(d["t"], it * LEVELS + LEVELS)
                for u in range(2):
                    for m in range(NT):
                        c = slice((2 * u + m) * P, (2 * u + m + 1) * P)
                        q = act.activation(g_tb[:, c], g_tt[:, c], ACT.Copy,
                                           scale=beta[:, bass.ds(it * 2 + (u + 8 * m), 1)])
                q.then_inc(d["tb"], 1)
                hi_of(3, 3)
                act.wait_ge(d["smm"], it + 1)
                act.copy(g_s, M[2][:, 0:2 * P]).then_inc(d["s"], 1)
                hi_of(4, 0)
                hi_of(4, 1)
                act.wait_ge(d["o"], it + 1)
                act.activation(g_osq, M[1][:], ACT.Square).then_inc(d["osq"], 1)
                hi_of(4, 2)
                hi_of(4, 3)
                gate(it * 4 + 3, it * 8 + (G_AB + 7))
                act.wait_ge(d["oss"], it + 1)
                act.activation(g_ort, M[2][:], ACT.Sqrt, bias=eps, scale=1.0 / P).then_inc(d["ort"], 1)
                head_squares(it + 1)
            act.wait_ge(d["y"], 1 + HEADS // 2)
            act.wait_ge(d["sq"], 1 + HEADS // 2)
            act.dma_start(xT[:], dr["x"]).then_inc(x_back, 16)
            act.dma_start(mem_in, dr["mem"]).then_inc(mem_loaded, 16)

            for c in range(0, 8, 2):
                act.copy(flat(yC_hi[:, c:c + 2, :]), flat(yC[:, c:c + 2, :])).then_inc(yc_hi, 1)

            def hi_c(job):
                hi_job(job % WSLOTS, G_C + job, R_C + job // WSLOTS, b=job % 2)

            for u in range(8):
                hi_c(3 * u + 2)
                gate(16 + u, G_C + 3 * u + 1, ACT.Sigmoid)
                hi_c(3 * u + 3)
                if u < 7:
                    hi_c(3 * u + 4)
            for c in range(KC):
                if c == KC - 2:
                    hi_c(3 * 8 + 1)
                    act.wait_ge(b_sum, 1 + 24)
                act.copy(h_hi[:, c, :], merged[:, c, :]).then_inc(mg_hi, 1)

            def o_round(r):
                for s in range(WSLOTS):
                    c = r * WSLOTS + s
                    if isinstance(r, int) and r >= 2:
                        round_chunks(n_f["mem"], n_hi["mem"], m_hi, 2 * (c - 8), 2 * (c - 8) + 2)
                    hi_job((s + 2) % WSLOTS, r * WSLOTS + (s + G_WO + 2), r + (R_WO + (s + 2) // WSLOTS))
                    square("xat", c, s % 2, o_ev, 2)
                    if r == 0:
                        if s == 0:
                            act.wait_ge(mem_loaded, 16)
                            act.wait_ge(mg_h, KC)
                        squares("mem", mem_in, s)

            o_round(0)
            o_round(1)
            root("mem")
            o_round(2)
            o_round(3)
            for s in range(WSLOTS):
                act.wait_ge(piece_used, 2 * (G_MEM + s) + 2)
                act.copy(mem_k[:, s, :], G[s % 2][:, 0:T]).then_inc(memk_ev, 1)
                hi_job((s + 2) % WSLOTS, G_MEM + s + 2, R_MEM + (s + 2) // WSLOTS)
                if s == 1:
                    root("xat")
            for s in range(WSLOTS):
                round_chunks(n_f["xat"], n_hi["xat"], h_hi, 4 * s, 4 * s + 4)
                hi_job((s + 2) % WSLOTS, G_MEM + s + 6, R_MEM + 1 + (s + 2) // WSLOTS)
            act.wait_ge(piece_used, 2 * (G_MEM + 8))
            for m in range(NT):
                act.copy(mem_v[:, m, :], M[1 + m][:]).then_inc(memv_ev, 1)
            for s in range(WSLOTS):
                act.wait_ge(piece_used, 2 * (G_XQ + s) + 2)
                act.copy(xqF[:, s, :], G[s % 2][:, 0:T]).then_inc(xq_ev, 1)
                if s < 2:
                    hi_job(s + 2, G_XQ + s + 2, R_X)
            def x_exp(h):
                act.wait_ge(a_max, HEADS + h + 3)
                for m in range(NT):
                    q = act.activation(x_s[h][:, m, :], x_s[h][:, m, :], ACT.Exp, bias=x_max[h][:, m:m + 1],
                                       accum_out=x_sum[h][:, m:m + 1])
                q.then_inc(a_exp, 1)

            x_exp(0)
            for h in range(XHEADS):
                if h < XHEADS - 1:
                    x_exp(h + 1)
                act.wait_ge(a_tr, HEADS + h + 1)
                act.copy(flat(x_pT[h]), (M[4], M[5], G[0], G[1])[h][:]).then_inc(a_pt, 1)
                hi(h // 2, h % 2, h // 2, G_XO + h // 2, R_X + 1)
            for h in range(XHEADS):
                act.wait_ge(a_o, HEADS + h + 1)
                act.copy(yX_hi[:, h, :], M[h][:, 0:T]).then_inc(a_ev, 1)
            for c in range(KC):
                if c >= 4:
                    act.wait_ge(sq_added, c - 3)
                square("ffn", c, c % 4, xo_ev)
                if c % 2:
                    s, q = c // 4, c // 2 % 2
                    hi(s % 2, q, (s + 2) % WSLOTS, G_XO + s + 2, R_X + 1 + (s + 2) // WSLOTS)
            root("ffn")
            round_chunks(n_f["ffn"], n_hi["ffn"], h_hi)

            def up_round(r, last):
                for s in range(WSLOTS):
                    u = s // 2
                    c = r * 2 + u
                    if s % 2 == 0:
                        act.wait_ge(up_conv, r * WSLOTS + (s + 3))
                        act.activation(flat(ff_t[:, u:u + 1, :]), flat(ff_t[:, u:u + 1, :]), ACT.Silu).then_inc(up_silu, 1)
                    down = last and s >= 2
                    hi_job((s + 2) % WSLOTS, r * WSLOTS + (s + G_UP + 2), r + (R_UP + (s + 2) // WSLOTS),
                           DOWN_BLOCKS - PIECE if down else PIECE)
                    if s % 2:
                        hold(up_f, c + 1)
                        act.copy(dyn(ff_hi, c), flat(ff_t[:, u:u + 1, :])).then_inc(up_hi, 1)

            rounds = 2 * FF_CH // WSLOTS
            with act.Fori(0, rounds - 1) as r:
                up_round(r, False)
            up_round(rounds - 1, True)
            def down_round(r, u, ahead=WSLOTS):
                for s in range(ahead):
                    hi_job((s + 2) % WSLOTS, r * WSLOTS + (s + G_DOWN + 2), r + (R_DOWN + (s + 2) // WSLOTS),
                           DOWN_BLOCKS - PIECE)
                square("out", r, u, dn_ev, 2)

            with act.Fori(0, KC // 2 - 1) as i:
                for u in range(2):
                    down_round(i * 2 + u, u)
            down_round(KC - 2, 0)
            down_round(KC - 1, 1, 2)
            root("out")

        @block.vector
        def _(dve):
            def lo(b, q, s, g, blocks=PIECE):
                dve.wait_ge(hi_done, g * 2 + (q + 1))
                n = blocks * P
                dve.tensor_tensor(w_lo[2 * b + q][:, 0:n], wring[s][:, q * PIECE * P:q * PIECE * P + n],
                                  w_hi[2 * b + q][:, 0:n].bitcast(F32), ALU.subtract).then_inc(w_used[s] if q else lo_first, 1)

            def lo_job(s, g, last=PIECE, b=None):
                for q in range(2):
                    lo(s % 2 if b is None else b, q, s, g, last if q else PIECE)

            def add_square(k, c, u):
                dve.wait_ge(n_sq[k], c + 1)
                return dve.tensor_tensor(sq_acc[k], sq_acc[k], sq_new[k][u], ALU.add)

            def norm(k, src, gain, hi=None, lo=None, first=0, last=KC):
                if first == 0:
                    dve.wait_ge(n_rt[k], 1)
                    dve.reciprocal(rt, rt)
                    dve.drain()
                for c in range(first, last + 2):
                    if c < last:
                        dve.scalar_tensor_tensor(out=hf[:, c, :], in0=src[:, c, :], scalar=col(gain, c), in1=rt,
                                                 op0=ALU.mult, op1=ALU.mult).then_inc(n_f[k], 1)
                    if c >= first + 2 and hi is not None:
                        dve.wait_ge(n_hi[k], c - 1)
                        dve.tensor_tensor(lo[:, c - 2, :], hf[:, c - 2, :], hi[:, c - 2, :].bitcast(F32),
                                          ALU.subtract).then_inc(n_h[k], 1)

            def conv(dst, src, name, taps, chunks, c, bias=None):
                def w(k):
                    return prm[:, bass.ds(PCOL[name] + k * chunks + c, 1)]
                if bias is None:
                    dve.tensor_scalar(dst, src, w(taps - 1), None, ALU.mult)
                else:
                    dve.tensor_scalar(dst, src, w(taps - 1), bias, ALU.mult, ALU.add)
                for lag in range(1, taps):
                    dve.drain()
                    q = dve.scalar_tensor_tensor(out=dst[:, lag:T], in0=src[:, 0:T - lag], scalar=w(taps - 1 - lag),
                                                 in1=dst[:, lag:T], op0=ALU.mult, op1=ALU.add)
                return q

            dve.sem_inc(b_sum, 1)
            dve.sem_inc(a_max, 2)
            dve.sem_inc(d["y"], 1)
            dve.sem_inc(o_ev, 2)
            dve.sem_inc(dn_ev, 2)
            dve.sem_inc(up_conv, 2)
            dve.wait_ge(const_in, 32)
            for q in range(4):
                dve.wait_ge(n_sq["mix"], q + 1)
                c = 4 * q
                dve.tensor_tensor(flat(hf[:, c:c + 2, :]), flat(hf[:, c:c + 2, :]), flat(hf[:, c + 2:c + 4, :]), ALU.add)
                dve.drain()
                dve.tensor_tensor(hf[:, c, :], hf[:, c, :], hf[:, c + 1, :], ALU.add).then_inc(n_acc["mix"], 1)
            for g in range(2):
                lo_job(g, g)
            norm("mix", xT, "ln_mix", h_hi, h_lo)

            def in_round(r, conv_x, ahead=WSLOTS):
                for s in range(WSLOTS):
                    c = r * WSLOTS + s
                    if s < ahead:
                        lo_job((s + 2) % WSLOTS, c + (G_IN + 2))
                    if conv_x:
                        dve.wait_ge(in_ev, c + 3)
                        conv(dyn(xc, c), dyn(z, c + Z_AX), "conv_a_w", 4, LRU_CH, c,
                             bias=col("conv_a_b", c)).then_inc(xconv, 1)

            def qkv_job(c, s):
                lo_job((s + 2) % WSLOTS, c + (G_IN + 2))
                dve.wait_ge(in_ev, c + 3)
                conv(ctmp[s % 2], dyn(z, c), "gdn_conv_w", 4, Z_CH - J_QKV, c - J_QKV).then_inc(qconv, 1)

            with dve.Fori(0, LRU_CH // WSLOTS) as r:
                in_round(r, True)
            with dve.Fori(LRU_CH // WSLOTS, R_DSA_A - 1) as r:
                in_round(r, False)
            in_round(R_DSA_A - 1, False, 2)
            dve.wait_ge(tok_mm, 1)
            dve.tensor_copy(tokc, M[1][:, 0:64].rearrange("p (m n) -> p m n", m=NT)).then_inc(tok_ev, 1)
            dve.wait_ge(lat_rt, 2)
            dve.reciprocal(drt, drt)
            dve.drain()
            for c in range(QR + KVR):
                name, cc, r = ("dsa_q_norm", c, drt[:, 0:T]) if c < QR else ("dsa_kv_norm", c - QR, drt[:, T:2 * T])
                q = dve.scalar_tensor_tensor(out=z[:, Z_CQ + c, :], in0=z[:, Z_CQ + c, :], scalar=col(name, cc), in1=r,
                                             op0=ALU.mult, op1=ALU.mult)
            q.then_inc(lat_n, 1)
            lam = prm[:, PCOL["lru_lambda"]:PCOL["lru_lambda"] + 8]
            dtb = prm[:, PCOL["gdn_dt_bias"]:PCOL["gdn_dt_bias"] + 8]
            dve.tensor_scalar(sp_x[:, 0:8], lam, -1.0, None, ALU.mult)
            dve.drain()
            for m in range(NT):
                dve.tensor_tensor(sp_x[:, 8 + 8 * m:16 + 8 * m], tokc[:, m, 16:24], dtb, ALU.add)
            dve.tensor_scalar(widx, tokc[:, :, 0:8], float(HEADS ** -0.5 * IDX_DIM ** -0.5), None, ALU.mult)
            dve.drain().then_inc(sp_in, 1)
            for s in range(2):
                lo_job(s, G_IN + J_GZ + s)
            dve.wait_ge(sp_ex, 1)
            dve.tensor_scalar(sp_s, sp_e, 2.0, None, ALU.add)
            dve.drain()
            dve.reciprocal(sp_s, sp_s)
            dve.drain()
            dve.tensor_tensor(sp_s, sp_s, sp_e, ALU.mult)
            dve.drain()
            dve.tensor_tensor(sp_z, sp_s, sp_s, ALU.mult)
            dve.drain()
            dve.tensor_scalar(sp_p, sp_z, 1.0 / 17, None, ALU.mult)
            for k in range(15, 1, -2):
                dve.drain()
                dve.scalar_tensor_tensor(out=sp_p, in0=sp_p, scalar=1.0 / k, in1=sp_z, op0=ALU.add, op1=ALU.mult)
            dve.drain()
            dve.scalar_tensor_tensor(out=sp_p, in0=sp_p, scalar=1.0, in1=sp_s, op0=ALU.add, op1=ALU.mult)
            dve.tensor_scalar(sp, sp_x, 0.0, None, ALU.max)
            dve.drain()
            dve.scalar_tensor_tensor(out=sp, in0=sp_p, scalar=2.0, in1=sp, op0=ALU.mult, op1=ALU.add)
            dve.drain()
            dve.tensor_scalar(lam_n, sp[:, 0:8], -LRU_C, None, ALU.mult)
            dve.tensor_scalar(lam_p, sp[:, 0:8], LRU_C, None, ALU.mult)
            for m in range(NT):
                dve.scalar_tensor_tensor(out=gdec[:, 8 * m:8 * m + 8], in0=sp[:, 8 + 8 * m:16 + 8 * m], scalar=-1.0,
                                         in1=ea, op0=ALU.mult, op1=ALU.mult)
            dve.drain().then_inc(sp_done, 1)
            for s in range(WSLOTS):
                lo_job((s + 2) % WSLOTS, G_IN + J_GZ + s + 2)
            dve.wait_ge(gcum_mm, 1)
            dve.tensor_copy(gcum, M[2][:, 0:16]).then_inc(gcum_ev, 1)
            dve.wait_ge(lru_at, LRU_CH)
            dve.tensor_tensor(flat(lr), flat(la), flat(la), ALU.mult)
            dve.drain()
            dve.scalar_tensor_tensor(out=flat(lt), in0=flat(lr), scalar=1.0, in1=flat(lt),
                                     op0=ALU.add, op1=ALU.mult).then_inc(lru_m2, 1)
            dve.tensor_tensor(flat(li), flat(li), flat(xc), ALU.mult)
            for s in range(2):
                lo_job(s + 2, G_IN + J_GZ + s + 6)
            dve.wait_ge(lru_root, 1)
            dve.memset(lr[:, :, 0:1], 1.0)
            dve.drain()
            dve.tensor_tensor(flat(li), flat(li), flat(lr), ALU.mult)
            dve.drain()
            for c in range(LRU_CH):
                dve.tensor_tensor_scan(lt[:, c, :], la[:, c, :], li[:, c, :], 0.0, ALU.mult, ALU.add)
            dve.wait_ge(gates_act, 1)
            dve.drain()
            dve.tensor_tensor(flat(yA), flat(yA), flat(lt), ALU.mult).then_inc(lru_done, 1)
            dve.wait_ge(masks_in, 32)
            for m in range(NT):
                for h in range(HEADS):
                    e = m * HEADS + h
                    dve.drain()
                    dve.wait_ge(idx_relu, e + 1)
                    dve.scalar_tensor_tensor(out=score[:, m, :], in0=rl[e % 2], scalar=widx[:, m, h:h + 1],
                                             in1=negmask[:, m, :] if h == 0 else score[:, m, :],
                                             op0=ALU.mult, op1=ALU.add).then_inc(idx_acc, 1)
                    if e in QKV_AHEAD:
                        s, q = QKV_AHEAD[e]
                        lo(s, q, s, G_IN + J_QKV + s)

            def topk(rounds):
                with dve.Fori(0, rounds) as _:
                    dve.drain()
                    for m in range(NT):
                        dve.max(top8[:, m, :], score[:, m, :])
                    dve.drain()
                    for m in range(NT):
                        dve.match_replace(score[:, m, :], top8[:, m, :], score[:, m, :], TAKEN)

            jobs = J_LOOP - J_QKV
            for c in range(jobs - 1):
                qkv_job(J_QKV + c, c % WSLOTS)
                topk(TOPK // 8 // jobs if c < jobs - 2 else TOPK // 8 - (jobs - 2) * (TOPK // 8 // jobs))
            dve.drain()
            dve.tensor_scalar(flat(sbias), flat(score), TAKEN, 1.0, ALU.is_equal, ALU.subtract)
            dve.drain()
            dve.scalar_tensor_tensor(out=flat(sbias), in0=flat(sbias), scalar=-NEG, in1=flat(negmask),
                                     op0=ALU.mult, op1=ALU.add)
            qkv_job(J_LOOP - 1, (J_LOOP - 1) % WSLOTS)

            def attention(first, pairs, bias, att_s, between):
                scale = float(P ** -0.5)
                with dve.Fori(0, pairs) as i:
                    n = i * 2 + first
                    for u in range(2):
                        dve.wait_ge(a_mm, n + (u + 1))
                        dve.scalar_tensor_tensor(out=flat(att_s[u]), in0=M[u][:], scalar=scale, in1=flat(bias),
                                                 op0=ALU.mult, op1=ALU.add)
                        dve.drain()
                        dve.tensor_reduce(amax[u], att_s[u], AX.X, ALU.max)
                        dve.drain()
                        dve.tensor_scalar(amax[u], amax[u], -1.0, None, ALU.mult).then_inc(a_max, 1)
                    for u in range(2):
                        dve.wait_ge(a_exp, n + (u + 1))
                        dve.reciprocal(asum[u], asum[u])
                        dve.drain()
                        for m in range(NT):
                            q = dve.tensor_scalar(att_s[u][:, m, :], att_s[u][:, m, :], asum[u][:, m:m + 1], None, ALU.mult)
                        q.then_inc(a_p, 1)
                    between(i)

            def qkv_jobs(i):
                for s in range(WSLOTS):
                    qkv_job(i * WSLOTS + (J_LOOP + s), s)

            attention(0, HEADS // 2, sbias, self_att[0], qkv_jobs)

            def merge(n, c, j, r0, first):
                dve.wait_ge(b_exp, n + 2)
                dve.tensor_scalar(sg, sg, 1.0, None, ALU.add)
                dve.drain()
                dve.reciprocal(sg, sg)
                dve.drain()
                at = 3 * j + 2
                dve.wait_ge(w_used[at % WSLOTS], r0 + (at // WSLOTS + 1))
                if first:
                    dve.tensor_tensor(dyn(merged, c, 2), G[1][:], sg, ALU.mult)
                else:
                    dve.tensor_tensor(sg, G[1][:], sg, ALU.mult)
                    dve.drain()
                    dve.tensor_tensor(dyn(merged, c, 2), dyn(merged, c, 2), sg, ALU.add)
                dve.drain().then_inc(b_sum, 1)

            def lo_unit(j, q, g0):
                at = 3 * j + q // 2
                lo(q // 2, q % 2, at % WSLOTS, g0 + (2 * j + q // 2))

            def heads(ap):
                return ap.rearrange("p (q n) -> p q n", q=4)

            def over(ap):
                return ap.unsqueeze(1).broadcast_to([P, 4, P])

            with dve.Fori(0, HEADS // 2) as it:
                def lo_of(j, q):
                    lo_unit(j, q, it * 8 + G_AB)

                def merge_ab(j):
                    merge(it * 4 + j, it * 4 + 2 * (j % 2), j, it * 3 + R_AB, j < 2)

                dve.wait_ge(d["rt"], it + 1)
                for u in range(2):
                    for m in range(NT):
                        c = slice((2 * u + m) * P, (2 * u + m + 1) * P)
                        at = it * 2 + (u + 8 * m)
                        dve.tensor_scalar(g_ug[:, c], tri, gdec[:, bass.ds(at, 1)], None, ALU.mult)
                        q = dve.tensor_scalar(g_db[:, c], ident, beta[:, bass.ds(at, 1)], None, ALU.mult)
                q.then_inc(d["rank1"], 1)
                dve.reciprocal(g_rt, g_rt)
                dve.drain()
                dve.scalar_tensor_tensor(out=g_q2, in0=dyn(z, it * 2 + Z_Q, 2), scalar=float(P ** -0.5),
                                         in1=g_rt[:, 0:512], op0=ALU.mult, op1=ALU.mult)
                dve.tensor_tensor(g_k2, dyn(z, it * 2 + Z_K, 2), g_rt[:, 512:1024], ALU.mult).then_inc(d["qk"], 1)
                dve.drain()
                dve.wait_ge(d["bc"], it + 1)
                for u in range(2):
                    for m in range(NT):
                        c = slice((2 * u + m) * P, (2 * u + m + 1) * P)
                        q = dve.tensor_scalar(g_dec[:, c], M[3][:, c], gcum[:, bass.ds(it * 2 + (u + 8 * m), 1)], 0.0,
                                              ALU.subtract, ALU.min)
                q.then_inc(d["diff"], 1)
                lo_of(1, 0)
                dve.wait_ge(d["dec"], it + 1)
                dve.tensor_tensor(heads(g_dec), heads(g_dec), over(tri), ALU.mult)
                lo_of(1, 1)
                dve.drain()
                dve.wait_ge(d["prod"], it + 1)
                dve.tensor_tensor(g_bd, g_dec, M[4][:], ALU.mult)
                dve.drain()
                dve.tensor_tensor(g_at, g_bd, M[0][:], ALU.mult).then_inc(d["at"], 1)
                dve.tensor_tensor(g_qk, g_dec, M[1][:], ALU.mult)
                dve.tensor_tensor(g_kw, g_k2, g_eg, ALU.mult)
                dve.tensor_tensor(g_qd, g_q2, g_eg, ALU.mult)
                dve.wait_ge(d["vt"], it + 1)
                for u in range(2):
                    last = (2 * u + 1) * P - 1
                    q = dve.tensor_scalar(g_ktail[:, u * P:(u + 1) * P], g_kt[:, u * P:(u + 1) * P],
                                          g_dec[:, last:last + 1], None, ALU.mult)
                q.then_inc(d["kt"], 1)
                lo_of(1, 2)
                dve.wait_ge(d["etr"], it + 1)
                dve.tensor_tensor(heads(g_t), over(ident), heads(M[2][:]), ALU.subtract)
                dve.tensor_tensor(heads(g_tt), over(ident), heads(g_e[0]), ALU.subtract).then_inc(d["t"], 1)
                lo_of(1, 3)
                merge_ab(0)
                after = {2: [(2, 0)], 3: [(2, 1), (2, 2)], 4: [(2, 3)], 5: [(3, 0)], 6: [(3, 1), (3, 2)]}
                for l in range(1, LEVELS):
                    dve.drain()
                    dve.wait_ge(d["x"], it * (LEVELS - 1) + l)
                    if l < LEVELS - 1:
                        dve.tensor_tensor(g_t, g_t, M[4][:], ALU.subtract)
                    dve.tensor_tensor(g_tt, g_tt, M[5][:], ALU.subtract).then_inc(d["t"], 1)
                    for j, q in after.get(l, ()):
                        lo_of(j, q)
                    if l == 4:
                        merge_ab(1)
                dve.wait_ge(d["v0mm"], it + 1)
                dve.tensor_copy(g_v0, M[0][:, 0:2 * P]).then_inc(d["v0"], 1)
                merge_ab(2)
                lo_of(3, 3)
                dve.wait_ge(d["ksmm"], it + 1)
                for u in range(2):
                    q = dve.tensor_tensor(g_r[:, u * P:(u + 1) * P], g_vt[:, (2 * u + 1) * P:(2 * u + 2) * P],
                                          M[3][:, u * P:(u + 1) * P], ALU.subtract)
                q.then_inc(d["r"], 1)
                dve.wait_ge(d["v1mm"], it + 1)
                dve.tensor_copy(g_v1, M[4][:, 0:2 * P]).then_inc(d["v1"], 1)
                for q in range(4):
                    lo_of(4, q)
                dve.wait_ge(d["ort"], it + 1)
                dve.reciprocal(g_ort, g_ort)
                dve.drain()
                dve.scalar_tensor_tensor(out=g_ort, in0=M[1][:], scalar=col("gdn_o_norm", 0), in1=g_ort,
                                         op0=ALU.mult, op1=ALU.mult)
                dve.drain()
                dve.tensor_tensor(dyn(yC, it * 2, 2), dyn(yC, it * 2, 2), g_ort, ALU.mult).then_inc(d["y"], 1)
                merge_ab(3)
            def merged_lo(first, last):
                for c in range(first, last):
                    dve.wait_ge(mg_hi, c + 1)
                    dve.tensor_tensor(h_lo[:, c, :], merged[:, c, :], h_hi[:, c, :].bitcast(F32),
                                      ALU.subtract).then_inc(mg_h, 1)

            for c in range(0, 8, 2):
                dve.wait_ge(yc_hi, c // 2 + 1)
                dve.tensor_tensor(flat(yC_lo[:, c:c + 2, :]), flat(yC[:, c:c + 2, :]),
                                  flat(yC_hi[:, c:c + 2, :]).bitcast(F32), ALU.subtract).then_inc(yc_lo, 1)

            def lo_c(job):
                lo_job(job % WSLOTS, G_C + job, b=job % 2)

            for u in range(8):
                lo_c(3 * u + 2)
                lo_c(3 * u + 3)
                if u == 7:
                    merged_lo(0, KC // 2)
                dve.wait_ge(b_exp, 16 + u + 2)
                dve.wait_ge(piece_used, 2 * (G_C + 3 * u + 3))
                dve.tensor_tensor(sg, G[1][:], sg, ALU.mult)
                dve.drain()
                dve.tensor_tensor(flat(merged[:, 2 * u:2 * u + 2, :]), flat(merged[:, 2 * u:2 * u + 2, :]), sg,
                                  ALU.add).then_inc(b_sum, 1)
                if u < 7:
                    lo_c(3 * u + 4)
            merged_lo(KC // 2, KC)
            lo_c(3 * 8 + 1)
            dve.memset(sq_acc["xat"], 0.0)
            dve.wait_ge(x_back, 16)
            for c in range(KC):
                s = c % WSLOTS
                if c >= 8:
                    norm("mem", mem_in, "mem_norm", m_hi, m_lo, 2 * (c - 8), 2 * (c - 8) + 2)
                lo_job((s + 2) % WSLOTS, c + (G_WO + 2))
                if c:
                    add_square("xat", c - 1, (c - 1) % 2)
                dve.wait_ge(piece_used, c * 2 + (2 * G_WO + 2))
                dve.tensor_tensor(xT[:, c, :], xT[:, c, :], G[s % 2][:, 0:T], ALU.add).then_inc(o_ev, 1)
                dve.drain()
                if c == 3:
                    dve.wait_ge(n_sq["mem"], 4)
                if 3 <= c < 7:
                    n = 1 << (6 - c)
                    q = dve.tensor_tensor(flat(hf[:, 0:n, :]), flat(hf[:, 0:n, :]), flat(hf[:, n:2 * n, :]), ALU.add)
                    if n == 1:
                        q.then_inc(n_acc["mem"], 1)
            add_square("xat", KC - 1, 1).then_inc(n_acc["xat"], 1)
            for s in range(WSLOTS):
                lo_job((s + 2) % WSLOTS, G_MEM + s + 2)
            for s in range(WSLOTS):
                norm("xat", xT, "ln_mem", h_hi, h_lo, 4 * s, 4 * s + 4)
                lo_job((s + 2) % WSLOTS, G_MEM + s + 6)
            for s in range(2):
                lo_job(s + 2, G_XQ + s + 2)
            def x_maxima(h):
                dve.wait_ge(a_mm, HEADS + h + 1)
                dve.tensor_scalar(flat(x_s[h]), M[h][:], float(P ** -0.5), None, ALU.mult)
                dve.drain()
                dve.tensor_reduce(x_max[h], x_s[h], AX.X, ALU.max)
                dve.drain()
                dve.tensor_scalar(x_max[h], x_max[h], -1.0, None, ALU.mult).then_inc(a_max, 1)

            x_maxima(0)
            for h in range(XHEADS):
                if h < XHEADS - 1:
                    x_maxima(h + 1)
                dve.wait_ge(a_exp, HEADS + h + 1)
                dve.reciprocal(x_sum[h], x_sum[h])
                dve.drain()
                for m in range(NT):
                    q = dve.tensor_scalar(x_s[h][:, m, :], x_s[h][:, m, :], x_sum[h][:, m:m + 1], None, ALU.mult)
                q.then_inc(a_p, 1)
                if h:
                    lo((h - 1) // 2, (h - 1) % 2, (h - 1) // 2, G_XO + (h - 1) // 2)
            lo(1, 1, 1, G_XO + 1)
            for h in range(XHEADS):
                dve.wait_ge(a_ev, HEADS + h + 2)
                dve.tensor_tensor(yX_lo[:, h, :], M[h][:, 0:T], yX_hi[:, h, :].bitcast(F32), ALU.subtract).then_inc(yx_lo, 1)
            for c in range(KC):
                s, q = c // 4, c // 2 % 2
                if c % 2:
                    dve.wait_ge(piece_used, 2 * (G_XO + s) + q + 1)
                else:
                    dve.wait_ge(xo_mm, c // 2 + 1)
                dve.tensor_tensor(xT[:, c, :], xT[:, c, :], xo_bank[c % 4][:, 0:T], ALU.add).then_inc(xo_ev, 1)
                if c % 2 and c < KC - 1:
                    lo(s % 2, q, (s + 2) % WSLOTS, G_XO + s + 2)
            dve.wait_ge(sq_added, KC - 2)
            add_square("ffn", KC - 2, (KC - 2) % 4)
            dve.drain()
            add_square("ffn", KC - 1, (KC - 1) % 4).then_inc(n_acc["ffn"], 1)
            lo(1, 1, 1, G_UP + 1)
            norm("ffn", xT, "ln_ffn", h_hi, h_lo)

            def up_round(r, last):
                for s in range(WSLOTS):
                    u = s // 2
                    c = r * 2 + u
                    dve.wait_ge(piece_used, r * 8 + (2 * (G_UP + s) + 2))
                    dst = flat(ff_t[:, u:u + 1, :]) if s % 2 == 0 else flat(ff_t[:, 2:3, :])
                    conv(dst, G[s % 2][:, 0:T], "ffn_conv_w", 3, 2 * FF_CH, c + (s % 2) * FF_CH).then_inc(up_conv, 1)
                    if s % 2:
                        dve.drain()
                        dve.wait_ge(up_silu, c + 1)
                        dve.tensor_tensor(flat(ff_t[:, u:u + 1, :]), flat(ff_t[:, u:u + 1, :]), dst, ALU.mult).then_inc(up_f, 1)
                    down = last and s >= 2
                    lo_job((s + 2) % WSLOTS, r * WSLOTS + (s + G_UP + 2), DOWN_BLOCKS - PIECE if down else PIECE)
                    if s % 2:
                        dve.wait_ge(up_hi, c + 1)
                        dve.tensor_tensor(dyn(ff_lo, c), flat(ff_t[:, u:u + 1, :]), dyn(ff_hi, c).bitcast(F32),
                                          ALU.subtract).then_inc(up_h, 1)

            rounds = 2 * FF_CH // WSLOTS
            with dve.Fori(0, rounds - 1) as r:
                up_round(r, False)
            up_round(rounds - 1, True)

            def down_chunk(c, u, ahead):
                for s in range(ahead):
                    lo_job((s + 2) % WSLOTS, c * WSLOTS + (s + G_DOWN + 2), DOWN_BLOCKS - PIECE)
                dve.drain()
                if not isinstance(c, int) or c:
                    add_square("out", c - 1, 1 - u)
                dve.wait_ge(piece_used, c * 8 + (2 * G_DOWN + 8))
                dve.tensor_tensor(dyn(xT, c), dyn(xT, c), G[u][:, 0:T], ALU.add).then_inc(dn_ev, 1)

            dve.wait_ge(up_hi, FF_CH)
            dve.memset(sq_acc["out"], 0.0)
            down_chunk(0, 0, WSLOTS)
            down_chunk(1, 1, WSLOTS)
            with dve.Fori(1, KC // 2 - 1) as i:
                for u in range(2):
                    down_chunk(i * 2 + u, u, WSLOTS)
            down_chunk(KC - 2, 0, WSLOTS)
            down_chunk(KC - 1, 1, 2)
            dve.drain()
            add_square("out", KC - 1, 1).then_inc(n_acc["out"], 1)
            norm("out", xT, "ln_f")

        @block.gpsimd
        def _(pool):
            def attention(first, pairs, queries, values, bufs):
                att_q, att_v = bufs[2:4]
                with pool.Fori(0, pairs) as i:
                    n = i * 2 + first
                    for u in range(2):
                        pool.wait_ge(a_ev, n + 1)
                        pool.tensor_copy(att_q[u], dyn(queries, i * 2 + u))
                        pool.tensor_copy(att_v[u], values[:, :, bass.ds((i * 2 + u) * P, P)])
                        pool.drain().then_inc(a_stage, 1)

            pool.wait_ge(prj_ev, 14)
            pool.wait_ge(lru_done, 1)
            attention(0, HEADS // 2, qF, vT, self_att)
            pool.wait_ge(a_ev, 1 + HEADS)
            with pool.Fori(0, HEADS // 2) as it:
                pool.wait_ge(d["y"], it + 1)
                pool.tensor_copy(g_v2, dyn(z, it * 2 + Z_V, 2)).then_inc(d["v2"], 1)
                pool.wait_ge(d["at"], it + 1)
                for l in range(LEVELS):
                    if l >= EBUF:
                        if l == EBUF:
                            pool.wait_ge(d["t"], it * LEVELS + 1)
                        else:
                            pool.wait_ge(d["m1"], it * (LEVELS - 1) + (l - EBUF))
                    pool.tensor_tensor(g_e[l % EBUF].rearrange("p (q n) -> p q n", q=4),
                                       g_at.rearrange("p (q n) -> p q n", q=4),
                                       level_mask(l).unsqueeze(1).broadcast_to([P, 4, P]), ALU.mult).then_inc(d["e"], 1)
            for c in range(KC - 2):
                pool.wait_ge(n_sq["ffn"], c + 1)
                if c == 0:
                    q = pool.tensor_copy(sq_acc["ffn"], sq_new["ffn"][0])
                else:
                    q = pool.tensor_tensor(sq_acc["ffn"], sq_acc["ffn"], sq_new["ffn"][c % 4], ALU.add)
                q.then_inc(sq_added, 1)
                pool.drain()


def _chunks(w):
    k, m = w.shape
    return np.ascontiguousarray(w.reshape(k // P, P, m // P, P).transpose(2, 1, 0, 3).reshape(m // P, P, k))


def _group(jobs, n):
    j, p, c = jobs.shape
    return np.ascontiguousarray(jobs.reshape(j // n, n, p, c).transpose(0, 2, 1, 3).reshape(j // n, p, n * c))


def _cols(v):
    return np.asarray(v).reshape(-1, P).T


def _feature_major(x):
    t, dd = x.shape
    return np.ascontiguousarray(x.T.reshape(dd // P, P, t).transpose(1, 0, 2))


def _constants():
    c = np.zeros((P, C_N), np.float32)
    c[:, C_ONE:C_ONE + P] = 1.0
    c[:, C_EPS] = EPS
    i = np.arange(P)
    m = np.zeros((P, C_MN), np.float32)
    m[:, C_ID:C_ID + P] = np.eye(P)
    m[:, C_TRI:C_TRI + P] = i[:, None] <= i[None, :]
    for l in range(LEVELS):
        b = 1 << l
        row, colm = i[None, :], i[:, None]
        m[:, C_MASK + l * P:C_MASK + (l + 1) * P] = (
            (row // (2 * b) == colm // (2 * b)) & (row // b % 2 == 1) & (colm // b % 2 == 0))
    neg = np.stack([np.where(np.arange(T)[None, :] > t * P + i[:, None], NEG, 0.0) for t in range(NT)], 1)
    return c, m, neg.astype(np.float32)


def kernel(**inp):
    import concourse.bacc as bacc
    from concourse.bass_utils import run_bass_kernel_spmd

    a = {k: np.asarray(v) for k, v in inp.items()}
    one = {k: v[0] for k, v in a.items() if k not in ("ln_f",)}
    w_in = one["w_in"]
    o = np.cumsum([0, 1024, 1024, 512, 256, 64, 8, 1024, 1024, 1024, 8, 8, 1024, 6144])
    part = [w_in[:, o[i]:o[i + 1]] for i in range(13)]
    a_x, a_gate, c_q, c_kv, k_idx, w_idx, g_q, g_k, g_v, g_b, g_a, g_z, gates = part
    pad = np.zeros((D, P - 24), np.float32)
    host = {
        "x_wk": _chunks(one["x_wkv"][:, 0:512]),
        "x_wv": np.ascontiguousarray(one["x_wkv"][:, 512:].reshape(4, 4, P, 512).transpose(0, 2, 1, 3).reshape(4, P, D)),
        "w_in": _chunks(np.concatenate([a_x, c_q, c_kv, k_idx, k_idx, w_idx, g_b, g_a, pad, a_gate, g_z, g_q, g_k, g_v], 1)),
        "w_gate": _chunks(gates),
        "lru_wa": np.ascontiguousarray(one["lru_wa"].transpose(1, 0, 2).reshape(P, LRU_CH * P)),
        "lru_wx": np.ascontiguousarray(one["lru_wx"].transpose(1, 0, 2).reshape(P, LRU_CH * P)),
        "w_uqi": _group(_chunks(one["dsa_w_uqi"].reshape(QR * P, -1)), 4)[0],
        "w_uk": _group(_chunks(one["dsa_w_uk"].reshape(KVR * P, -1)), 8)[0],
        "w_uq": _group(_chunks(one["dsa_w_uq"].reshape(QR * P, -1)), 4),
        "w_uv": np.ascontiguousarray(one["dsa_w_uv"].reshape(KVR, P, HEADS * P)),
        "p_a": _group(_chunks(one["p_a"]), 2),
        "p_b": _group(_chunks(one["p_b"]), 2),
        "p_c": _group(_chunks(one["p_c"]), 2),
        "w_o": _chunks(one["w_o"]),
        "x_wq": _chunks(one["x_wq"]),
        "x_wo": _group(_chunks(one["x_wo"]), 4),
        "w_up": _chunks(one["ffn_w_up"]),
        "w_down": _chunks(one["ffn_w_down"]),
        "x": _feature_major(one["x"]),
        "mem": _feature_major(one["mem"]),
        **dict(zip(("consts", "masks", "negmask"), _constants())),
    }
    one["ln_f"] = a["ln_f"]
    cols = []
    for name, width in PARAMS:
        v = one[name]
        cols.append(np.broadcast_to(v, (P, 8)) if name in ("gdn_a_log", "gdn_dt_bias") else _cols(v))
        assert cols[-1].shape[1] == width
    host["prm"] = np.ascontiguousarray(np.concatenate(cols, 1))

    nc = bacc.Bacc("TRN2", target_bir_lowering=False, num_devices=1)
    dr = {k: nc.dram_tensor("in_" + k, v.shape, F32, kind="ExternalInput").ap() for k, v in host.items()}
    out = nc.dram_tensor("out_0", (P, KC, T), F32, kind="ExternalOutput").ap()
    build(nc, dr, out)
    r = run_bass_kernel_spmd(nc, [{"in_" + k: v for k, v in host.items()}], core_ids=[0])
    y = r.results[0]["out_0"]
    return np.ascontiguousarray(y.transpose(2, 1, 0).reshape(1, T, D))
```
